# Optimizing a Trainium2 kernel written in Bass

```python
import jax, jax.numpy as jnp
from jax import lax
import numpy as np

D_MODEL = 1024
BATCH = 1
SEQ = 1024
DEPTH = 1

CHUNK = 64
D_MIX = D_MODEL
A_DIM = D_MIX // 4
A_HEADS = 4
A_HEAD_DIM = A_DIM // A_HEADS
GMLP_BLOCK = 128
B_HEADS = 4
B_DV = (D_MIX // 2) // B_HEADS
B_DK = B_DV // 2
B_KDIM = B_HEADS * B_DK
B_VDIM = B_HEADS * B_DV
GLA_RANK = 16
GLA_TAU = 16.0
C_DIM = D_MIX - A_DIM - B_VDIM
CONV_WIDTH = 3
P_SIZES = (2 * A_DIM, B_KDIM, B_KDIM, B_VDIM, GLA_RANK, B_VDIM, C_DIM, C_DIM, C_DIM)
P_IN = sum(P_SIZES)
P_SPLITS = tuple(int(s) for s in np.cumsum(P_SIZES)[:-1])
N_EXPERTS = 32
N_GROUPS = 4
EXPERTS_PER_GROUP = N_EXPERTS // N_GROUPS
TOP_K = 2
D_FF_EXPERT = 512
EXPERT_BLOCK = 128
EPS = 1e-6

kernel_name = 'hybrid_gmlp_gla_shortconv_groupmoe_adaln'

def rmsnorm(x, g):
    xf = x.astype(jnp.float32)
    y = xf * lax.rsqrt(jnp.mean(xf * xf, axis=-1, keepdims=True) + EPS)
    return (y * g.astype(jnp.float32)).astype(x.dtype)

def spatial_gating(u, v, ln_g, ln_b, w_s, b_s):
    Bn, T, _ = v.shape
    vf = v.astype(jnp.float32)
    mu = jnp.mean(vf, axis=-1, keepdims=True)
    var = jnp.mean((vf - mu) ** 2, axis=-1, keepdims=True)
    vn = ((vf - mu) * lax.rsqrt(var + EPS) * ln_g.astype(jnp.float32) + ln_b.astype(jnp.float32)).astype(v.dtype)
    vn = vn.reshape(Bn, T // GMLP_BLOCK, GMLP_BLOCK, A_HEADS, A_HEAD_DIM)
    pos_chunk = jnp.arange(GMLP_BLOCK) // CHUNK
    mask = pos_chunk[:, None] >= pos_chunk[None, :]
    w = jnp.where(mask, w_s, 0).astype(vn.dtype)
    sv = jnp.einsum('hts,bnshd->bnthd', w, vn) + b_s.T[:, :, None].astype(vn.dtype)
    return u * sv.reshape(Bn, T, A_DIM)

def gla_chunked(q, k, v, glog):
    Bn, T, H, DK = q.shape
    DV = v.shape[-1]
    nC = T // CHUNK
    qf = q.astype(jnp.float32).reshape(Bn, nC, CHUNK, H, DK)
    kf = k.astype(jnp.float32).reshape(Bn, nC, CHUNK, H, DK)
    vf = v.astype(jnp.float32).reshape(Bn, nC, CHUNK, H, DV)
    b = jnp.cumsum(glog.astype(jnp.float32).reshape(Bn, nC, CHUNK, H, DK), axis=2)
    b_ref = b[:, :, CHUNK // 2:CHUNK // 2 + 1]
    b_last = b[:, :, CHUNK - 1:CHUNK]
    scores = jnp.einsum('bnihk,bnjhk->bnhij', qf * jnp.exp(b - b_ref), kf * jnp.exp(b_ref - b))
    causal = jnp.tril(jnp.ones((CHUNK, CHUNK), dtype=bool))
    scores = jnp.where(causal, scores, 0.0)
    o_intra = jnp.einsum('bnhij,bnjhv->bnihv', scores, vf)
    kv = jnp.einsum('bnjhk,bnjhv->bnhkv', kf * jnp.exp(b_last - b), vf)
    decay = jnp.exp(b_last[:, :, 0])

    def step(S, inp):
        dec, kv_c = inp
        return dec[..., None] * S + kv_c, S

    S0 = jnp.zeros((Bn, H, DK, DV), jnp.float32)
    _, S_prev = lax.scan(step, S0, (decay.transpose(1, 0, 2, 3), kv.transpose(1, 0, 2, 3, 4)))
    S_prev = S_prev.transpose(1, 0, 2, 3, 4)
    o_inter = jnp.einsum('bnihk,bnhkv->bnihv', qf * jnp.exp(b), S_prev)
    return (o_intra + o_inter).reshape(Bn, T, H, DV).astype(q.dtype)

def short_conv_mixer(gate_b, gate_c, xin, conv_w, conv_b):
    T = xin.shape[1]
    z = gate_c * xin
    zp = jnp.pad(z, ((0, 0), (CONV_WIDTH - 1, 0), (0, 0)))
    y = conv_b
    for j in range(CONV_WIDTH):
        y = y + conv_w[j] * zp[:, j:j + T]
    return gate_b * y

def hybrid_mixer(h, w_in, w_out, ln_g, ln_b, w_s, b_s, w_gate, b_gate, gla_g, conv_w, conv_b):
    Bn, T, _ = h.shape
    p = h @ w_in
    a_uv, q, k, v, g_lr, og, cb, cc, cx = jnp.split(p, P_SPLITS, axis=-1)
    u, vv = jnp.split(jax.nn.gelu(a_uv, approximate=False), 2, axis=-1)
    y_a = spatial_gating(u, vv, ln_g, ln_b, w_s, b_s)
    glog = jax.nn.log_sigmoid((g_lr @ w_gate + b_gate).astype(jnp.float32)) / GLA_TAU
    o = gla_chunked(q.reshape(Bn, T, B_HEADS, B_DK) * (B_DK ** -0.5),
                    k.reshape(Bn, T, B_HEADS, B_DK),
                    v.reshape(Bn, T, B_HEADS, B_DV),
                    glog.reshape(Bn, T, B_HEADS, B_DK))
    of = o.astype(jnp.float32)
    on = of * lax.rsqrt(jnp.mean(of * of, axis=-1, keepdims=True) + EPS)
    y_b = (on.reshape(Bn, T, B_VDIM) * gla_g.astype(jnp.float32)).astype(h.dtype) * jax.nn.silu(og)
    y_c = short_conv_mixer(cb, cc, cx, conv_w, conv_b)
    return jnp.concatenate([y_a, y_b, y_c], axis=-1) @ w_out

def moe(h, router_w, router_b, w1, w3, w2):
    Bn, T, D = h.shape
    N = Bn * T
    xt = h.reshape(N, D)
    logits = xt.astype(jnp.float32) @ router_w.astype(jnp.float32) + router_b.astype(jnp.float32)
    probs = jax.nn.softmax(logits, axis=-1)
    pg = probs.reshape(N, N_GROUPS, EXPERTS_PER_GROUP)
    gscore = jnp.sum(lax.top_k(pg, 2)[0], axis=-1)
    gidx = lax.top_k(gscore, 1)[1]
    in_group = jnp.take_along_axis(pg, gidx[:, :, None], axis=1)[:, 0]
    top_p, local = lax.top_k(in_group, TOP_K)
    experts = gidx * EXPERTS_PER_GROUP + local
    weights = top_p / jnp.sum(top_p, axis=-1, keepdims=True)
    A = N * TOP_K
    flat_e = experts.reshape(A)
    order = jnp.argsort(flat_e)
    sorted_e = flat_e[order]
    counts = jnp.bincount(flat_e, length=N_EXPERTS)
    padded = ((counts + EXPERT_BLOCK - 1) // EXPERT_BLOCK) * EXPERT_BLOCK
    pad_end = jnp.cumsum(padded)
    pad_start = pad_end - padded
    start = jnp.cumsum(counts) - counts
    dest = pad_start[sorted_e] + (jnp.arange(A) - start[sorted_e])
    n_blocks = -(-A // EXPERT_BLOCK) + N_EXPERTS
    xs = jnp.zeros((n_blocks * EXPERT_BLOCK, D), h.dtype).at[dest].set(xt[order // TOP_K])
    block_e = jnp.minimum(jnp.searchsorted(pad_end, jnp.arange(n_blocks) * EXPERT_BLOCK, side='right'),
                          N_EXPERTS - 1)

    def expert_block(args):
        xb, e = args
        return (jax.nn.silu(xb @ w1[e]) * (xb @ w3[e])) @ w2[e]

    ys = lax.map(expert_block, (xs.reshape(n_blocks, EXPERT_BLOCK, D), block_e)).reshape(-1, D)
    y_assign = jnp.zeros((A, D), h.dtype).at[order].set(ys[dest]).reshape(N, TOP_K, D)
    out = jnp.einsum('nk,nkd->nd', weights.astype(h.dtype), y_assign)
    return out.reshape(Bn, T, D)

def setup_inputs(seed: int = 0) -> dict:
    key = jax.random.key(seed)
    ks = jax.random.split(key, 24)

    def nrm(k, shape, scale):
        return jax.random.normal(k, shape, jnp.float32) * scale

    return {
        'x': nrm(ks[0], (BATCH, SEQ, D_MODEL), 1.0),
        'c': nrm(ks[1], (BATCH, D_MODEL), 1.0),
        'w_ada': nrm(ks[2], (DEPTH, D_MODEL, 6 * D_MODEL), 0.5 * D_MODEL ** -0.5),
        'b_ada': nrm(ks[3], (DEPTH, 6 * D_MODEL), 0.02),
        'g_norm1': 1.0 + nrm(ks[4], (DEPTH, D_MODEL), 0.02),
        'g_norm2': 1.0 + nrm(ks[5], (DEPTH, D_MODEL), 0.02),
        'w_in': nrm(ks[6], (DEPTH, D_MODEL, P_IN), D_MODEL ** -0.5),
        'w_out': nrm(ks[7], (DEPTH, D_MIX, D_MODEL), D_MIX ** -0.5),
        'gmlp_ln_g': 1.0 + nrm(ks[8], (DEPTH, A_DIM), 0.02),
        'gmlp_ln_b': nrm(ks[9], (DEPTH, A_DIM), 0.02),
        'gmlp_ws': nrm(ks[10], (DEPTH, A_HEADS, GMLP_BLOCK, GMLP_BLOCK), GMLP_BLOCK ** -0.5),
        'gmlp_bs': 1.0 + nrm(ks[11], (DEPTH, A_HEADS, GMLP_BLOCK), 0.02),
        'gla_w_gate': nrm(ks[12], (DEPTH, GLA_RANK, B_KDIM), GLA_RANK ** -0.5),
        'gla_b_gate': nrm(ks[13], (DEPTH, B_KDIM), 0.1),
        'gla_norm_g': 1.0 + nrm(ks[14], (DEPTH, B_VDIM), 0.02),
        'conv_w': nrm(ks[15], (DEPTH, CONV_WIDTH, C_DIM), CONV_WIDTH ** -0.5),
        'conv_b': nrm(ks[16], (DEPTH, C_DIM), 0.02),
        'router_w': nrm(ks[17], (D_MODEL, N_EXPERTS), D_MODEL ** -0.5),
        'router_b': nrm(ks[18], (N_EXPERTS,), 0.01),
        'exp_w1': nrm(ks[19], (DEPTH, N_EXPERTS, D_MODEL, D_FF_EXPERT), D_MODEL ** -0.5),
        'exp_w3': nrm(ks[20], (DEPTH, N_EXPERTS, D_MODEL, D_FF_EXPERT), D_MODEL ** -0.5),
        'exp_w2': nrm(ks[21], (DEPTH, N_EXPERTS, D_FF_EXPERT, D_MODEL), D_FF_EXPERT ** -0.5),
        'g_final': 1.0 + nrm(ks[22], (D_MODEL,), 0.02),
    }

def reference(x, c, w_ada, b_ada, g_norm1, g_norm2, w_in, w_out, gmlp_ln_g, gmlp_ln_b,
              gmlp_ws, gmlp_bs, gla_w_gate, gla_b_gate, gla_norm_g, conv_w, conv_b,
              router_w, router_b, exp_w1, exp_w3, exp_w2, g_final):
    for l in range(DEPTH):
        mod = jax.nn.silu(c) @ w_ada[l] + b_ada[l]
        sh1, sc1, gt1, sh2, sc2, gt2 = jnp.split(mod[:, None, :], 6, axis=-1)
        h = rmsnorm(x, g_norm1[l]) * (1.0 + sc1) + sh1
        x = x + gt1 * hybrid_mixer(h, w_in[l], w_out[l], gmlp_ln_g[l], gmlp_ln_b[l], gmlp_ws[l],
                                   gmlp_bs[l], gla_w_gate[l], gla_b_gate[l], gla_norm_g[l],
                                   conv_w[l], conv_b[l])
        h = rmsnorm(x, g_norm2[l]) * (1.0 + sc2) + sh2
        x = x + gt2 * moe(h, router_w, router_b, exp_w1[l], exp_w3[l], exp_w2[l])
    return rmsnorm(x, g_final)


_drawn_inputs = setup_inputs


def setup_inputs(seed=0):
    import zlib

    import numpy as np

    out = dict(_drawn_inputs(seed))
    spreads = {}
    factors = {'g_norm1': 3.429,
     'gmlp_ln_g': 64.0,
     'gmlp_ln_b': 57.44,
     'gmlp_bs': 29.384,
     'gla_b_gate': 3.314,
     'gla_norm_g': 45.815,
     'conv_b': 38.424,
     'router_b': 24.776,
     'g_final': 7.876,
     'g_norm2': 8.0,
     'router_w': 3.067,
     'exp_w1': 3.167,
     'exp_w3': 2.958,
     'exp_w2': 2.973}
    for name, (base, spread) in spreads.items():
        noise = np.random.default_rng([zlib.crc32(name.encode()), seed]).standard_normal(out[name].shape)
        drawn = base * np.exp(spread * noise) if base else spread * noise
        out[name] = __import__('jax').numpy.asarray(drawn.astype(out[name].dtype))
    for name, factor in factors.items():
        out[name] = (out[name] * factor).astype(out[name].dtype)
    return out
```

```python
from contextlib import ExitStack

import concourse.bass as bass
from concourse import mybir

ALU = mybir.AluOpType
ACT = mybir.ActivationFunctionType
AX = mybir.AxisListType.X
F32 = mybir.dt.float32
I32 = mybir.dt.int32

P = 128
EPS = 1e-6
TAU = 16.0
CHUNK = 64


def build(nc, x, c, w_ada, b_ada, g_norm1, g_norm2, w_in, w_out, gmlp_ln_g, gmlp_ln_b, gmlp_ws, gmlp_bs,
          gla_w_gate, gla_b_gate, gla_norm_g, conv_w, conv_b, router_w, router_b, exp_w1, exp_w3, exp_w2,
          g_final, out, cap=P):
    T, D = x.shape[1], x.shape[2]
    TILES = T // P
    KD = D // P
    PIN = w_in.shape[2]
    RANK, KDIM = gla_w_gate.shape[1], gla_w_gate.shape[2]
    VDIM = gla_norm_g.shape[1]
    ADIM = gmlp_ln_g.shape[1]
    CDIM = conv_b.shape[1]
    AH = gmlp_ws.shape[1]
    HD = ADIM // AH
    BH = 4
    DK, DV = KDIM // BH, VDIM // BH
    PAIRS = BH // 2
    E = exp_w1.shape[1]
    FF = exp_w1.shape[3]
    KF = FF // P
    GROUPS = 4
    PER = E // GROUPS
    OVER = 2 * T // cap - 1
    LISTS = T // cap
    NONE = 4 * T
    at, col = 0, {}
    for name, n in (("uv", 2 * ADIM), ("q", KDIM), ("k", KDIM), ("v", VDIM), ("g", RANK), ("og", VDIM),
                    ("cb", CDIM), ("cc", CDIM), ("cx", CDIM)):
        col[name] = at
        at += n

    x2_dram = nc.dram_tensor("x2_dram", (T, D), F32, kind="Internal").ap()
    xn2_dram = nc.dram_tensor("xn2_dram", (T, D), F32, kind="Internal").ap()
    y_dram = nc.dram_tensor("y_dram", (2 * T, D), F32, kind="Internal").ap()
    list_dram = nc.dram_tensor("list_dram", ((LISTS + 1) * cap * E, 1), I32, kind="Internal").ap()

    with ExitStack() as ctx:
        def sb(name, shape, dt=F32):
            return ctx.enter_context(nc.sbuf_tensor(name, shape, dt))[:]

        def sem(name):
            return ctx.enter_context(nc.semaphore(name))

        ident = sb("ident", [P, P])
        ones = sb("ones", [P, P])
        gate_rows = sb("gate_rows", [P, 2, D])
        mod_col = sb("mod_col", [P, 4, KD])
        scale1, scale2 = sb("scale1", [P, KD]), sb("scale2", [P, KD])
        top_w = sb("top_w", [P, TILES, 2])
        count_f = sb("count_f", [P, E])
        count_i = sb("count_i", [P, 1], I32)
        slots = sb("slots", [P, LISTS + 1, E], I32)
        slots_tok = sb("slots_tok", [P, LISTS + 1, E], I32)
        gather_idx = sb("gather_idx", [P, 2], I32)
        scatter_idx = sb("scatter_idx", [P, 2], I32)
        half = sb("half", [P, 1])
        small = sb("small", [P, 16])
        ss = small[:, 0:1]
        ms = small[:, 1:2]
        rstd = small[:, 2:3]

        ARENA = 47200
        arena = sb("arena", [P, ARENA])

        class Region:
            def __init__(self, start):
                self.at = start

            def take(self, *dims):
                n = 1
                for d in dims:
                    n *= d
                v = arena[:, self.at:self.at + n]
                self.at += n
                assert self.at <= ARENA, self.at
                if len(dims) == 2:
                    return v.rearrange("p (a b) -> p a b", a=dims[0])
                if len(dims) == 3:
                    return v.rearrange("p (a b c) -> p a b c", a=dims[0], b=dims[1])
                return v

        R = Region(0)
        win = R.take(KD, PIN)
        wout_at = R.at
        wout = R.take(KD, D)
        Z = Region(wout_at)
        wada = [Z.take(KD, 512) for _ in range(2)]
        tri, tri_ref, tri_last, strict = (R.take(P) for _ in range(4))
        chunk_ind = R.take(2)
        wsT = R.take(AH, P)
        bs_col = R.take(AH)
        ln_g, ln_b = R.take(ADIM), R.take(ADIM)
        gla_g = R.take(VDIM)
        wgate = R.take(KDIM)
        bgate = R.take(KDIM)
        rw = R.take(KD, E)
        rb = R.take(E)
        convw, convb = R.take(3, 2), R.take(2)
        g1c, g2c, cc_col = R.take(KD), R.take(KD), R.take(KD)
        rev, revg, eidx = R.take(PER), R.take(GROUPS), R.take(E)
        csil = R.take(KD)
        state = [R.take(PAIRS, 2 * DV) for _ in range(2)]
        Z = Region(R.at)
        csil_b = Z.take(KD, P)
        bada = [Z.take(512) for _ in range(2)]
        modb = Z.take(6, D)
        xt = R.take(D)
        xn = R.take(D)
        hT = R.take(KD, P)
        qkT, qeT = R.take(4, P), R.take(2, P)
        E1, E2, E3, E4 = (R.take(KDIM) for _ in range(4))
        dec = R.take(4)
        q1, qe, k2, k3 = (R.take(KDIM) for _ in range(4))
        v_sb = R.take(VDIM)
        uv = R.take(2 * ADIM)
        og = R.take(VDIM)
        lg1, lg2 = R.take(KDIM), R.take(KDIM)
        cc_sb, cb_sb, z_sb = R.take(CDIM), R.take(CDIM), R.take(CDIM)
        zT = R.take(2, P + 2)
        cbT = R.take(2, P)
        conv_acc = R.take(2, P)
        ya = R.take(ADIM)
        yT = R.take(KD, P)
        g_sb, gT = R.take(RANK), R.take(P)
        sT = R.take(2, 2, P)
        bn6, mv = R.take(6), R.take(2)
        aid = sb("aid", [P, TILES, 2], I32)
        aid_now = sb("aid_now", [P, 2], I32)
        idx_now = sb("idx_now", [P, 2], I32)
        yb, vn = xn[:, 0:VDIM], xn[:, VDIM:VDIM + ADIM]
        r_ = {n: R.take(E) for n in ("lg", "e", "p", "c", "oh1", "oh2", "p2", "sel1", "sel2", "m", "run", "a", "t")}
        g_ = {n: R.take(GROUPS) for n in ("m1", "m2", "r", "gs", "sel", "t")}
        print("stage 1 ends", R.at, Z.at, nc.sbuf_bytes_remaining)
        M = Region(0)
        W1 = [None, None]; W3 = [None, None]; W2 = [None, None]
        for s in range(2):
            W1[s], W3[s], W2[s] = M.take(KD, FF), M.take(KD, FF), M.take(KF, D)
        xg = [M.take(D) for _ in range(2)]
        xT = [M.take(KD, P) for _ in range(2)]
        hT2 = [M.take(KF, P) for _ in range(2)]
        sil, hid = M.take(FF), M.take(FF)
        y_sb = [M.take(D) for _ in range(2)]
        cnt8 = M.take(8)
        ob, cum, cum2 = M.take(E), M.take(E), M.take(E)
        le3, bidx, ob3 = M.take(OVER, E), M.take(OVER, E), M.take(OVER, E)
        eb, jb, nb, bsmall = M.take(OVER), M.take(OVER), M.take(OVER), M.take(OVER)
        table = sb("table", [P, 2, OVER], I32)
        F = Region(M.at)
        gfin = F.take(D)
        x2b = [F.take(D) for _ in range(2)]
        yy = [F.take(2, D) for _ in range(2)]
        acc = [F.take(D) for _ in range(2)]
        sq_junk = F.take(D)
        fin = sb("fin", [P, 8])

        bank = [ctx.enter_context(nc.psum_tensor(f"bank{i}", [P, 512], F32)) for i in range(8)]

        S = {}
        for n in ("params_ld", "consts", "win_ld", "wout_ld", "csil_ready", "csilb_ready", "cols_mm", "ws_tr",
                  "mod_ready", "ws_ready", "lists_clear", "list_st",
                  "x_ld", "xss", "ms1", "rstd1", "xn_ready", "x_tr", "hT_act", "hT_dve", "g_mm", "qk_mm", "v_mm",
                  "uv_mm", "og_mm", "cx_mm", "cb_mm", "g_copied", "g_tr", "gT_ready", "z_mm", "absz", "lnz", "L_ready",
                  "D_mm", "exps", "prods", "qkv_tr", "qkT_ready", "v_ready", "kv_mm", "states", "sc_mm", "sT_ready",
                  "o_mm", "oss", "oms", "ors", "yb_ready", "act_uv", "act_og", "cc_ready", "z_ready", "z_tr", "zT_ready",
                  "conv_done", "bn", "bnr", "vn0", "vn_ready", "sv_mm", "ya_ready", "y_tr", "yT_ready", "out_mm",
                  "x2_ready", "x2ss", "ms2", "rstd2", "xn2_ready", "x2_st", "x2_tr", "h2_act", "h2_dve", "r_mm",
                  "lg_ready", "e_ready", "m_ready", "pos_mm", "idx_ready", "aid_ready", "list_sc0", "list_sc1",
                  "cnt_mm", "cnt_ready", "slots_ld", "slots_ready", "tile_done",
                  "xg_zero", "xt_tr", "xT_act", "xT_dve", "h1_mm", "h3_mm", "sil_ready", "h_ready", "h_tr", "hT_ready",
                  "y_mm", "y_ready",
                  "ov_table", "ov_gidx", "ov_w", "ov_gather", "ov_tr", "ov_xT", "ov_h", "ov_sil", "ov_hid", "ov_htr", "ov_hT",
                  "ov_y", "ov_ysb", "ov_sc", "ov_iota", "gp_passed", "dve_passed", "gf_ld", "fin_ss", "fin_ms", "fin_rs", "fin_acc", "fin_out"):
            S[n] = sem(n)
        wada_ld = [sem(f"wada_ld{h}") for h in range(2)]
        mod_mm = [sem(f"mod_mm{h}") for h in range(2)]
        mod_evac = [sem(f"mod_evac{h}") for h in range(2)]
        w1_ld = [sem(f"w1_ld{h}") for h in range(2)]
        w3_ld = [sem(f"w3_ld{h}") for h in range(2)]
        w2_ld = [sem(f"w2_ld{h}") for h in range(2)]
        gath = [sem(f"gath{h}") for h in range(2)]
        scat = [sem(f"scat{h}") for h in range(2)]
        fin_ld = [sem(f"fin_ld{h}") for h in range(2)]
        fin_st = [sem(f"fin_st{h}") for h in range(2)]

        x_t = x[0].rearrange("(t p) d -> t p d", p=P)
        wada_v = w_ada[0].rearrange("(p k) n -> p k n", k=KD)
        win_v = w_in[0].rearrange("(p k) n -> p k n", k=KD)
        wout_v = w_out[0].rearrange("(k p) n -> p k n", k=KD)
        x2_t = x2_dram.rearrange("(t p) d -> t p d", p=P)
        xn2_t = xn2_dram.rearrange("(t p) d -> t p d", p=P)
        y_t = y_dram.rearrange("(t p two) d -> t p two d", p=P, two=2)
        out_t = out[0].rearrange("(t p) d -> t p d", p=P)
        list_v = list_dram.rearrange("(j s e) one -> s j (e one)", s=cap, e=E)
        w1_v = exp_w1[0].rearrange("e (p k) f -> e p (k f)", k=KD)
        w3_v = exp_w3[0].rearrange("e (p k) f -> e p (k f)", k=KD)
        w2_v = exp_w2[0].rearrange("e (p k) f -> e p (k f)", k=KF)

        def one(v, i):
            return v[bass.ds(i, 1)].rearrange("a p n -> (a p) n")

        block = ctx.enter_context(nc.Block())
        PARAMS = 17

        @block.sync
        def _(sp):
            with nc.allow_non_contiguous_dma(reason="small parameter vectors"):
                for dst, src in (
                    (cc_col, c.rearrange("a (p k) -> p (a k)", k=KD)),
                    (g1c, g_norm1.rearrange("a (p k) -> p (a k)", k=KD)),
                    (g2c, g_norm2.rearrange("a (p k) -> p (a k)", k=KD)),
                    (wsT, gmlp_ws[0].rearrange("h t s -> t h s")),
                    (bs_col, gmlp_bs[0].rearrange("h t -> t h")),
                    (ln_g, gmlp_ln_g.partition_broadcast(P).rearrange("p a n -> p (a n)")),
                    (ln_b, gmlp_ln_b.partition_broadcast(P).rearrange("p a n -> p (a n)")),
                    (gla_g, gla_norm_g.partition_broadcast(P).rearrange("p a n -> p (a n)")),
                    (wgate[0:RANK, :], gla_w_gate[0]),
                    (bgate[0:1, :], gla_b_gate),
                    (rw, router_w.rearrange("(p k) e -> p k e", k=KD)),
                    (rb, router_b.rearrange("(a e) -> a e", a=1).partition_broadcast(P).rearrange("p a n -> p (a n)")),
                    (convw[:, 0, :], conv_w[0, 0].rearrange("(t p) -> p t", p=P)),
                    (convw[:, 1, :], conv_w[0, 1].rearrange("(t p) -> p t", p=P)),
                    (convw[:, 2, :], conv_w[0, 2].rearrange("(t p) -> p t", p=P)),
                    (convb, conv_b[0].rearrange("(t p) -> p t", p=P)),
                ):
                    sp.dma_start(dst, src).then_inc(S["params_ld"], 16)
            sp.wait_ge(S["lists_clear"], 1)
            sp.dma_start(list_v, slots[0:cap]).then_inc(S["params_ld"], 16)
            with sp.Fori(0, 6) as i:
                for h in range(2):
                    sp.wait_ge(mod_mm[h], i)
                    sp.wait_ge(mod_evac[h], i)
                    sp.dma_start(wada[h], wada_v[:, :, bass.ds((2 * i + h) * 512, 512)]).then_inc(wada_ld[h], 16)
                    sp.dma_start(bada[h], b_ada[:, bass.ds((2 * i + h) * 512, 512)].partition_broadcast(P)
                                 .rearrange("p a n -> p (a n)")).then_inc(wada_ld[h], 16)
            sp.dma_start(win, win_v).then_inc(S["win_ld"], 16)
            sp.wait_ge(mod_evac[0], 6)
            sp.wait_ge(mod_evac[1], 6)
            sp.dma_start(wout, wout_v).then_inc(S["wout_ld"], 16)
            sp.wait_ge(S["mod_ready"], 1)
            with sp.Fori(0, TILES) as t:
                sp.wait_ge(S["tile_done"], t)
                sp.dma_start(xt, one(x_t, t)).then_inc(S["x_ld"], 16)
                sp.wait_ge(S["x2_ready"], t + 1)
                sp.dma_start(one(x2_t, t), xt).then_inc(S["x2_st"], 16)
                sp.wait_ge(S["xn2_ready"], t + 1)
                sp.dma_start(one(xn2_t, t), xn).then_inc(S["x2_st"], 16)
            sp.wait_ge(S["list_sc0"], 16 * TILES)
            sp.wait_ge(S["list_sc1"], 16 * TILES)
            sp.dma_start(slots[0:cap], list_v).then_inc(S["slots_ld"], 16)
            sp.wait_ge(S["tile_done"], TILES)
            sp.wait_ge(S["cnt_ready"], 1)
            for e in range(2):
                sp.dma_start(W1[e].rearrange("p k f -> p (k f)"), w1_v[e]).then_inc(w1_ld[e], 16)
                sp.dma_start(W3[e].rearrange("p k f -> p (k f)"), w3_v[e]).then_inc(w3_ld[e], 16)
                sp.dma_start(W2[e].rearrange("p k f -> p (k f)"), w2_v[e]).then_inc(w2_ld[e], 16)
            with sp.Fori(1, E // 2) as i:
                for h in range(2):
                    e = 2 * i + h
                    sp.wait_ge(S["h1_mm"], e - 1)
                    sp.dma_start(W1[h].rearrange("p k f -> p (k f)"), one(w1_v, e)).then_inc(w1_ld[h], 16)
                    sp.wait_ge(S["h3_mm"], e - 1)
                    sp.dma_start(W3[h].rearrange("p k f -> p (k f)"), one(w3_v, e)).then_inc(w3_ld[h], 16)
                    sp.wait_ge(S["y_mm"], e - 1)
                    sp.dma_start(W2[h].rearrange("p k f -> p (k f)"), one(w2_v, e)).then_inc(w2_ld[h], 16)
            sp.wait_ge(S["y_mm"], E)
            most = sp.value_load(count_i[0:1, 0:1], min_val=0, max_val=T)
            with sp.If(most > cap):
                sp.wait_ge(S["ov_table"], 1)
                with sp.Fori(0, OVER) as b:
                    sp.wait_ge(S["ov_y"], b)
                    e = sp.value_load(table[0:1, 0, bass.ds(b, 1)], min_val=0, max_val=E - 1)
                    sp.dma_start(W1[0].rearrange("p k f -> p (k f)"), one(w1_v, e)).then_inc(S["ov_w"], 16)
                    sp.dma_start(W3[0].rearrange("p k f -> p (k f)"), one(w3_v, e)).then_inc(S["ov_w"], 16)
                    sp.dma_start(W2[0].rearrange("p k f -> p (k f)"), one(w2_v, e)).then_inc(S["ov_w"], 16)
                sp.wait_ge(S["ov_sc"], 16 * OVER)
            for h in range(2):
                sp.wait_ge(scat[h], 16 * E // 2)
            sp.dma_start(gfin, g_final.rearrange("(a n) -> a n", a=1).partition_broadcast(P)
                         .rearrange("p a n -> p (a n)")).then_inc(S["gf_ld"], 16)
            with sp.Fori(0, TILES // 2) as i:
                for h in range(2):
                    t = 2 * i + h
                    sp.wait_ge(fin_st[h], 16 * i)
                    sp.dma_start(x2b[h], one(x2_t, t)).then_inc(fin_ld[h], 16)
                    sp.dma_start(yy[h], y_t[bass.ds(t, 1)].rearrange("a p two d -> (a p) two d")).then_inc(fin_ld[h], 16)
            for h in range(2):
                sp.wait_ge(fin_st[h], 16 * TILES // 2)

        @block.gpsimd
        def _(gp):
            gp.memset(half, -0.5)
            gp.memset(ident, 0.0)
            gp.memset(ones, 1.0)
            gp.memset(slots.rearrange("p a b -> p (a b)"), NONE).then_inc(S["lists_clear"], 1)
            for m in (tri, tri_ref, tri_last):
                gp.memset(m, 1.0 / TAU)
            gp.memset(chunk_ind, 1.0 / TAU)
            gp.memset(strict, 1.0)
            gp.iota(rev, pattern=[[-1, PER]], base=PER, channel_multiplier=0, allow_small_or_imprecise_dtypes=True)
            gp.iota(revg, pattern=[[-1, GROUPS]], base=GROUPS, channel_multiplier=0, allow_small_or_imprecise_dtypes=True)
            gp.iota(eidx, pattern=[[1, E]], base=0, channel_multiplier=0, allow_small_or_imprecise_dtypes=True)
            gp.iota(aid, pattern=[[2 * P, TILES], [1, 2]], base=0, channel_multiplier=2)
            gp.drain()

            def keep(v, base, per_row, per_col, n, op=ALU.is_ge, fill=0.0):
                gp.affine_select(out=v, in_=v, pattern=[[per_col, n]], compare_op=op, fill=fill, base=base,
                                 channel_multiplier=per_row)
                gp.drain()

            C = CHUNK
            keep(ident, 0, 1, -1, P, ALU.not_equal, 1.0)
            keep(strict, -1, -1, 1, P)
            keep(tri, 0, -1, 1, P)
            keep(tri[:, C:P], -C, 1, 0, C)
            keep(tri_last, -1, 1, -1, P)
            keep(tri_last[:, 0:C], C - 1, -1, 0, C)
            keep(tri_ref[:, 0:C], C // 2, -1, 0, C)
            keep(tri_ref[:, C:P], C + C // 2, -1, 0, C)
            keep(tri_ref[:, C:P], -C, 1, 0, C)
            keep(chunk_ind[:, 0:1], C - 1, -1, 0, 1)
            keep(chunk_ind[:, 1:2], -C, 1, 0, 1)
            gp.tensor_tensor(tri_ref, tri, tri_ref, ALU.subtract).then_inc(S["consts"], 1)

            def powers(dst, src, n, wait, value, done):
                gp.wait_ge(wait, value)
                gp.tensor_tensor(dst, src, half.to_broadcast([P, n]) if n > 1 else half[:, 0:1], ALU.pow).then_inc(done, 1)

            with gp.Fori(0, TILES) as t:
                gp.tensor_copy(aid_now, aid[:, bass.ds(t, 1), :].rearrange("p a b -> p (a b)")).then_inc(S["aid_ready"], 1)
                powers(rstd, ms, 1, S["ms1"], t + 1, S["rstd1"])
                powers(small[:, 4:5], small[:, 3:4], 1, S["bn"], t + 1, S["bnr"])
                gp.wait_ge(S["vn0"], t + 1)
                gp.tensor_tensor(vn, vn, ln_g, ALU.mult)
                gp.drain()
                gp.tensor_tensor(vn, vn, ln_b, ALU.add).then_inc(S["vn_ready"], 1)
                powers(small[:, 12:16], small[:, 8:12], 4, S["oms"], t + 1, S["ors"])
                powers(rstd, ms, 1, S["ms2"], t + 1, S["rstd2"])
                gp.wait_ge(S["idx_ready"], t + 1)
                gp.sem_inc(S["gp_passed"], 1)
                for k in range(2):
                    gp.indirect_dma_start(out=list_dram, out_offset=bass.IndirectOffsetOnAxis(ap=idx_now[:, k:k + 1], axis=0),
                                          in_=aid_now[:, k:k + 1], in_offset=None, bounds_check=LISTS * cap * E - 1,
                                          oob_is_err=False).then_inc(S[f"list_sc{k}"], 16)
                for k in range(2):
                    gp.wait_ge(S[f"list_sc{k}"], 16 * t + 16)

            for s in range(2):
                gp.wait_ge(S["tile_done"], TILES)
                gp.memset(xg[s], 0.0)
            gp.wait_ge(S["slots_ready"], 1)
            gp.wait_ge(S["x2_st"], 32 * TILES)
            gp.drain()

            def gather(e, h):
                gp.tensor_copy(gather_idx[:, h:h + 1], slots_tok[:, 0, bass.ds(e, 1)] if not isinstance(e, int) else slots_tok[:, 0, e:e + 1])
                gp.drain()
                gp.indirect_dma_start(out=xg[h], out_offset=None, in_=xn2_dram,
                                      in_offset=bass.IndirectOffsetOnAxis(ap=gather_idx[:, h:h + 1], axis=0),
                                      bounds_check=T - 1, oob_is_err=False).then_inc(gath[h], 16)

            def scatter(e, h):
                gp.tensor_copy(scatter_idx[:, h:h + 1], slots[:, 0, bass.ds(e, 1)] if not isinstance(e, int) else slots[:, 0, e:e + 1])
                gp.drain()
                gp.wait_ge(S["y_ready"], e + 1)
                gp.sem_inc(S["gp_passed"], 1)
                gp.indirect_dma_start(out=y_dram, out_offset=bass.IndirectOffsetOnAxis(ap=scatter_idx[:, h:h + 1], axis=0),
                                      in_=y_sb[h], in_offset=None, bounds_check=2 * T - 1,
                                      oob_is_err=False).then_inc(scat[h], 16)

            gather(0, 0)
            gather(1, 1)
            for e in range(2):
                gp.wait_ge(S["xt_tr"], e + 1)
                gp.wait_ge(gath[e], 16)
                gather(e + 2, e)
                scatter(e, e)
            with gp.Fori(1, E // 2 - 1) as i:
                for h in range(2):
                    e = 2 * i + h
                    gp.wait_ge(S["xt_tr"], e + 1)
                    gp.wait_ge(gath[h], 16 * i + 16)
                    gather(e + 2, h)
                    gp.wait_ge(scat[h], 16 * i)
                    scatter(e, h)
            for h in range(2):
                gp.wait_ge(scat[h], 16 * (E // 2 - 1))
                scatter(E - 2 + h, h)
            most = gp.value_load(count_i[0:1, 0:1], min_val=0, max_val=T)
            with gp.If(most > cap):
                gp.iota(bidx.rearrange("p a b -> p (a b)"), pattern=[[1, OVER], [0, E]], base=0, channel_multiplier=0,
                        allow_small_or_imprecise_dtypes=True)
                gp.iota(nb, pattern=[[1, OVER]], base=0, channel_multiplier=0,
                        allow_small_or_imprecise_dtypes=True).then_inc(S["ov_iota"], 1)
                gp.wait_ge(S["ov_table"], 1)
                for h in range(2):
                    gp.wait_ge(scat[h], 16 * E // 2)
                with gp.Fori(0, OVER) as b:
                    at_ = gp.value_load(table[0:1, 1, bass.ds(b, 1)], min_val=0, max_val=(LISTS + 1) * E - 1)
                    gp.tensor_copy(gather_idx[:, 0:1], slots_tok.rearrange("p a b -> p (a b)")[:, bass.ds(at_, 1)])
                    gp.tensor_copy(scatter_idx[:, 0:1], slots.rearrange("p a b -> p (a b)")[:, bass.ds(at_, 1)])
                    gp.drain()
                    gp.wait_ge(S["ov_tr"], b)
                    gp.sem_inc(S["gp_passed"], 1)
                    gp.indirect_dma_start(out=xg[0], out_offset=None, in_=xn2_dram,
                                          in_offset=bass.IndirectOffsetOnAxis(ap=gather_idx[:, 0:1], axis=0),
                                          bounds_check=T - 1, oob_is_err=False).then_inc(S["ov_gather"], 16)
                    gp.wait_ge(S["ov_ysb"], b + 1)
                    gp.sem_inc(S["gp_passed"], 1)
                    gp.indirect_dma_start(out=y_dram, out_offset=bass.IndirectOffsetOnAxis(ap=scatter_idx[:, 0:1], axis=0),
                                          in_=y_sb[0], in_offset=None, bounds_check=2 * T - 1,
                                          oob_is_err=False).then_inc(S["ov_sc"], 16)
                    gp.wait_ge(S["ov_gather"], 16 * b + 16)
                    gp.wait_ge(S["ov_sc"], 16 * b + 16)
            with gp.Fori(0, TILES) as t:
                powers(fin[:, 2:3], fin[:, 1:2], 1, S["fin_ms"], t + 1, S["fin_rs"])

        @block.tensor
        def _(pe):
            pe.wait_ge(S["csilb_ready"], 1)
            with pe.Fori(0, 6) as i:
                for h in range(2):
                    pe.wait_ge(wada_ld[h], 32 * i + 32)
                    pe.wait_ge(mod_evac[h], i)
                    for k in range(KD):
                        mm = pe.matmul(bank[h][:], csil_b[:, k, :], wada[h][:, k, :], start=(k == 0), stop=(k == KD - 1))
                    mm.then_inc(mod_mm[h], 1)
            pe.wait_ge(mod_evac[0], 6)
            pe.wait_ge(mod_evac[1], 6)
            pe.wait_ge(S["consts"], 1)
            for n, piece in enumerate((0, 1, 3, 4)):
                row = modb[0:1, piece, :].rearrange("p (m k) -> p k m", k=KD)
                for k in range(KD):
                    mm = pe.matmul(bank[2][:, n * KD + k:n * KD + k + 1], row[:, k, :], ones[0:1, 0:1], start=True, stop=True)
            mm.then_inc(S["cols_mm"], 1)
            pe.wait_ge(S["params_ld"], 16 * PARAMS)
            for h in range(AH):
                mm = pe.transpose(bank[3][:, h * P:(h + 1) * P], wsT[:, h, :], ident[:])
            mm.then_inc(S["ws_tr"], 1)
            pe.wait_ge(S["ws_ready"], 1)
            pe.wait_ge(S["mod_ready"], 1)
            pe.wait_ge(S["win_ld"], 16)
            pe.wait_ge(S["wout_ld"], 16)

            def rows(out_, c0, n):
                for k in range(KD):
                    mm = pe.matmul(out_, hT[:, k, :], win[:, k, c0:c0 + n], start=(k == 0), stop=(k == KD - 1))
                return mm

            def transpose8(src, done):
                cols = src.rearrange("p (m k) -> p k m", k=KD)
                for k in range(KD):
                    mm = pe.transpose(bank[k // 4][:, (k % 4) * P:(k % 4 + 1) * P], cols[:, k, :], ident[:])
                mm.then_inc(done, 1)

            with pe.Fori(0, TILES) as t:
                pe.wait_ge(S["xn_ready"], t + 1)
                transpose8(xn, S["x_tr"])
                pe.wait_ge(S["hT_act"], t + 1)
                pe.wait_ge(S["hT_dve"], t + 1)
                rows(bank[2][:, 0:RANK], col["g"], RANK).then_inc(S["g_mm"], 1)
                rows(bank[3][:], col["q"], 2 * KDIM).then_inc(S["qk_mm"], 1)
                pe.wait_ge(S["g_copied"], t + 1)
                pe.transpose(bank[2][0:RANK, 0:P], g_sb, ident[:]).then_inc(S["g_tr"], 1)
                rows(bank[4][:], col["v"], VDIM).then_inc(S["v_mm"], 1)
                pe.wait_ge(S["gT_ready"], t + 1)
                pe.matmul(bank[2][:, 0:KDIM], gT[0:RANK, :], wgate[0:RANK, :], start=True, stop=False)
                pe.matmul(bank[2][:, 0:KDIM], ones[0:1, :], bgate[0:1, :], start=False, stop=True).then_inc(S["z_mm"], 1)
                rows(bank[5][:], col["uv"], 2 * ADIM).then_inc(S["uv_mm"], 1)
                rows(bank[6][:], col["og"], VDIM).then_inc(S["og_mm"], 1)
                rows(bank[7][:], col["cc"], 2 * CDIM).then_inc(S["cx_mm"], 1)
                rows(bank[0][:, 0:CDIM], col["cb"], CDIM).then_inc(S["cb_mm"], 1)
                pe.wait_ge(S["L_ready"], t + 1)
                pe.matmul(bank[1][:, 0:KDIM], tri, lg1, start=True, stop=True)
                pe.matmul(bank[1][:, KDIM:2 * KDIM], tri_ref, lg1, start=True, stop=True)
                pe.matmul(bank[2][:, 0:KDIM], tri_last, lg1, start=True, stop=True)
                for p in range(PAIRS):
                    mm = pe.matmul(bank[2][:, KDIM + 2 * p:KDIM + 2 * p + 2], lg1[:, p * P:(p + 1) * P], chunk_ind,
                                   start=True, stop=True)
                mm.then_inc(S["D_mm"], 1)
                pe.wait_ge(S["z_ready"], t + 1)
                pe.wait_ge(S["cc_ready"], 2 * t + 2)
                for j in range(2):
                    pe.transpose(bank[7][:, j * P:(j + 1) * P], z_sb[:, j * P:(j + 1) * P], ident[:])
                for j in range(2):
                    mm = pe.transpose(bank[7][:, (2 + j) * P:(3 + j) * P], cb_sb[:, j * P:(j + 1) * P], ident[:])
                mm.then_inc(S["z_tr"], 1)
                pe.wait_ge(S["prods"], t + 1)
                pe.wait_ge(S["act_uv"], t + 1)
                for j in range(2):
                    pe.transpose(bank[0][:, j * P:(j + 1) * P], q1[:, j * P:(j + 1) * P], ident[:])
                    pe.transpose(bank[0][:, (2 + j) * P:(3 + j) * P], k2[:, j * P:(j + 1) * P], ident[:])
                    mm = pe.transpose(bank[5][:, j * P:(j + 1) * P], qe[:, j * P:(j + 1) * P], ident[:])
                mm.then_inc(S["qkv_tr"], 1)
                pe.wait_ge(S["v_ready"], t + 1)
                for ch in range(2):
                    r = slice(ch * CHUNK, (ch + 1) * CHUNK)
                    for p in range(PAIRS):
                        mm = pe.matmul(bank[3 + ch][:, p * 2 * DV:(p + 1) * 2 * DV], k3[r, p * P:(p + 1) * P],
                                       v_sb[r, p * 2 * DV:(p + 1) * 2 * DV], start=True, stop=True)
                mm.then_inc(S["kv_mm"], 1)
                pe.wait_ge(S["qkT_ready"], t + 1)
                for hh in range(2):
                    r = slice(hh * DK, (hh + 1) * DK)
                    for p in range(PAIRS):
                        mm = pe.matmul(bank[1 + hh][:, p * P:(p + 1) * P], qkT[r, 2 + p, :], qkT[r, p, :],
                                       start=True, stop=True)
                mm.then_inc(S["sc_mm"], 1)
                pe.wait_ge(S["vn_ready"], t + 1)
                pe.wait_ge(S["zT_ready"], t + 1)
                for h in range(AH):
                    mm = pe.matmul(bank[7][:, h * HD:(h + 1) * HD], wsT[:, h, :], vn[:, h * HD:(h + 1) * HD],
                                   start=True, stop=True)
                mm.then_inc(S["sv_mm"], 1)
                pe.wait_ge(S["sT_ready"], t + 1)
                pe.wait_ge(S["states"], 2 * t + 1)
                pe.wait_ge(S["act_og"], t + 1)
                for p in range(PAIRS):
                    cols = slice(p * 2 * DV, (p + 1) * 2 * DV)
                    for ch in range(2):
                        r = slice(ch * CHUNK, (ch + 1) * CHUNK)
                        pe.matmul(bank[6][r, cols], qeT[:, p, r], state[ch][:, p, :], start=True, stop=False,
                                  skip_group_check=True)
                    for hh in range(2):
                        h = 2 * p + hh
                        mm = pe.matmul(bank[6][:, h * DV:(h + 1) * DV], sT[:, hh, p, :], v_sb[:, h * DV:(h + 1) * DV],
                                       start=False, stop=True, skip_group_check=True)
                mm.then_inc(S["o_mm"], 1)
                pe.wait_ge(S["ya_ready"], t + 1)
                for j in range(2):
                    pe.transpose(bank[0][:, j * P:(j + 1) * P], ya[:, j * P:(j + 1) * P], ident[:])
                pe.wait_ge(S["yb_ready"], t + 1)
                for j in range(4):
                    dst = bank[0][:, (2 + j) * P:(3 + j) * P] if j < 2 else bank[3][:, (j - 2) * P:(j - 1) * P]
                    mm = pe.transpose(dst, yb[:, j * P:(j + 1) * P], ident[:])
                mm.then_inc(S["y_tr"], 1)
                pe.wait_ge(S["yT_ready"], t + 1)
                pe.wait_ge(S["conv_done"], t + 1)
                for n in range(2):
                    for k in range(KD):
                        mm = pe.matmul(bank[4 + n][:], yT[:, k, :], wout[:, k, n * 512:(n + 1) * 512],
                                       start=(k == 0), stop=(k == KD - 1))
                mm.then_inc(S["out_mm"], 1)
                pe.wait_ge(S["xn2_ready"], t + 1)
                transpose8(xn, S["x2_tr"])
                pe.wait_ge(S["h2_act"], t + 1)
                pe.wait_ge(S["h2_dve"], t + 1)
                for k in range(KD):
                    mm = pe.matmul(bank[2][:, 0:E], hT[:, k, :], rw[:, k, :], start=(k == 0), stop=(k == KD - 1))
                mm.then_inc(S["r_mm"], 1)
                pe.wait_ge(S["m_ready"], t + 1)
                pe.matmul(bank[3][:, 0:E], strict, r_["m"], start=True, stop=False)
                pe.matmul(bank[3][:, 0:E], ones[:], r_["run"], start=False, stop=True).then_inc(S["pos_mm"], 1)
            pe.wait_ge(S["tile_done"], TILES)
            pe.matmul(bank[4][:, 0:E], ones[:], r_["run"], start=True, stop=True).then_inc(S["cnt_mm"], 1)

            def x_turn(h, n, done, gsem):
                pe.wait_ge(gsem, n)
                cols = xg[h].rearrange("p (m k) -> p k m", k=KD)
                for k in range(KD):
                    mm = pe.transpose(bank[k // 4][:, (k % 4) * P:(k % 4 + 1) * P], cols[:, k, :], ident[:])
                mm.then_inc(done, 1)

            def up(h, n, e):
                pe.wait_ge(S["xT_act"], e + 1)
                pe.wait_ge(S["xT_dve"], e + 1)
                pe.wait_ge(w1_ld[h], 16 * n + 16)
                pe.wait_ge(S["sil_ready"], e)
                for k in range(KD):
                    mm = pe.matmul(bank[2][:], xT[h][:, k, :], W1[h][:, k, :], start=(k == 0), stop=(k == KD - 1))
                mm.then_inc(S["h1_mm"], 1)
                pe.wait_ge(w3_ld[h], 16 * n + 16)
                pe.wait_ge(S["h_ready"], e)
                for k in range(KD):
                    mm = pe.matmul(bank[3][:], xT[h][:, k, :], W3[h][:, k, :], start=(k == 0), stop=(k == KD - 1))
                mm.then_inc(S["h3_mm"], 1)

            def h_turn(h, e):
                pe.wait_ge(S["h_ready"], e + 1)
                pe.wait_ge(S["hT_ready"], e)
                cols = hid.rearrange("p (m k) -> p k m", k=KF)
                for k in range(KF):
                    mm = pe.transpose(bank[4][:, k * P:(k + 1) * P], cols[:, k, :], ident[:])
                mm.then_inc(S["h_tr"], 1)

            def down(h, n, e):
                pe.wait_ge(S["hT_ready"], e + 1)
                pe.wait_ge(w2_ld[h], 16 * n + 16)
                pe.wait_ge(S["y_ready"], e)
                for j in range(2):
                    for k in range(KF):
                        mm = pe.matmul(bank[5 + j][:], hT2[h][:, k, :], W2[h][:, k, j * 512:(j + 1) * 512],
                                       start=(k == 0), stop=(k == KF - 1))
                mm.then_inc(S["y_mm"], 1)

            x_turn(0, 16, S["xt_tr"], gath[0])
            up(0, 0, 0)
            x_turn(1, 16, S["xt_tr"], gath[1])
            h_turn(0, 0)
            with pe.Fori(0, E // 2 - 1) as i:
                for h, e, n in ((1, 2 * i + 1, i), (0, 2 * i + 2, i + 1)):
                    up(h, n, e)
                    x_turn(1 - h, 16 * (i + 1) + 16, S["xt_tr"], gath[1 - h])
                    down(1 - h, i, e - 1)
                    h_turn(h, e)
            up(1, E // 2 - 1, E - 1)
            down(0, E // 2 - 1, E - 2)
            h_turn(1, E - 1)
            down(1, E // 2 - 1, E - 1)
            most = pe.value_load(count_i[0:1, 0:1], min_val=0, max_val=T)
            with pe.If(most > cap):
                with pe.Fori(0, OVER) as b:
                    x_turn(0, 16 * b + 16, S["ov_tr"], S["ov_gather"])
                    pe.wait_ge(S["ov_xT"], b + 1)
                    pe.wait_ge(S["ov_w"], 48 * b + 48)
                    for w, bk in ((W1[0], 2), (W3[0], 3)):
                        for k in range(KD):
                            mm = pe.matmul(bank[bk][:], xT[0][:, k, :], w[:, k, :], start=(k == 0), stop=(k == KD - 1))
                    mm.then_inc(S["ov_h"], 1)
                    pe.wait_ge(S["ov_hid"], b + 1)
                    cols = hid.rearrange("p (m k) -> p k m", k=KF)
                    for k in range(KF):
                        mm = pe.transpose(bank[4][:, k * P:(k + 1) * P], cols[:, k, :], ident[:])
                    mm.then_inc(S["ov_htr"], 1)
                    pe.wait_ge(S["ov_hT"], b + 1)
                    for j in range(2):
                        for k in range(KF):
                            mm = pe.matmul(bank[5 + j][:], hT2[0][:, k, :], W2[0][:, k, j * 512:(j + 1) * 512],
                                           start=(k == 0), stop=(k == KF - 1))
                    mm.then_inc(S["ov_y"], 1)

        @block.scalar
        def _(act):
            act.wait_ge(S["params_ld"], 16 * PARAMS)
            act.activation(csil, cc_col, ACT.Silu).then_inc(S["csil_ready"], 1)
            with act.Fori(0, TILES) as t:
                act.wait_ge(S["x_ld"], 16 * t + 16)
                act.activation(hT.rearrange("p a b -> p (a b)"), xt, ACT.Square, accum_out=ss)
                act.drain().then_inc(S["xss"], 1)
                act.wait_ge(S["x_tr"], t + 1)
                for k in range(4):
                    ins = act.activation(hT[:, k, :], bank[0][:, k * P:(k + 1) * P], ACT.Identity,
                                         scale=scale1[:, k:k + 1], bias=mod_col[:, 0, k:k + 1])
                ins.then_inc(S["hT_act"], 1)
                act.wait_ge(S["g_mm"], t + 1)
                act.copy(g_sb, bank[2][:, 0:RANK]).then_inc(S["g_copied"], 1)
                act.wait_ge(S["g_tr"], t + 1)
                act.copy(gT[0:RANK, :], bank[2][0:RANK, 0:P]).then_inc(S["gT_ready"], 1)
                act.wait_ge(S["v_mm"], t + 1)
                act.copy(v_sb, bank[4][:]).then_inc(S["v_ready"], 1)
                act.wait_ge(S["absz"], t + 1)
                act.activation(lg2, lg2, ACT.Exp)
                act.drain()
                act.activation(lg2, lg2, ACT.Ln, bias=1.0).then_inc(S["lnz"], 1)
                act.wait_ge(S["cx_mm"], t + 1)
                act.copy(cc_sb, bank[7][:, 0:CDIM]).then_inc(S["cc_ready"], 1)
                act.wait_ge(S["cb_mm"], t + 1)
                act.copy(cb_sb, bank[0][:, 0:CDIM])
                act.drain().then_inc(S["cc_ready"], 1)
                act.wait_ge(S["D_mm"], t + 1)
                act.activation(E4, bank[1][:, 0:KDIM], ACT.Exp)
                act.activation(E1, bank[1][:, KDIM:2 * KDIM], ACT.Exp)
                act.activation(E2, bank[1][:, KDIM:2 * KDIM], ACT.Exp, scale=-1.0)
                act.activation(E3, bank[2][:, 0:KDIM], ACT.Exp)
                act.activation(dec, bank[2][:, KDIM:KDIM + 4], ACT.Exp)
                act.drain().then_inc(S["exps"], 1)
                act.wait_ge(S["uv_mm"], t + 1)
                act.activation(uv, bank[5][:], ACT.Gelu).then_inc(S["act_uv"], 1)
                act.wait_ge(S["og_mm"], t + 1)
                act.activation(og, bank[6][:], ACT.Silu).then_inc(S["act_og"], 1)
                act.wait_ge(S["z_tr"], t + 1)
                act.wait_ge(S["conv_done"], t)
                act.copy(zT[:, :, 2:], bank[7][:, 0:2 * P].rearrange("p (a b) -> p a b", a=2))
                act.copy(cbT, bank[7][:, 2 * P:4 * P].rearrange("p (a b) -> p a b", a=2))
                act.drain().then_inc(S["zT_ready"], 1)
                act.wait_ge(S["qkv_tr"], t + 1)
                act.copy(qkT.rearrange("p a b -> p (a b)"), bank[0][:])
                act.copy(qeT.rearrange("p a b -> p (a b)"), bank[5][:, 0:2 * P])
                act.drain().then_inc(S["qkT_ready"], 1)
                act.wait_ge(S["o_mm"], t + 1)
                for h in range(BH):
                    act.activation(q1[:, 0:DV], bank[6][:, h * DV:(h + 1) * DV], ACT.Square, accum_out=fin[:, 4 + h:5 + h])
                    act.drain()
                act.drain().then_inc(S["oss"], 1)
                act.wait_ge(S["y_tr"], t + 1)
                act.copy(yT[:, 0:4, :].rearrange("p a b -> p (a b)"), bank[0][:])
                act.copy(yT[:, 4:6, :].rearrange("p a b -> p (a b)"), bank[3][:, 0:2 * P])
                act.drain().then_inc(S["yT_ready"], 1)
                act.wait_ge(S["x2_ready"], t + 1)
                act.activation(hT.rearrange("p a b -> p (a b)"), xt, ACT.Square, accum_out=ss)
                act.drain().then_inc(S["x2ss"], 1)
                act.wait_ge(S["x2_tr"], t + 1)
                for k in range(4):
                    ins = act.activation(hT[:, k, :], bank[0][:, k * P:(k + 1) * P], ACT.Identity,
                                         scale=scale2[:, k:k + 1], bias=mod_col[:, 2, k:k + 1])
                ins.then_inc(S["h2_act"], 1)
                act.wait_ge(S["lg_ready"], t + 1)
                act.activation(r_["e"], r_["lg"], ACT.Exp, bias=small[:, 5:6], accum_out=small[:, 6:7])
                act.drain().then_inc(S["e_ready"], 1)

            def x_evac(h, e, turned, done):
                act.wait_ge(turned, e + 1)
                for k in range(4):
                    ins = act.activation(xT[h][:, k, :], bank[0][:, k * P:(k + 1) * P], ACT.Identity,
                                         scale=scale2[:, k:k + 1], bias=mod_col[:, 2, k:k + 1])
                ins.then_inc(done, 1)

            def silu(e):
                act.wait_ge(S["h1_mm"], e + 1)
                act.wait_ge(S["h_ready"], e)
                act.activation(sil, bank[2][:], ACT.Silu).then_inc(S["sil_ready"], 1)

            def h_evac(h, e):
                act.wait_ge(S["h_tr"], e + 1)
                act.copy(hT2[h].rearrange("p a b -> p (a b)"), bank[4][:]).then_inc(S["hT_ready"], 1)

            act.wait_ge(S["tile_done"], TILES)
            x_evac(0, 0, S["xt_tr"], S["xT_act"])
            silu(0)
            x_evac(1, 1, S["xt_tr"], S["xT_act"])
            h_evac(0, 0)
            with act.Fori(0, E // 2 - 1) as i:
                for h, e in ((1, 2 * i + 1), (0, 2 * i + 2)):
                    silu(e)
                    x_evac(1 - h, e + 1, S["xt_tr"], S["xT_act"])
                    act.wait_ge(S["y_mm"], e - 1)
                    h_evac(h, e)
            silu(E - 1)
            act.wait_ge(S["y_mm"], E - 2)
            h_evac(1, E - 1)
            most = act.value_load(count_i[0:1, 0:1], min_val=0, max_val=T)
            with act.If(most > cap):
                with act.Fori(0, OVER) as b:
                    act.wait_ge(S["ov_tr"], b + 1)
                    act.wait_ge(S["y_mm"], E)
                    for k in range(KD):
                        ins = act.activation(xT[0][:, k, :], bank[k // 4][:, (k % 4) * P:(k % 4 + 1) * P], ACT.Identity,
                                             scale=scale2[:, k:k + 1], bias=mod_col[:, 2, k:k + 1])
                    ins.then_inc(S["ov_xT"], 1)
                    act.wait_ge(S["ov_h"], b + 1)
                    act.activation(sil, bank[2][:], ACT.Silu).then_inc(S["ov_sil"], 1)
                    act.wait_ge(S["ov_htr"], b + 1)
                    act.copy(hT2[0].rearrange("p a b -> p (a b)"), bank[4][:]).then_inc(S["ov_hT"], 1)
            with act.Fori(0, TILES // 2) as i:
                for h in range(2):
                    t = 2 * i + h
                    act.wait_ge(S["fin_acc"], t + 1)
                    act.activation(sq_junk, acc[h], ACT.Square, accum_out=fin[:, 0:1])
                    act.drain().then_inc(S["fin_ss"], 1)
                    act.wait_ge(S["fin_out"], t + 1)
                    act.dma_start(one(out_t, t), acc[h]).then_inc(fin_st[h], 16)

        @block.vector
        def _(dve):
            TT, TS, STT = dve.tensor_tensor, dve.tensor_scalar, dve.scalar_tensor_tensor
            dve.wait_ge(S["csil_ready"], 1)
            dve.tensor_copy(csil_b, csil.unsqueeze(2).to_broadcast([P, KD, P])).then_inc(S["csilb_ready"], 1)
            with dve.Fori(0, 6) as i:
                for h in range(2):
                    dve.wait_ge(mod_mm[h], i + 1)
                    dve.wait_ge(wada_ld[h], 32 * i + 32)
                    TT(modb.rearrange("p a b -> p (a b)")[:, bass.ds((2 * i + h) * 512, 512)], bank[h][:], bada[h],
                       ALU.add).then_inc(mod_evac[h], 1)
            dve.drain()
            for n, piece in enumerate((2, 5)):
                dve.tensor_copy(gate_rows[:, n, :], modb[:, piece, :])
            dve.wait_ge(S["cols_mm"], 1)
            dve.wait_ge(S["params_ld"], 16 * PARAMS)
            dve.tensor_copy(mod_col.rearrange("p a b -> p (a b)"), bank[2][:, 0:4 * KD])
            dve.drain()
            STT(scale1[:], mod_col[:, 1, :], 1.0, g1c, ALU.add, ALU.mult)
            STT(scale2[:], mod_col[:, 3, :], 1.0, g2c, ALU.add, ALU.mult)
            dve.wait_ge(S["ws_tr"], 1)
            dve.tensor_copy(wsT.rearrange("p a b -> p (a b)"), bank[3][:])
            dve.drain()
            dve.memset(wsT[CHUNK:P, :, 0:CHUNK], 0.0)
            for s in range(2):
                dve.memset(state[s].rearrange("p a b -> p (a b)"), 0.0)
            dve.memset(zT.rearrange("p a b -> p (a b)"), 0.0)
            dve.memset(sT.rearrange("p a b c -> p (a b c)"), 0.0)
            dve.memset(r_["run"], 0.0)
            dve.drain().then_inc(S["ws_ready"], 1)
            dve.wait_ge(S["ws_ready"], 1)
            dve.sem_inc(S["mod_ready"], 1)

            def mean_sq(src, dst, n, done):
                TS(dst, src, 1.0 / n, EPS, ALU.mult, ALU.add).then_inc(done, 1)

            with dve.Fori(0, TILES) as t:
                dve.wait_ge(S["xss"], t + 1)
                mean_sq(ss, ms, D, S["ms1"])
                dve.wait_ge(S["rstd1"], t + 1)
                TS(xn, xt, rstd, None, ALU.mult).then_inc(S["xn_ready"], 1)
                dve.wait_ge(S["x_tr"], t + 1)
                dve.wait_ge(S["hT_act"], t + 1)
                for k in range(4, 8):
                    ins = TS(hT[:, k, :], bank[1][:, (k - 4) * P:(k - 3) * P], scale1[:, k:k + 1], mod_col[:, 0, k:k + 1],
                             ALU.mult, ALU.add)
                ins.then_inc(S["hT_dve"], 1)
                dve.wait_ge(S["z_mm"], t + 1)
                TS(lg1, bank[2][:, 0:KDIM], 0.0, None, ALU.min)
                dve.drain()
                STT(lg2, lg1, 2.0, bank[2][:, 0:KDIM], ALU.mult, ALU.subtract).then_inc(S["absz"], 1)
                dve.wait_ge(S["lnz"], t + 1)
                TT(lg1, lg1, lg2, ALU.subtract).then_inc(S["L_ready"], 1)
                dve.wait_ge(S["cc_ready"], 2 * t + 1)
                TT(z_sb, bank[7][:, CDIM:2 * CDIM], cc_sb, ALU.mult)
                dve.drain().then_inc(S["z_ready"], 1)
                dve.wait_ge(S["exps"], t + 1)
                STT(q1, bank[3][:, 0:KDIM], DK ** -0.5, E1, ALU.mult, ALU.mult)
                STT(qe, bank[3][:, 0:KDIM], DK ** -0.5, E4, ALU.mult, ALU.mult)
                TT(k2, bank[3][:, KDIM:], E2, ALU.mult)
                TT(k3, bank[3][:, KDIM:], E3, ALU.mult)
                dve.drain().then_inc(S["prods"], 1)
                dve.wait_ge(S["act_uv"], t + 1)
                dve.bn_stats(bn6, uv[:, ADIM:])
                dve.drain()
                dve.bn_aggr(mv, bn6)
                dve.drain()
                TS(small[:, 3:4], mv[:, 1:2], EPS, None, ALU.add).then_inc(S["bn"], 1)
                dve.wait_ge(S["bnr"], t + 1)
                dve.wait_ge(S["x_tr"], t + 1)
                TS(vn, uv[:, ADIM:], mv[:, 0:1], small[:, 4:5], ALU.subtract, ALU.mult).then_inc(S["vn0"], 1)
                dve.wait_ge(S["kv_mm"], t + 1)

                def step(src, dst, ch):
                    for p in range(PAIRS):
                        for hh in range(2):
                            r = slice(hh * DK, (hh + 1) * DK)
                            cc_ = slice(hh * DV, (hh + 1) * DV)
                            STT(dst[r, p, cc_], src[r, p, cc_], dec[r, 2 * p + ch:2 * p + ch + 1],
                                bank[3 + ch][r, p * 2 * DV + hh * DV:p * 2 * DV + (hh + 1) * DV], ALU.mult, ALU.add)

                step(state[0], state[1], 0)
                dve.drain().then_inc(S["states"], 1)
                dve.wait_ge(S["sc_mm"], t + 1)
                dve.sem_inc(S["dve_passed"], 1)
                for hh in range(2):
                    dve.copy_predicated(sT[:, hh], tri.bitcast(I32).unsqueeze(1).to_broadcast([P, 2, P]),
                                        bank[1 + hh][:, 0:2 * P].rearrange("p (a b) -> p a b", a=2))
                dve.drain().then_inc(S["sT_ready"], 1)
                dve.wait_ge(S["zT_ready"], t + 1)
                for j in range(2):
                    TS(conv_acc[:, j, :], zT[:, j, 0:P], convw[:, 0, j:j + 1], convb[:, j:j + 1], ALU.mult, ALU.add)
                dve.drain()
                for s in (1, 2):
                    for j in range(2):
                        STT(conv_acc[:, j, :], zT[:, j, s:s + P], convw[:, s, j:j + 1], conv_acc[:, j, :], ALU.mult, ALU.add)
                    dve.drain()
                TT(yT[:, 6:8, :], conv_acc, cbT, ALU.mult)
                dve.tensor_copy(zT[:, :, 0:2], zT[:, :, P:P + 2])
                dve.drain().then_inc(S["conv_done"], 1)
                dve.wait_ge(S["sv_mm"], t + 1)
                for h in range(AH):
                    c_ = slice(h * HD, (h + 1) * HD)
                    STT(ya[:, c_], bank[7][:, c_], bs_col[:, h:h + 1], uv[:, c_], ALU.add, ALU.mult)
                dve.drain().then_inc(S["ya_ready"], 1)
                dve.wait_ge(S["oss"], t + 1)
                step(state[1], state[0], 1)
                dve.drain().then_inc(S["states"], 1)
                mean_sq(fin[:, 4:8], small[:, 8:12], DV, S["oms"])
                dve.wait_ge(S["ors"], t + 1)
                for h in range(BH):
                    c_ = slice(h * DV, (h + 1) * DV)
                    STT(yb[:, c_], bank[6][:, c_], small[:, 12 + h:13 + h], gla_g[:, c_], ALU.mult, ALU.mult)
                dve.drain()
                TT(yb, yb, og, ALU.mult).then_inc(S["yb_ready"], 1)
                dve.wait_ge(S["out_mm"], t + 1)
                for n in range(2):
                    TT(xn[:, n * 512:(n + 1) * 512], bank[4 + n][:], gate_rows[:, 0, n * 512:(n + 1) * 512], ALU.mult)
                dve.drain()
                TT(xt, xt, xn, ALU.add).then_inc(S["x2_ready"], 1)
                dve.wait_ge(S["x2ss"], t + 1)
                mean_sq(ss, ms, D, S["ms2"])
                dve.wait_ge(S["rstd2"], t + 1)
                TS(xn, xt, rstd, None, ALU.mult).then_inc(S["xn2_ready"], 1)
                dve.wait_ge(S["x2_tr"], t + 1)
                dve.wait_ge(S["h2_act"], t + 1)
                for k in range(4, 8):
                    ins = TS(hT[:, k, :], bank[1][:, (k - 4) * P:(k - 3) * P], scale2[:, k:k + 1], mod_col[:, 2, k:k + 1],
                             ALU.mult, ALU.add)
                ins.then_inc(S["h2_dve"], 1)
                dve.wait_ge(S["r_mm"], t + 1)
                TT(r_["lg"], bank[2][:, 0:E], rb, ALU.add)
                dve.drain()
                dve.tensor_reduce(small[:, 7:8], r_["lg"], AX, ALU.max)
                dve.drain()
                TS(small[:, 5:6], small[:, 7:8], -1.0, None, ALU.mult).then_inc(S["lg_ready"], 1)
                dve.wait_ge(S["e_ready"], t + 1)
                dve.reciprocal(small[:, 7:8], small[:, 6:7])
                dve.drain()
                TS(r_["p"], r_["e"], small[:, 7:8], None, ALU.mult)
                dve.drain()
                by_group = lambda v: v.rearrange("p (g i) -> p g i", g=GROUPS)
                wide = lambda v: v.unsqueeze(2).to_broadcast([P, GROUPS, PER])
                rev_b = rev.unsqueeze(1).to_broadcast([P, GROUPS, PER])

                def first_max(src, best, onehot):
                    dve.tensor_reduce(g_[best], by_group(r_[src]), AX, ALU.max)
                    dve.drain()
                    TT(by_group(r_["c"]), by_group(r_[src]), wide(g_[best]), ALU.is_equal)
                    dve.drain()
                    TT(by_group(r_["c"]), by_group(r_["c"]), rev_b, ALU.mult)
                    dve.drain()
                    dve.tensor_reduce(g_["r"], by_group(r_["c"]), AX, ALU.max)
                    dve.drain()
                    TT(by_group(r_[onehot]), rev_b, wide(g_["r"]), ALU.is_equal)
                    dve.drain()

                first_max("p", "m1", "oh1")
                STT(r_["p2"], r_["oh1"], -2.0, r_["p"], ALU.mult, ALU.add)
                dve.drain()
                first_max("p2", "m2", "oh2")
                TT(g_["gs"], g_["m1"], g_["m2"], ALU.add)
                dve.drain()
                dve.tensor_reduce(small[:, 7:8], g_["gs"], AX, ALU.max)
                dve.drain()
                STT(g_["t"], g_["gs"], small[:, 7:8], revg, ALU.is_equal, ALU.mult)
                dve.drain()
                dve.tensor_reduce(small[:, 7:8], g_["t"], AX, ALU.max)
                dve.drain()
                TS(g_["sel"], revg, small[:, 7:8], None, ALU.is_equal)
                dve.drain()
                TT(by_group(r_["sel1"]), by_group(r_["oh1"]), wide(g_["sel"]), ALU.mult)
                TT(by_group(r_["sel2"]), by_group(r_["oh2"]), wide(g_["sel"]), ALU.mult)
                dve.drain()
                TT(r_["m"], r_["sel1"], r_["sel2"], ALU.add)
                dve.tensor_tensor_reduce(out=g_["t"], in0=g_["m1"], in1=g_["sel"], scale=1.0, scalar=0.0, op0=ALU.mult,
                                         op1=ALU.add, accum_out=small[:, 6:7])
                dve.drain().then_inc(S["m_ready"], 1)
                dve.tensor_tensor_reduce(out=g_["r"], in0=g_["m2"], in1=g_["sel"], scale=1.0, scalar=0.0, op0=ALU.mult,
                                         op1=ALU.add, accum_out=small[:, 7:8])
                dve.drain()
                TT(small[:, 5:6], small[:, 6:7], small[:, 7:8], ALU.add)
                dve.drain()
                dve.reciprocal(small[:, 3:4], small[:, 5:6])
                dve.drain()
                TS(top_w[:, bass.ds(t, 1), :].rearrange("p a b -> p (a b)"), small[:, 6:8], small[:, 3:4], None, ALU.mult)
                dve.wait_ge(S["pos_mm"], t + 1)
                STT(r_["a"], bank[3][:, 0:E], float(E), eidx, ALU.mult, ALU.add)
                TT(r_["run"], r_["run"], r_["m"], ALU.add)
                dve.drain()
                for k in range(2):
                    dve.tensor_tensor_reduce(out=r_["t"], in0=r_["a"], in1=r_[f"sel{k + 1}"], scale=1.0, scalar=0.0,
                                             op0=ALU.mult, op1=ALU.add, accum_out=fin[:, 2 + k:3 + k])
                    dve.drain()
                dve.wait_ge(S["aid_ready"], t + 1)
                dve.tensor_copy(idx_now[:], fin[:, 2:4]).then_inc(S["idx_ready"], 1)
                for k in range(2):
                    dve.wait_ge(S[f"list_sc{k}"], 16 * t + 16)
                dve.wait_ge(S["x2_st"], 32 * t + 32)
                dve.sem_inc(S["tile_done"], 1)

            dve.wait_ge(S["cnt_mm"], 1)
            dve.tensor_copy(count_f[:], bank[4][:, 0:E])
            dve.drain()
            dve.tensor_reduce(small[:, 7:8], count_f[:], AX, ALU.max)
            dve.drain()
            dve.tensor_copy(count_i[:], small[:, 7:8]).then_inc(S["cnt_ready"], 1)
            dve.wait_ge(S["slots_ld"], 16)
            TS(slots_tok.rearrange("p a b -> p (a b)"), slots.rearrange("p a b -> p (a b)"), 1, None,
               ALU.logical_shift_right).then_inc(S["slots_ready"], 1)

            def x_evac(h, e):
                dve.wait_ge(S["xt_tr"], e + 1)
                for k in range(4, 8):
                    ins = TS(xT[h][:, k, :], bank[1][:, (k - 4) * P:(k - 3) * P], scale2[:, k:k + 1],
                             mod_col[:, 2, k:k + 1], ALU.mult, ALU.add)
                ins.then_inc(S["xT_dve"], 1)

            def gate(e):
                dve.wait_ge(S["h3_mm"], e + 1)
                dve.wait_ge(S["sil_ready"], e + 1)
                dve.wait_ge(S["h_tr"], e)
                TT(hid, bank[3][:], sil, ALU.mult).then_inc(S["h_ready"], 1)

            def y_evac(h, e, sc):
                dve.wait_ge(S["y_mm"], e + 1)
                dve.wait_ge(scat[h], sc)
                for j in range(2):
                    ins = TT(y_sb[h][:, j * 512:(j + 1) * 512], bank[5 + j][:], gate_rows[:, 1, j * 512:(j + 1) * 512],
                             ALU.mult)
                ins.then_inc(S["y_ready"], 1)

            x_evac(0, 0)
            gate(0)
            x_evac(1, 1)
            with dve.Fori(0, E // 2 - 1) as i:
                for h, e in ((1, 2 * i + 1), (0, 2 * i + 2)):
                    gate(e)
                    x_evac(1 - h, e + 1)
                    y_evac(1 - h, e - 1, 16 * i)
            gate(E - 1)
            y_evac(0, E - 2, 16 * (E // 2 - 1))
            y_evac(1, E - 1, 16 * (E // 2 - 1))
            most = dve.value_load(count_i[0:1, 0:1], min_val=0, max_val=T)
            with dve.If(most > cap):
                dve.wait_ge(S["ov_iota"], 1)
                TS(ob, count_f[:], float(cap), None, ALU.is_gt)
                dve.drain()
                for j in range(2, LISTS):
                    STT(ob, count_f[:], float(cap * j), ob, ALU.is_gt, ALU.add)
                    dve.drain()
                src, dst = ob, cum
                s = 1
                while s < E:
                    dve.tensor_copy(dst[:, 0:s], src[:, 0:s])
                    TT(dst[:, s:], src[:, s:], src[:, 0:E - s], ALU.add)
                    dve.drain()
                    src, dst = dst, (cum2 if dst is cum else cum)
                    s *= 2
                TT(le3, src.unsqueeze(1).to_broadcast([P, OVER, E]), bidx, ALU.is_le)
                dve.drain()
                TT(ob3, ob.unsqueeze(1).to_broadcast([P, OVER, E]), le3, ALU.mult)
                dve.tensor_reduce(eb, le3, AX, ALU.add)
                dve.drain()
                dve.tensor_reduce(jb, ob3, AX, ALU.add)
                TS(bsmall, eb, float(E), float(LISTS), ALU.is_ge, ALU.mult)
                TS(eb, eb, float(E - 1), None, ALU.min)
                dve.drain()
                TT(jb, nb, jb, ALU.subtract)
                dve.drain()
                TS(jb, jb, 1.0, float(LISTS), ALU.add, ALU.min)
                dve.drain()
                TT(jb, jb, bsmall, ALU.max)
                dve.drain()
                STT(jb, jb, float(E), eb, ALU.mult, ALU.add)
                dve.tensor_copy(table[:, 0, :], eb)
                dve.drain()
                dve.tensor_copy(table[:, 1, :], jb).then_inc(S["ov_table"], 1)
                for h in range(2):
                    dve.wait_ge(scat[h], 16 * E // 2)
                with dve.Fori(0, OVER) as b:
                    dve.wait_ge(S["ov_sil"], b + 1)
                    TT(hid, bank[3][:], sil, ALU.mult).then_inc(S["ov_hid"], 1)
                    dve.wait_ge(S["ov_y"], b + 1)
                    dve.wait_ge(S["ov_sc"], 16 * b)
                    for j in range(2):
                        ins = TT(y_sb[0][:, j * 512:(j + 1) * 512], bank[5 + j][:],
                                 gate_rows[:, 1, j * 512:(j + 1) * 512], ALU.mult)
                    ins.then_inc(S["ov_ysb"], 1)
            dve.wait_ge(S["gf_ld"], 16)
            with dve.Fori(0, TILES // 2) as i:
                for h in range(2):
                    t = 2 * i + h
                    dve.wait_ge(fin_ld[h], 32 * i + 32)
                    dve.wait_ge(fin_st[h], 16 * i)
                    STT(acc[h], yy[h][:, 0, :], top_w[:, bass.ds(t, 1), 0:1].rearrange("p a b -> p (a b)"), x2b[h],
                        ALU.mult, ALU.add)
                    dve.drain()
                    STT(acc[h], yy[h][:, 1, :], top_w[:, bass.ds(t, 1), 1:2].rearrange("p a b -> p (a b)"), acc[h],
                        ALU.mult, ALU.add).then_inc(S["fin_acc"], 1)
                    dve.wait_ge(S["fin_ss"], t + 1)
                    mean_sq(fin[:, 0:1], fin[:, 1:2], D, S["fin_ms"])
                    dve.wait_ge(S["fin_rs"], t + 1)
                    STT(acc[h], acc[h], fin[:, 2:3], gfin, ALU.mult, ALU.mult).then_inc(S["fin_out"], 1)


_INS = ['x', 'c', 'w_ada', 'b_ada', 'g_norm1', 'g_norm2', 'w_in', 'w_out', 'gmlp_ln_g', 'gmlp_ln_b', 'gmlp_ws', 'gmlp_bs',
        'gla_w_gate', 'gla_b_gate', 'gla_norm_g', 'conv_w', 'conv_b', 'router_w', 'router_b', 'exp_w1', 'exp_w3', 'exp_w2',
        'g_final']
_OUTS = [((1, 1024, 1024), 'float32')]


def kernel(**inputs):
    import numpy as _np
    import concourse.bacc as _bacc
    from concourse import mybir as _mybir
    from concourse.bass_utils import run_bass_kernel_spmd as _run

    nc = _bacc.Bacc("TRN2", target_bir_lowering=False, num_devices=1)
    arrays, args = {}, []
    for name in _INS:
        a = _np.ascontiguousarray(inputs[name])
        arrays[f"in_{name}_dram"] = a
        args.append(nc.dram_tensor(f"in_{name}_dram", a.shape, _mybir.dt.from_np(a.dtype), kind="ExternalInput").ap())
    for i, (shape, dtype) in enumerate(_OUTS):
        dt = _mybir.dt.from_np(_np.dtype(dtype))
        args.append(nc.dram_tensor(f"out_{i}_dram", shape, dt, kind="ExternalOutput").ap())
    build(nc, *args)
    r = _run(nc, [arrays], core_ids=[0])
    got = tuple(r.results[0][f"out_{i}_dram"] for i in range(len(_OUTS)))
    return got[0]
```

```python
from contextlib import ExitStack

import concourse.bass as bass
from concourse import mybir

ALU = mybir.AluOpType
ACT = mybir.ActivationFunctionType
AX = mybir.AxisListType.X
F32 = mybir.dt.float32
I32 = mybir.dt.int32

P = 128
EPS = 1e-6
TAU = 16.0
CHUNK = 64


def build(nc, x, c, w_ada, b_ada, g_norm1, g_norm2, w_in, w_out, gmlp_ln_g, gmlp_ln_b, gmlp_ws, gmlp_bs,
          gla_w_gate, gla_b_gate, gla_norm_g, conv_w, conv_b, router_w, router_b, exp_w1, exp_w3, exp_w2,
          g_final, out, cap=P):
    T, D = x.shape[1], x.shape[2]
    TILES = T // P
    KD = D // P
    PIN = w_in.shape[2]
    RANK, KDIM = gla_w_gate.shape[1], gla_w_gate.shape[2]
    VDIM = gla_norm_g.shape[1]
    ADIM = gmlp_ln_g.shape[1]
    CDIM = conv_b.shape[1]
    AH = gmlp_ws.shape[1]
    HD = ADIM // AH
    BH = 4
    DK, DV = KDIM // BH, VDIM // BH
    PAIRS = BH // 2
    E = exp_w1.shape[1]
    FF = exp_w1.shape[3]
    KF = FF // P
    GROUPS = 4
    PER = E // GROUPS
    OVER = 2 * T // cap - 1
    LISTS = T // cap
    NONE = 4 * T
    at, col = 0, {}
    for name, n in (("uv", 2 * ADIM), ("q", KDIM), ("k", KDIM), ("v", VDIM), ("g", RANK), ("og", VDIM),
                    ("cb", CDIM), ("cc", CDIM), ("cx", CDIM)):
        col[name] = at
        at += n

    x2_dram = nc.dram_tensor("x2_dram", (T, D), F32, kind="Internal").ap()
    xn2_dram = nc.dram_tensor("xn2_dram", (T, D), F32, kind="Internal").ap()
    y_dram = nc.dram_tensor("y_dram", (2 * T, D), F32, kind="Internal").ap()
    list_dram = nc.dram_tensor("list_dram", ((LISTS + 1) * cap * E, 1), I32, kind="Internal").ap()

    with ExitStack() as ctx:
        def sb(name, shape, dt=F32):
            return ctx.enter_context(nc.sbuf_tensor(name, shape, dt))[:]

        def sem(name):
            return ctx.enter_context(nc.semaphore(name))

        def wait(eng, s, n):
            if not isinstance(n, int) or n > 0:
                eng.wait_ge(s, n)

        ident = sb("ident", [P, P])
        ones = sb("ones", [P, P])
        gate_rows = sb("gate_rows", [P, 2, D])
        mod_col = sb("mod_col", [P, 4, KD])
        scale1, scale2 = sb("scale1", [P, KD]), sb("scale2", [P, KD])
        top_w = sb("top_w", [P, TILES, 2])
        count_f = sb("count_f", [P, E])
        count_i = sb("count_i", [P, 1], I32)
        slots = sb("slots", [P, LISTS + 1, E], I32)
        slots_tok = sb("slots_tok", [P, LISTS + 1, E], I32)
        gather_idx = sb("gather_idx", [P, 4], I32)
        scatter_idx = sb("scatter_idx", [P, 2], I32)
        aid = sb("aid", [P, TILES, 2], I32)
        aid_now = sb("aid_now", [P, 2], I32)
        idx_now = sb("idx_now", [P, 2], I32)
        idx_f = sb("idx_f", [P, 2])
        table = sb("table", [P, 2, OVER], I32)
        half = sb("half", [P, 1])
        stats = sb("stats", [P, 64])
        n_stats = [0]

        def stat(n=1):
            n_stats[0] += n
            return stats[:, n_stats[0] - n:n_stats[0]]

        ss1, ms1, rs1, ss2, ms2, rs2, bn_v, bn_r = (stat() for _ in range(8))
        ssf, msf, rsf = (stat(TILES) for _ in range(3))
        row_max, neg_max, exp_sum, exp_rec, best_g, pick_g, w_sum, w_rec = (stat() for _ in range(8))
        top2, oss, oms, ors = stat(2), stat(BH), stat(BH), stat(BH)

        ARENA = 49502

        arena = sb("arena", [P, ARENA])

        class Region:
            def __init__(self, start):
                self.at = start

            def take(self, *dims):
                n = 1
                for d in dims:
                    n *= d
                v = arena[:, self.at:self.at + n]
                self.at += n
                assert self.at <= ARENA, self.at
                if len(dims) == 2:
                    return v.rearrange("p (a b) -> p a b", a=dims[0])
                if len(dims) == 3:
                    return v.rearrange("p (a b c) -> p a b c", a=dims[0], b=dims[1])
                return v

        R = Region(0)
        groups = (("g", RANK, "g"), ("cb", CDIM, "cb"), ("q", 2 * KDIM, "qk"), ("cc", 2 * CDIM, "ccx"), ("v", VDIM, "v"),
                  ("uv", 2 * ADIM, "uv"), ("og", VDIM, "og"))
        win, win_at = {}, {}
        for first, n, name in groups:
            win_at[name] = R.at
            win[name] = R.take(KD, n)
        wout_at = R.at
        wout = R.take(KD, D)
        tri, tri_ref, tri_last, strict = (R.take(P) for _ in range(4))
        chunk_ind = R.take(2)
        wsT = R.take(AH, P)
        bs_col = R.take(AH)
        ln_g, ln_b = R.take(ADIM), R.take(ADIM)
        gla_g = R.take(VDIM)
        wgate = R.take(KDIM)
        bgate = R.take(KDIM)
        rw = R.take(KD, E)
        rb = R.take(E)
        convw, convb = R.take(3, 2), R.take(2)
        g1c, g2c, c_col = R.take(KD), R.take(KD), R.take(KD)
        rev, revg, eidx = R.take(PER), R.take(GROUPS), R.take(E)
        csil = R.take(KD)
        state = [R.take(PAIRS, 2 * DV) for _ in range(2)]
        loop_at = R.at
        x_in, x_nrm = R.take(D), R.take(D)
        x_res, x_nrm2 = R.take(D), R.take(D)
        hT, h2T = R.take(KD, P), R.take(KD, P)
        qk_sb = R.take(2 * KDIM)
        qkT, qeT = R.take(4, P), R.take(2, P)
        E1, E2, E3, E4 = (R.take(KDIM) for _ in range(4))
        q1, k2, k3, qe = E1, E2, E3, E4
        dec = R.take(4)
        v_sb = R.take(VDIM)
        uv = R.take(2 * ADIM)
        og = R.take(VDIM)
        lg1, lg2 = R.take(KDIM), R.take(KDIM)
        ccx_sb, cb_sb, z_sb = R.take(2 * CDIM), R.take(CDIM), R.take(CDIM)
        zT = R.take(2, P + 2)
        cbT = R.take(2, P)
        conv_acc = R.take(2, P)
        ya = R.take(ADIM)
        yT = R.take(KD, P)
        yb, vn = x_nrm2[:, 0:VDIM], x_nrm2[:, VDIM:VDIM + ADIM]
        g_sb, gT = R.take(RANK), R.take(P)
        sT = R.take(2, PAIRS, P)
        bn6, mv = R.take(6), R.take(2)
        r_ = {n: R.take(E) for n in ("lg", "e", "p", "c", "oh1", "oh2", "p2", "sel1", "sel2", "m", "run", "a", "t")}
        g_ = {n: R.take(GROUPS) for n in ("m1", "m2", "r", "gs", "sel", "t")}
        NB = 3
        wada = [Region(o).take(KD, 512) for o in (wout_at, wout_at + KD * 512, win_at["og"])]
        Z = Region(loop_at)
        bada = [Z.take(512) for _ in range(NB)]
        mod_acc = [[Z.take(512) for _ in range(2)] for _ in range(2)]
        modb = Z.take(6, D)
        W1 = [Region(win_at["qk"]).take(KD, FF), Region(win_at["uv"]).take(KD, FF)]
        W3 = [Region(win_at["ccx"]).take(KD, FF), Region(win_at["og"]).take(KD, FF)]
        W2 = [Region(win_at["v"]).take(KF, D), Region(wout_at).take(KF, D)]
        M_at = wout_at + KF * D
        M = Region(M_at)
        xg = [M.take(D) for _ in range(4)]
        xT = [M.take(KD, P) for _ in range(2)]
        hT2 = [M.take(KF, P) for _ in range(2)]
        sil, hid = M.take(FF), M.take(FF)
        y_sb = [M.take(D) for _ in range(2)]
        ob, cum, cum2 = M.take(E), M.take(E), M.take(E)
        le3, bidx, ob3 = M.take(OVER, E), M.take(OVER, E), M.take(OVER, E)
        eb, jb, nb, is_none = M.take(OVER), M.take(OVER), M.take(OVER), M.take(OVER)
        gfin = M.take(D)
        x2_all = M.take(TILES, D)
        F = Region(0)
        yy = F.take(TILES, 2 * D)
        acc = F.take(TILES, D)
        sq_junk = F.take(D)
        y_parts = ((0, 1), (1, 2), (2, 4), (4, TILES))
        assert F.at <= M_at

        bank = [ctx.enter_context(nc.psum_tensor(f"bank{i}", [P, 512], F32)) for i in range(8)]

        S = {}
        for n in ("params_ld", "consts", "wout_ld", "csil_ready", "lists_st", "setup_mm", "loop_ready",
                  "acc_ready", "mod_mm", "mod_evac",
                  "x_ld", "xr_ld", "xss", "ms1", "rs1", "xn_ready", "x_tr", "hT_act", "hT_dve",
                  "g_mm", "qk_mm", "ccx_mm", "cb_mm", "v_mm", "uv_mm", "og_mm",
                  "g_copied", "g_tr", "gT_ready", "z_mm", "absz", "lnz", "L_ready", "qk_ready", "ccx_ready", "cb_ready",
                  "D_mm", "exps", "prods", "qk_tr", "qkT_ready", "v_ready", "kv_mm", "state1", "state0", "sc_mm", "sT_ready",
                  "o_mm", "oss", "oms", "ors", "yb_ready", "uv_ready", "og_ready", "z_ready", "z_tr", "zT_ready",
                  "conv_done", "bn", "bnr", "vn0", "vn1", "vn_ready", "sv_mm", "ya_ready", "y_tr", "yT_ready", "out_mm",
                  "x2_ready", "x2ss", "ms2", "rs2", "xn2_ready", "x2_st", "x2_tr", "h2_act", "h2_dve", "r_mm",
                  "lg_read", "lg_ready", "e_ready", "m_ready", "pos_mm", "pos_read", "idx_ready", "aid_ready",
                  "list_sc0", "list_sc1", "run_ready", "cnt_mm", "cnt_ready", "slots_ld", "slots_ready",
                  "gidx", "sidx", "xt_tr", "xT_act", "xT_dve", "h1_mm", "h3_mm", "sil_ready", "h_ready",
                  "h_tr", "hT_ready", "y_mm", "y_ready",
                  "ov_iota", "ov_table", "ov_w", "ov_gather", "ov_tr", "ov_xT", "ov_h", "ov_sil", "ov_hid",
                  "ov_htr", "ov_hT", "ov_y", "ov_ysb", "ov_sc", "gp_passed", "dve_passed",
                  "early_ld", "fin_acc", "fin_ss", "fin_ms", "fin_rs", "fin_out"):
            S[n] = sem(n)
        win_ld = {name: sem(f"win_ld_{name}") for _, _, name in groups}
        wada_ld = [sem(f"wada_ld{h}") for h in range(NB)]
        w1_ld = [sem(f"w1_ld{h}") for h in range(2)]
        w3_ld = [sem(f"w3_ld{h}") for h in range(2)]
        w2_ld = [sem(f"w2_ld{h}") for h in range(2)]
        gath = [sem(f"gath{h}") for h in range(4)]
        scat = [sem(f"scat{h}") for h in range(2)]
        y_ld = [sem(f"y_ld{h}") for h in range(len(y_parts))]
        out_st = sem("out_st")

        x_t = x[0].rearrange("(t p) d -> t p d", p=P)
        wada_v = w_ada[0].rearrange("(p k) n -> p k n", k=KD)
        win_v = w_in[0].rearrange("(p k) n -> p k n", k=KD)
        wout_v = w_out[0].rearrange("(k p) n -> p k n", k=KD)
        x2_t = x2_dram.rearrange("(t p) d -> t p d", p=P)
        xn2_t = xn2_dram.rearrange("(t p) d -> t p d", p=P)
        y_t = y_dram.rearrange("(t p two) d -> p t (two d)", p=P, two=2)
        out_t = out[0].rearrange("(t p) d -> t p d", p=P)
        list_v = list_dram.rearrange("(j s e) one -> s j (e one)", s=cap, e=E)
        w1_v = exp_w1[0].rearrange("e (p k) f -> e p (k f)", k=KD)
        w3_v = exp_w3[0].rearrange("e (p k) f -> e p (k f)", k=KD)
        w2_v = exp_w2[0].rearrange("e (p k) f -> e p (k f)", k=KF)
        flat = lambda v: v.rearrange("p k f -> p (k f)")

        def one(v, i):
            return v[i] if isinstance(i, int) else v[bass.ds(i, 1)].rearrange("a p n -> (a p) n")

        def column(v, i):
            return v[:, i:i + 1] if isinstance(i, int) else v[:, bass.ds(i, 1)]

        def tiles(eng, body):
            body(0)
            with eng.Fori(1, TILES - 2) as t:
                body(t)
            body(TILES - 2)
            body(TILES - 1)

        def before(t, last):
            return not isinstance(t, int) or t < last

        def after(t, first):
            return not isinstance(t, int) or t > first

        block = ctx.enter_context(nc.Block())
        PARAMS = 16

        @block.sync
        def _(sp):
            with nc.allow_non_contiguous_dma(reason="small parameter vectors"):
                for dst, src in (
                    (c_col, c.rearrange("a (p k) -> p (a k)", k=KD)),
                    (g1c, g_norm1.rearrange("a (p k) -> p (a k)", k=KD)),
                    (g2c, g_norm2.rearrange("a (p k) -> p (a k)", k=KD)),
                    (wsT, gmlp_ws[0].rearrange("h t s -> t h s")),
                    (bs_col, gmlp_bs[0].rearrange("h t -> t h")),
                    (ln_g, gmlp_ln_g.partition_broadcast(P).rearrange("p a n -> p (a n)")),
                    (ln_b, gmlp_ln_b.partition_broadcast(P).rearrange("p a n -> p (a n)")),
                    (gla_g, gla_norm_g.partition_broadcast(P).rearrange("p a n -> p (a n)")),
                    (wgate[0:RANK, :], gla_w_gate[0]),
                    (bgate[0:1, :], gla_b_gate),
                    (rw, router_w.rearrange("(p k) e -> p k e", k=KD)),
                    (rb, router_b.rearrange("(a e) -> a e", a=1).partition_broadcast(P).rearrange("p a n -> p (a n)")),
                    (convw[:, 0, :], conv_w[0, 0].rearrange("(t p) -> p t", p=P)),
                    (convw[:, 1, :], conv_w[0, 1].rearrange("(t p) -> p t", p=P)),
                    (convw[:, 2, :], conv_w[0, 2].rearrange("(t p) -> p t", p=P)),
                    (convb, conv_b[0].rearrange("(t p) -> p t", p=P)),
                ):
                    sp.dma_start(dst, src).then_inc(S["params_ld"], 16)

            def ada(i, h):
                n = NB * i + h
                wait(sp, S["mod_evac"], n - NB + 1)
                cols = slice(n * 512, n * 512 + 512) if isinstance(n, int) else bass.ds(n * 512, 512)
                sp.dma_start(wada[h], wada_v[:, :, cols]).then_inc(wada_ld[h], 16)
                sp.dma_start(bada[h], b_ada[:, cols].partition_broadcast(P).rearrange("p a n -> p (a n)")).then_inc(wada_ld[h], 16)

            for h in range(NB):
                ada(0, h)
            sp.wait_ge(S["consts"], 1)
            sp.dma_start(list_v, slots[0:cap]).then_inc(S["lists_st"], 16)
            with sp.Fori(1, 6 * D // 512 // NB) as i:
                for h in range(NB):
                    ada(i, h)
            for first, n, name in groups[:-1]:
                sp.dma_start(win[name], win_v[:, :, col[first]:col[first] + n]).then_inc(win_ld[name], 16)
            sp.wait_ge(S["mod_evac"], 6 * D // 512)
            first, n, name = groups[-1]
            sp.dma_start(win[name], win_v[:, :, col[first]:col[first] + n]).then_inc(win_ld[name], 16)
            sp.wait_ge(S["loop_ready"], 1)
            sp.dma_start(x_in, x_t[0]).then_inc(S["x_ld"], 16)
            sp.dma_start(wout, wout_v).then_inc(S["wout_ld"], 16)
            sp.wait_ge(S["xn_ready"], 1)
            sp.dma_start(x_in, x_t[1]).then_inc(S["x_ld"], 16)

            def tile(t):
                wait(sp, S["x2_st"], 32 * t)
                sp.dma_start(x_res, one(x_t, t)).then_inc(S["xr_ld"], 16)
                if before(t, TILES - 2):
                    sp.wait_ge(S["xn_ready"], t + 2)
                    sp.dma_start(x_in, one(x_t, t + 2)).then_inc(S["x_ld"], 16)
                sp.wait_ge(S["x2_ready"], t + 1)
                sp.dma_start(one(x2_t, t), x_res).then_inc(S["x2_st"], 16)
                sp.wait_ge(S["xn2_ready"], t + 1)
                sp.dma_start(one(xn2_t, t), x_nrm2).then_inc(S["x2_st"], 16)

            def expert_weights(e, h):
                wait(sp, S["h1_mm"], e - 1)
                sp.dma_start(flat(W1[h]), one(w1_v, e)).then_inc(w1_ld[h], 16)
                wait(sp, S["h3_mm"], e - 1)
                sp.dma_start(flat(W3[h]), one(w3_v, e)).then_inc(w3_ld[h], 16)
                wait(sp, S["y_mm"], e - 1)
                sp.dma_start(flat(W2[h]), one(w2_v, e)).then_inc(w2_ld[h], 16)

            tile(0)
            with sp.Fori(1, TILES - 2) as t:
                tile(t)
            tile(TILES - 2)
            sp.wait_ge(S["og_mm"], TILES)
            sp.dma_start(flat(W1[0]), w1_v[0]).then_inc(w1_ld[0], 16)
            sp.dma_start(flat(W3[0]), w3_v[0]).then_inc(w3_ld[0], 16)
            sp.dma_start(flat(W2[0]), w2_v[0]).then_inc(w2_ld[0], 16)
            tile(TILES - 1)
            sp.dma_start(flat(W1[1]), w1_v[1]).then_inc(w1_ld[1], 16)
            for k in range(2):
                sp.wait_ge(S[f"list_sc{k}"], 16 * TILES)
            sp.dma_start(slots[0:cap], list_v).then_inc(S["slots_ld"], 16)
            sp.dma_start(flat(W3[1]), w3_v[1]).then_inc(w3_ld[1], 16)
            sp.wait_ge(S["out_mm"], TILES)
            sp.dma_start(flat(W2[1]), w2_v[1]).then_inc(w2_ld[1], 16)
            with sp.Fori(1, E // 2) as i:
                for h in range(2):
                    expert_weights(2 * i + h, h)
            sp.wait_ge(S["x2_st"], 32 * TILES)
            sp.dma_start(gfin, g_final.rearrange("(a n) -> a n", a=1).partition_broadcast(P)
                         .rearrange("p a n -> p (a n)")).then_inc(S["early_ld"], 16)
            sp.dma_start(x2_all, x2_dram.rearrange("(t p) d -> p t d", p=P)).then_inc(S["early_ld"], 16)
            most = sp.value_load(count_i[0:1, 0:1], min_val=0, max_val=T)
            with sp.If(most > cap):
                sp.wait_ge(S["y_mm"], E)
                sp.wait_ge(S["ov_table"], 1)
                with sp.Fori(0, OVER) as b:
                    sp.wait_ge(S["ov_y"], b + 1)
                    e = sp.value_load(table[0:1, 0, bass.ds(b, 1)], min_val=0, max_val=E - 1)
                    sp.dma_start(flat(W1[0]), one(w1_v, e)).then_inc(S["ov_w"], 16)
                    sp.dma_start(flat(W3[0]), one(w3_v, e)).then_inc(S["ov_w"], 16)
                    sp.dma_start(flat(W2[0]), one(w2_v, e)).then_inc(S["ov_w"], 16)
                sp.wait_ge(S["ov_sc"], 16 * OVER)
            for h in range(2):
                sp.wait_ge(scat[h], 16 * E // 2)
            for h, (a, b) in enumerate(y_parts):
                sp.dma_start(yy[:, a:b, :], y_t[:, a:b, :]).then_inc(y_ld[h], 16)
            sp.wait_ge(out_st, 16 * TILES)

        @block.gpsimd
        def _(gp):
            gp.memset(slots.rearrange("p a b -> p (a b)"), NONE).then_inc(S["consts"], 1)
            gp.memset(half, -0.5)
            gp.memset(ident, 0.0)
            gp.memset(ones, 1.0)
            for m in (tri, tri_ref, tri_last):
                gp.memset(m, 1.0 / TAU)
            gp.memset(chunk_ind, 1.0 / TAU)
            gp.memset(strict, 1.0)
            gp.iota(rev, pattern=[[-1, PER]], base=PER, channel_multiplier=0, allow_small_or_imprecise_dtypes=True)
            gp.iota(revg, pattern=[[-1, GROUPS]], base=GROUPS, channel_multiplier=0, allow_small_or_imprecise_dtypes=True)
            gp.iota(eidx, pattern=[[1, E]], base=0, channel_multiplier=0, allow_small_or_imprecise_dtypes=True)
            gp.iota(aid, pattern=[[2 * P, TILES], [1, 2]], base=0, channel_multiplier=2)
            gp.drain()

            def keep(v, base, per_row, per_col, n, op=ALU.is_ge, fill=0.0):
                gp.affine_select(out=v, in_=v, pattern=[[per_col, n]], compare_op=op, fill=fill, base=base,
                                 channel_multiplier=per_row)
                gp.drain()

            C = CHUNK
            keep(ident, 0, 1, -1, P, ALU.not_equal, 1.0)
            keep(strict, -1, -1, 1, P)
            keep(tri, 0, -1, 1, P)
            keep(tri[:, C:P], -C, 1, 0, C)
            keep(tri_last, -1, 1, -1, P)
            keep(tri_last[:, 0:C], C - 1, -1, 0, C)
            keep(tri_ref[:, 0:C], C // 2, -1, 0, C)
            keep(tri_ref[:, C:P], C + C // 2, -1, 0, C)
            keep(tri_ref[:, C:P], -C, 1, 0, C)
            keep(chunk_ind[:, 0:1], C - 1, -1, 0, 1)
            keep(chunk_ind[:, 1:2], -C, 1, 0, 1)
            gp.tensor_tensor(tri_ref, tri, tri_ref, ALU.subtract).then_inc(S["consts"], 1)

            def rsqrt(dst, src, n, ready, value, done):
                gp.wait_ge(ready, value)
                gp.tensor_tensor(dst, src, half.to_broadcast([P, n]) if n > 1 else half, ALU.pow).then_inc(done, 1)

            def enlist(t):
                for k in range(2):
                    wait(gp, S[f"list_sc{k}"], 16 * t)
                gp.tensor_copy(aid_now, aid[:, t, :] if isinstance(t, int) else
                               aid[:, bass.ds(t, 1), :].rearrange("p a b -> p (a b)")).then_inc(S["aid_ready"], 1)
                gp.wait_ge(S["aid_ready"], t + 1)
                gp.wait_ge(S["idx_ready"], t + 1)
                gp.sem_inc(S["gp_passed"], 1)
                for k in range(2):
                    gp.indirect_dma_start(out=list_dram, out_offset=bass.IndirectOffsetOnAxis(ap=idx_now[:, k:k + 1], axis=0),
                                          in_=aid_now[:, k:k + 1], in_offset=None, bounds_check=LISTS * cap * E - 1,
                                          oob_is_err=False).then_inc(S[f"list_sc{k}"], 16)

            def tile(t):
                rsqrt(bn_r, bn_v, 1, S["bn"], t + 1, S["bnr"])
                gp.wait_ge(S["vn0"], t + 1)
                gp.tensor_tensor(vn, vn, ln_g, ALU.mult).then_inc(S["vn1"], 1)
                gp.wait_ge(S["vn1"], t + 1)
                gp.tensor_tensor(vn, vn, ln_b, ALU.add).then_inc(S["vn_ready"], 1)
                rsqrt(ors, oms, BH, S["oms"], t + 1, S["ors"])
                rsqrt(rs2, ms2, 1, S["ms2"], t + 1, S["rs2"])
                if before(t, TILES - 2):
                    rsqrt(rs1, ms1, 1, S["ms1"], t + 3, S["rs1"])
                if after(t, 0):
                    enlist(t - 1)

            for t in range(2):
                rsqrt(rs1, ms1, 1, S["ms1"], t + 1, S["rs1"])
            gp.wait_ge(S["lists_st"], 16)
            tiles(gp, tile)
            enlist(TILES - 1)

            gp.wait_ge(S["cnt_mm"], 1)
            for s in range(4):
                gp.memset(xg[s], 0.0)
            gp.drain()
            gp.wait_ge(S["slots_ready"], 1)
            gp.wait_ge(S["x2_st"], 32 * TILES)

            def gather(e, h):
                gp.tensor_copy(gather_idx[:, h:h + 1], column(slots_tok[:, 0, :], e)).then_inc(S["gidx"], 1)
                gp.wait_ge(S["gidx"], e + 1)
                gp.sem_inc(S["gp_passed"], 1)
                gp.indirect_dma_start(out=xg[h], out_offset=None, in_=xn2_dram,
                                      in_offset=bass.IndirectOffsetOnAxis(ap=gather_idx[:, h:h + 1], axis=0),
                                      bounds_check=T - 1, oob_is_err=False).then_inc(gath[h], 16)

            def scatter(e, h, before_):
                wait(gp, scat[h], before_)
                gp.tensor_copy(scatter_idx[:, h:h + 1], column(slots[:, 0, :], e)).then_inc(S["sidx"], 1)
                gp.wait_ge(S["sidx"], e + 1)
                gp.wait_ge(S["y_ready"], e + 1)
                gp.sem_inc(S["gp_passed"], 1)
                gp.indirect_dma_start(out=y_dram, out_offset=bass.IndirectOffsetOnAxis(ap=scatter_idx[:, h:h + 1], axis=0),
                                      in_=y_sb[h], in_offset=None, bounds_check=2 * T - 1,
                                      oob_is_err=False).then_inc(scat[h], 16)

            for e in range(4):
                gather(e, e)

            def step(e, j, half_e):
                if before(e, E - 3):
                    gp.wait_ge(S["xt_tr"], e)
                    gather(e + 3, (j + 3) % 4)
                if after(e, 1):
                    scatter(e - 2, j % 2, 16 * (half_e - 1))

            for e in range(1, 4):
                step(e, e, e // 2)
            with gp.Fori(1, E // 4 - 1) as i:
                for j in range(4):
                    step(4 * i + j, j, 2 * i + j // 2)
            for e in range(E - 4, E + 2):
                step(e, e % 4, e // 2)
            most = gp.value_load(count_i[0:1, 0:1], min_val=0, max_val=T)
            with gp.If(most > cap):
                gp.iota(bidx.rearrange("p a b -> p (a b)"), pattern=[[1, OVER], [0, E]], base=0, channel_multiplier=0,
                        allow_small_or_imprecise_dtypes=True)
                gp.iota(nb, pattern=[[1, OVER]], base=0, channel_multiplier=0,
                        allow_small_or_imprecise_dtypes=True).then_inc(S["ov_iota"], 1)
                gp.wait_ge(S["ov_table"], 1)
                for h in range(2):
                    gp.wait_ge(scat[h], 16 * E // 2)
                with gp.Fori(0, OVER) as b:
                    at_ = gp.value_load(table[0:1, 1, bass.ds(b, 1)], min_val=0, max_val=(LISTS + 1) * E - 1)
                    gp.tensor_copy(gather_idx[:, 0:1], slots_tok.rearrange("p a b -> p (a b)")[:, bass.ds(at_, 1)]).then_inc(S["gidx"], 1)
                    gp.tensor_copy(scatter_idx[:, 0:1], slots.rearrange("p a b -> p (a b)")[:, bass.ds(at_, 1)]).then_inc(S["sidx"], 1)
                    gp.wait_ge(S["gidx"], E + b + 1)
                    gp.wait_ge(S["sidx"], E + b + 1)
                    gp.sem_inc(S["gp_passed"], 1)
                    gp.indirect_dma_start(out=xg[0], out_offset=None, in_=xn2_dram,
                                          in_offset=bass.IndirectOffsetOnAxis(ap=gather_idx[:, 0:1], axis=0),
                                          bounds_check=T - 1, oob_is_err=False).then_inc(S["ov_gather"], 16)
                    gp.wait_ge(S["ov_ysb"], b + 1)
                    gp.sem_inc(S["gp_passed"], 1)
                    gp.indirect_dma_start(out=y_dram, out_offset=bass.IndirectOffsetOnAxis(ap=scatter_idx[:, 0:1], axis=0),
                                          in_=y_sb[0], in_offset=None, bounds_check=2 * T - 1,
                                          oob_is_err=False).then_inc(S["ov_sc"], 16)
                    gp.wait_ge(S["ov_gather"], 16 * b + 16)
                    gp.wait_ge(S["ov_sc"], 16 * b + 16)
            for t in range(TILES):
                rsqrt(rsf[:, t:t + 1], msf[:, t:t + 1], 1, S["fin_ms"], t + 1, S["fin_rs"])

        @block.tensor
        def _(pe):
            pe.wait_ge(S["consts"], 2)
            with pe.Fori(0, 6 * D // 1024) as i:
                for h in range(2):
                    n = 2 * i + h
                    pe.wait_ge(S["acc_ready"], n + 1)
                    for a in range(2):
                        mm = pe.matmul(bank[h][:], ones, mod_acc[h][a], start=(a == 0), stop=(a == 1))
                    mm.then_inc(S["mod_mm"], 1)
            pe.wait_ge(S["mod_evac"], 6 * D // 512)
            for n, piece in enumerate((0, 1, 3, 4)):
                row = modb[0:1, piece, :].rearrange("p (m k) -> p k m", k=KD)
                for k in range(KD):
                    mm = pe.matmul(bank[2][:, n * KD + k:n * KD + k + 1], row[:, k, :], ones[0:1, 0:1], start=True, stop=True)
            mm.then_inc(S["setup_mm"], 1)
            pe.wait_ge(S["params_ld"], 16 * PARAMS)
            for h in range(AH):
                mm = pe.transpose(bank[3][:, h * P:(h + 1) * P], wsT[:, h, :], ident)
            mm.then_inc(S["setup_mm"], 1)
            pe.wait_ge(S["loop_ready"], 1)

            def rows(out_, name, n, done):
                for k in range(KD):
                    mm = pe.matmul(out_, hT[:, k, :], win[name][:, k, :], start=(k == 0), stop=(k == KD - 1))
                mm.then_inc(done, 1)

            def transpose8(src, done):
                cols = src.rearrange("p (m k) -> p k m", k=KD)
                for k in range(KD):
                    mm = pe.transpose(bank[k // 4][:, (k % 4) * P:(k % 4 + 1) * P], cols[:, k, :], ident)
                mm.then_inc(done, 1)

            def gates(t):
                pe.wait_ge(S["L_ready"], t + 1)
                wait(pe, S["x2_ready"], t)
                pe.matmul(bank[2][:, 0:KDIM], tri, lg1, start=True, stop=True)
                pe.matmul(bank[2][:, KDIM:2 * KDIM], tri_ref, lg1, start=True, stop=True)
                pe.matmul(bank[3][:, 0:KDIM], tri_last, lg1, start=True, stop=True)
                for p in range(PAIRS):
                    mm = pe.matmul(bank[3][:, KDIM + 2 * p:KDIM + 2 * p + 2], lg1[:, p * P:(p + 1) * P], chunk_ind,
                                   start=True, stop=True)
                mm.then_inc(S["D_mm"], 1)

            def low_rank_turn(t):
                pe.wait_ge(S["g_copied"], t + 1)
                pe.transpose(bank[6][0:RANK, 0:P], g_sb, ident).then_inc(S["g_tr"], 1)

            def low_rank(t):
                pe.wait_ge(S["gT_ready"], t + 1)
                pe.matmul(bank[6][:, 0:KDIM], gT[0:RANK, :], wgate[0:RANK, :], start=True, stop=False)
                pe.matmul(bank[6][:, 0:KDIM], ones[0:1, :], bgate[0:1, :], start=False, stop=True).then_inc(S["z_mm"], 1)

            def router(t):
                pe.wait_ge(S["h2_act"], t + 1)
                pe.wait_ge(S["h2_dve"], t + 1)
                wait(pe, S["pos_read"], t)
                for k in range(KD):
                    mm = pe.matmul(bank[5][:, 0:E], h2T[:, k, :], rw[:, k, :], start=(k == 0), stop=(k == KD - 1))
                mm.then_inc(S["r_mm"], 1)

            def places(t):
                pe.wait_ge(S["m_ready"], t + 1)
                pe.matmul(bank[5][:, 0:E], strict, r_["m"], start=True, stop=False)
                pe.matmul(bank[5][:, 0:E], ones, r_["run"], start=False, stop=True).then_inc(S["pos_mm"], 1)

            pe.wait_ge(S["xn_ready"], 1)
            transpose8(x_nrm, S["x_tr"])
            pe.wait_ge(S["hT_act"], 1)
            pe.wait_ge(S["hT_dve"], 1)
            pe.wait_ge(win_ld["g"], 16)
            rows(bank[6][:, 0:RANK], "g", RANK, S["g_mm"])
            pe.wait_ge(win_ld["qk"], 16)
            rows(bank[7][:], "qk", 2 * KDIM, S["qk_mm"])
            low_rank_turn(0)
            pe.wait_ge(win_ld["ccx"], 16)
            rows(bank[4][:], "ccx", 2 * CDIM, S["ccx_mm"])
            pe.wait_ge(win_ld["cb"], 16)
            pe.wait_ge(S["qk_ready"], 1)
            rows(bank[7][:, 0:CDIM], "cb", CDIM, S["cb_mm"])
            low_rank(0)
            pe.wait_ge(win_ld["v"], 16)
            pe.wait_ge(S["cb_ready"], 1)
            rows(bank[7][:], "v", VDIM, S["v_mm"])
            pe.wait_ge(win_ld["uv"], 16)
            rows(bank[5][:], "uv", 2 * ADIM, S["uv_mm"])
            pe.wait_ge(win_ld["og"], 16)
            pe.wait_ge(S["v_ready"], 1)
            rows(bank[7][:], "og", VDIM, S["og_mm"])
            pe.wait_ge(S["wout_ld"], 16)

            def tile(t):
                nxt = before(t, TILES - 1)
                if nxt:
                    pe.wait_ge(S["xn_ready"], t + 2)
                    wait(pe, S["h2_act"], t)
                    wait(pe, S["h2_dve"], t)
                    transpose8(x_nrm, S["x_tr"])
                gates(t)
                pe.wait_ge(S["z_ready"], t + 1)
                pe.wait_ge(S["cb_ready"], t + 1)
                wait(pe, S["yb_ready"], t)
                for j in range(2):
                    pe.transpose(bank[4][:, j * P:(j + 1) * P], z_sb[:, j * P:(j + 1) * P], ident)
                for j in range(2):
                    mm = pe.transpose(bank[4][:, (2 + j) * P:(3 + j) * P], cb_sb[:, j * P:(j + 1) * P], ident)
                mm.then_inc(S["z_tr"], 1)
                if after(t, 0):
                    pe.wait_ge(S["uv_ready"], t + 1)
                    router(t - 1)
                if nxt:
                    pe.wait_ge(S["hT_act"], t + 2)
                    pe.wait_ge(S["hT_dve"], t + 2)
                    pe.wait_ge(S["absz"], t + 1)
                    rows(bank[6][:, 0:RANK], "g", RANK, S["g_mm"])
                    pe.wait_ge(S["og_ready"], t + 1)
                    rows(bank[7][:], "qk", 2 * KDIM, S["qk_mm"])
                pe.wait_ge(S["prods"], t + 1)
                for j in range(2):
                    pe.transpose(bank[0][:, j * P:(j + 1) * P], q1[:, j * P:(j + 1) * P], ident)
                    pe.transpose(bank[0][:, (2 + j) * P:(3 + j) * P], k2[:, j * P:(j + 1) * P], ident)
                    mm = pe.transpose(bank[1][:, j * P:(j + 1) * P], qe[:, j * P:(j + 1) * P], ident)
                mm.then_inc(S["qk_tr"], 1)
                for ch in range(2):
                    r = slice(ch * CHUNK, (ch + 1) * CHUNK)
                    for p in range(PAIRS):
                        mm = pe.matmul(bank[2 + ch][:, p * 2 * DV:(p + 1) * 2 * DV], k3[r, p * P:(p + 1) * P],
                                       v_sb[r, p * 2 * DV:(p + 1) * 2 * DV], start=True, stop=True)
                mm.then_inc(S["kv_mm"], 1)
                if nxt:
                    low_rank_turn(t + 1)
                    pe.wait_ge(S["zT_ready"], t + 1)
                    rows(bank[4][:], "ccx", 2 * CDIM, S["ccx_mm"])
                pe.wait_ge(S["qkT_ready"], t + 1)
                for hh in range(2):
                    r = slice(hh * DK, (hh + 1) * DK)
                    for p in range(PAIRS):
                        mm = pe.matmul(bank[hh][:, p * P:(p + 1) * P], qkT[r, 2 + p, :], qkT[r, p, :],
                                       start=True, stop=True)
                mm.then_inc(S["sc_mm"], 1)
                if nxt:
                    pe.wait_ge(S["qk_ready"], t + 2)
                    rows(bank[7][:, 0:CDIM], "cb", CDIM, S["cb_mm"])
                pe.wait_ge(S["vn_ready"], t + 1)
                wait(pe, S["lg_read"], t)
                for h in range(AH):
                    mm = pe.matmul(bank[5][:, h * HD:(h + 1) * HD], wsT[:, h, :], vn[:, h * HD:(h + 1) * HD],
                                   start=True, stop=True)
                mm.then_inc(S["sv_mm"], 1)
                pe.wait_ge(S["sT_ready"], t + 1)
                pe.wait_ge(S["state1"], t + 1)
                if nxt:
                    pe.wait_ge(S["ccx_ready"], t + 2)
                for p in range(PAIRS):
                    cols = slice(p * 2 * DV, (p + 1) * 2 * DV)
                    for ch in range(2):
                        r = slice(ch * CHUNK, (ch + 1) * CHUNK)
                        pe.matmul(bank[4][r, cols], qeT[:, p, r], state[ch][:, p, :], start=True, stop=False,
                                  skip_group_check=True)
                    for hh in range(2):
                        h = 2 * p + hh
                        mm = pe.matmul(bank[4][:, h * DV:(h + 1) * DV], sT[:, hh, p, :], v_sb[:, h * DV:(h + 1) * DV],
                                       start=False, stop=True, skip_group_check=True)
                mm.then_inc(S["o_mm"], 1)
                if nxt:
                    pe.wait_ge(S["cb_ready"], t + 2)
                    rows(bank[7][:], "v", VDIM, S["v_mm"])
                pe.wait_ge(S["ya_ready"], t + 1)
                for j in range(2):
                    pe.transpose(bank[0][:, j * P:(j + 1) * P], ya[:, j * P:(j + 1) * P], ident)
                pe.wait_ge(S["yb_ready"], t + 1)
                for j in range(4):
                    mm = pe.transpose(bank[j // 2][:, (2 * (j < 2) + j % 2) * P:(2 * (j < 2) + j % 2 + 1) * P],
                                      yb[:, j * P:(j + 1) * P], ident)
                mm.then_inc(S["y_tr"], 1)
                if nxt:
                    rows(bank[5][:], "uv", 2 * ADIM, S["uv_mm"])
                    low_rank(t + 1)
                pe.wait_ge(S["yT_ready"], t + 1)
                pe.wait_ge(S["conv_done"], t + 1)
                pe.wait_ge(S["state0"], t + 1)
                for n in range(2):
                    for k in range(KD):
                        mm = pe.matmul(bank[2 + n][:], yT[:, k, :], wout[:, k, n * 512:(n + 1) * 512],
                                       start=(k == 0), stop=(k == KD - 1))
                mm.then_inc(S["out_mm"], 1)
                if nxt:
                    pe.wait_ge(S["v_ready"], t + 2)
                    rows(bank[7][:], "og", VDIM, S["og_mm"])
                if after(t, 0):
                    if nxt:
                        pe.wait_ge(S["uv_ready"], t + 2)
                    places(t - 1)
                pe.wait_ge(S["xn2_ready"], t + 1)
                transpose8(x_nrm2, S["x2_tr"])

            tiles(pe, tile)
            router(TILES - 1)
            pe.wait_ge(S["lg_read"], TILES)
            places(TILES - 1)
            pe.wait_ge(S["run_ready"], TILES)
            pe.wait_ge(S["pos_read"], TILES)
            pe.matmul(bank[5][:, 0:E], ones, r_["run"], start=True, stop=True).then_inc(S["cnt_mm"], 1)

            def x_turn(buf, ready, n, done):
                pe.wait_ge(ready, n)
                cols = buf.rearrange("p (m k) -> p k m", k=KD)
                for k in range(KD):
                    mm = pe.transpose(bank[k // 4][:, (k % 4) * P:(k % 4 + 1) * P], cols[:, k, :], ident)
                mm.then_inc(done, 1)

            def up(h, n, e):
                pe.wait_ge(S["xT_act"], e + 1)
                pe.wait_ge(S["xT_dve"], e + 1)
                pe.wait_ge(w1_ld[h], 16 * n + 16)
                wait(pe, S["sil_ready"], e)
                for k in range(KD):
                    mm = pe.matmul(bank[2][:], xT[h][:, k, :], W1[h][:, k, :], start=(k == 0), stop=(k == KD - 1))
                mm.then_inc(S["h1_mm"], 1)
                pe.wait_ge(w3_ld[h], 16 * n + 16)
                wait(pe, S["h_ready"], e)
                for k in range(KD):
                    mm = pe.matmul(bank[3][:], xT[h][:, k, :], W3[h][:, k, :], start=(k == 0), stop=(k == KD - 1))
                mm.then_inc(S["h3_mm"], 1)

            def h_turn(h, e):
                pe.wait_ge(S["h_ready"], e + 1)
                wait(pe, S["hT_ready"], e)
                cols = hid.rearrange("p (m k) -> p k m", k=KF)
                for k in range(KF):
                    mm = pe.transpose(bank[4][:, k * P:(k + 1) * P], cols[:, k, :], ident)
                mm.then_inc(S["h_tr"], 1)

            def down(h, n, e):
                pe.wait_ge(S["hT_ready"], e + 1)
                pe.wait_ge(w2_ld[h], 16 * n + 16)
                wait(pe, S["y_ready"], e)
                for j in range(2):
                    for k in range(KF):
                        mm = pe.matmul(bank[5 + j][:], hT2[h][:, k, :], W2[h][:, k, j * 512:(j + 1) * 512],
                                       start=(k == 0), stop=(k == KF - 1))
                mm.then_inc(S["y_mm"], 1)

            def expert(e, j, half_e, quarter):
                h = j % 2
                up(h, half_e, e)
                if before(e, E - 1):
                    x_turn(xg[(j + 1) % 4], gath[(j + 1) % 4], 16 * quarter + 16, S["xt_tr"])
                if after(e, 0):
                    down(1 - h, half_e - 1 + h, e - 1)
                h_turn(h, e)

            x_turn(xg[0], gath[0], 16, S["xt_tr"])
            for e in range(3):
                expert(e, e, e // 2, (e + 1) // 4)
            with pe.Fori(0, E // 4 - 1) as i:
                for j in range(4):
                    expert(4 * i + 3 + j, (3 + j) % 4, 2 * i + (3 + j) // 2, i + 1 + j // 4)
            expert(E - 1, (E - 1) % 4, (E - 1) // 2, E // 4)
            down(1, E // 2 - 1, E - 1)
            most = pe.value_load(count_i[0:1, 0:1], min_val=0, max_val=T)
            with pe.If(most > cap):
                pe.sem_inc(S["ov_y"], 1)
                with pe.Fori(0, OVER) as b:
                    x_turn(xg[0], S["ov_gather"], 16 * b + 16, S["ov_tr"])
                    pe.wait_ge(S["ov_xT"], b + 1)
                    pe.wait_ge(S["ov_w"], 48 * b + 48)
                    for w, bk in ((W1[0], 2), (W3[0], 3)):
                        for k in range(KD):
                            mm = pe.matmul(bank[bk][:], xT[0][:, k, :], w[:, k, :], start=(k == 0), stop=(k == KD - 1))
                    mm.then_inc(S["ov_h"], 1)
                    pe.wait_ge(S["ov_hid"], b + 1)
                    cols = hid.rearrange("p (m k) -> p k m", k=KF)
                    for k in range(KF):
                        mm = pe.transpose(bank[4][:, k * P:(k + 1) * P], cols[:, k, :], ident)
                    mm.then_inc(S["ov_htr"], 1)
                    pe.wait_ge(S["ov_hT"], b + 1)
                    for j in range(2):
                        for k in range(KF):
                            mm = pe.matmul(bank[5 + j][:], hT2[0][:, k, :], W2[0][:, k, j * 512:(j + 1) * 512],
                                           start=(k == 0), stop=(k == KF - 1))
                    mm.then_inc(S["ov_y"], 1)

        @block.scalar
        def _(act):
            act.wait_ge(S["params_ld"], 16 * PARAMS)
            act.activation(csil, c_col, ACT.Silu).then_inc(S["csil_ready"], 1)
            act.wait_ge(S["loop_ready"], 1)

            def norm_in(t):
                act.wait_ge(S["x_ld"], 16 * t + 16)
                act.activation(yT.rearrange("p a b -> p (a b)"), x_in, ACT.Square, accum_out=ss1)
                act.drain().then_inc(S["xss"], 1)

            def hT_half(dst, scale, shift, n, ready, done):
                act.wait_ge(ready, n)
                for k in range(4):
                    ins = act.activation(dst[:, k, :], bank[0][:, k * P:(k + 1) * P], ACT.Identity,
                                         scale=scale[:, k:k + 1], bias=mod_col[:, shift, k:k + 1])
                ins.then_inc(done, 1)

            def copy(dst, src, ready, n, done):
                act.wait_ge(ready, n)
                act.copy(dst, src).then_inc(done, 1)

            def early_rows(t):
                copy(g_sb, bank[6][:, 0:RANK], S["g_mm"], t + 1, S["g_copied"])
                wait(act, S["prods"], t)
                copy(qk_sb, bank[7][:], S["qk_mm"], t + 1, S["qk_ready"])

            def log_part(t):
                act.wait_ge(S["absz"], t + 1)
                act.activation(lg2, lg2, ACT.Exp)
                act.drain()
                act.activation(lg2, lg2, ACT.Ln, bias=1.0).then_inc(S["lnz"], 1)

            def softmax_exp(t):
                act.wait_ge(S["lg_ready"], t + 1)
                act.activation(r_["e"], r_["lg"], ACT.Exp, bias=neg_max, accum_out=exp_sum)
                act.drain().then_inc(S["e_ready"], 1)

            norm_in(0)
            hT_half(hT, scale1, 0, 1, S["x_tr"], S["hT_act"])
            norm_in(1)
            early_rows(0)
            copy(gT[0:RANK, :], bank[6][0:RANK, 0:P], S["g_tr"], 1, S["gT_ready"])
            copy(ccx_sb, bank[4][:], S["ccx_mm"], 1, S["ccx_ready"])
            copy(cb_sb, bank[7][:, 0:CDIM], S["cb_mm"], 1, S["cb_ready"])
            log_part(0)
            copy(v_sb, bank[7][:], S["v_mm"], 1, S["v_ready"])
            act.wait_ge(S["uv_mm"], 1)
            act.activation(uv, bank[5][:], ACT.Gelu).then_inc(S["uv_ready"], 1)
            act.wait_ge(S["og_mm"], 1)
            act.activation(og, bank[7][:], ACT.Silu).then_inc(S["og_ready"], 1)

            def tile(t):
                nxt = before(t, TILES - 1)
                if nxt:
                    hT_half(hT, scale1, 0, t + 2, S["x_tr"], S["hT_act"])
                act.wait_ge(S["D_mm"], t + 1)
                act.activation(E1, bank[2][:, KDIM:2 * KDIM], ACT.Exp)
                act.activation(E4, bank[2][:, 0:KDIM], ACT.Exp)
                act.activation(E2, bank[2][:, KDIM:2 * KDIM], ACT.Exp, scale=-1.0)
                act.activation(E3, bank[3][:, 0:KDIM], ACT.Exp)
                act.activation(dec, bank[3][:, KDIM:KDIM + 4], ACT.Exp)
                act.drain().then_inc(S["exps"], 1)
                act.wait_ge(S["z_tr"], t + 1)
                wait(act, S["conv_done"], t)
                act.copy(zT[:, :, 2:], bank[4][:, 0:2 * P].rearrange("p (a b) -> p a b", a=2))
                act.copy(cbT, bank[4][:, 2 * P:4 * P].rearrange("p (a b) -> p a b", a=2))
                act.drain().then_inc(S["zT_ready"], 1)
                if nxt:
                    early_rows(t + 1)
                act.wait_ge(S["qk_tr"], t + 1)
                act.copy(qkT.rearrange("p a b -> p (a b)"), bank[0][:])
                act.copy(qeT.rearrange("p a b -> p (a b)"), bank[1][:, 0:2 * P])
                act.drain().then_inc(S["qkT_ready"], 1)
                if nxt:
                    copy(gT[0:RANK, :], bank[6][0:RANK, 0:P], S["g_tr"], t + 2, S["gT_ready"])
                    copy(ccx_sb, bank[4][:], S["ccx_mm"], t + 2, S["ccx_ready"])
                    copy(cb_sb, bank[7][:, 0:CDIM], S["cb_mm"], t + 2, S["cb_ready"])
                act.wait_ge(S["o_mm"], t + 1)
                for h in range(BH):
                    act.activation(lg2[:, 0:DV], bank[4][:, h * DV:(h + 1) * DV], ACT.Square, accum_out=oss[:, h:h + 1])
                    act.drain()
                act.sem_inc(S["oss"], 1)
                if nxt:
                    copy(v_sb, bank[7][:], S["v_mm"], t + 2, S["v_ready"])
                act.wait_ge(S["y_tr"], t + 1)
                act.copy(yT[:, 0:4, :].rearrange("p a b -> p (a b)"), bank[0][:])
                act.copy(yT[:, 4:6, :].rearrange("p a b -> p (a b)"), bank[1][:, 0:2 * P])
                act.drain().then_inc(S["yT_ready"], 1)
                if nxt:
                    log_part(t + 1)
                if after(t, 0):
                    softmax_exp(t - 1)
                if nxt:
                    act.wait_ge(S["uv_mm"], t + 2)
                    act.activation(uv, bank[5][:], ACT.Gelu).then_inc(S["uv_ready"], 1)
                act.wait_ge(S["x2_ready"], t + 1)
                act.activation(yT.rearrange("p a b -> p (a b)"), x_res, ACT.Square, accum_out=ss2)
                act.drain().then_inc(S["x2ss"], 1)
                if nxt:
                    act.wait_ge(S["og_mm"], t + 2)
                    act.activation(og, bank[7][:], ACT.Silu).then_inc(S["og_ready"], 1)
                if before(t, TILES - 2):
                    norm_in(t + 2)
                hT_half(h2T, scale2, 2, t + 1, S["x2_tr"], S["h2_act"])

            tiles(act, tile)
            softmax_exp(TILES - 1)

            def x_evac(h, e):
                act.wait_ge(S["xt_tr"], e + 1)
                for k in range(4):
                    ins = act.activation(xT[h][:, k, :], bank[0][:, k * P:(k + 1) * P], ACT.Identity,
                                         scale=scale2[:, k:k + 1], bias=mod_col[:, 2, k:k + 1])
                ins.then_inc(S["xT_act"], 1)

            def expert(e, h):
                act.wait_ge(S["h1_mm"], e + 1)
                wait(act, S["h_ready"], e)
                act.activation(sil, bank[2][:], ACT.Silu).then_inc(S["sil_ready"], 1)
                if before(e, E - 1):
                    x_evac(1 - h, e + 1)
                act.wait_ge(S["h_tr"], e + 1)
                wait(act, S["y_mm"], e - 1)
                act.copy(hT2[h].rearrange("p a b -> p (a b)"), bank[4][:]).then_inc(S["hT_ready"], 1)

            x_evac(0, 0)
            for e in range(2):
                expert(e, e)
            with act.Fori(1, E // 2 - 1) as i:
                for h in range(2):
                    expert(2 * i + h, h)
            for h in range(2):
                expert(E - 2 + h, h)
            most = act.value_load(count_i[0:1, 0:1], min_val=0, max_val=T)
            with act.If(most > cap):
                act.wait_ge(S["y_mm"], E)
                with act.Fori(0, OVER) as b:
                    act.wait_ge(S["ov_tr"], b + 1)
                    for k in range(KD):
                        ins = act.activation(xT[0][:, k, :], bank[k // 4][:, (k % 4) * P:(k % 4 + 1) * P], ACT.Identity,
                                             scale=scale2[:, k:k + 1], bias=mod_col[:, 2, k:k + 1])
                    ins.then_inc(S["ov_xT"], 1)
                    act.wait_ge(S["ov_h"], b + 1)
                    act.activation(sil, bank[2][:], ACT.Silu).then_inc(S["ov_sil"], 1)
                    act.wait_ge(S["ov_htr"], b + 1)
                    act.copy(hT2[0].rearrange("p a b -> p (a b)"), bank[4][:]).then_inc(S["ov_hT"], 1)
            def store(t):
                act.wait_ge(S["fin_out"], t + 1)
                act.dma_start(out_t[t], acc[:, t, :]).then_inc(out_st, 16)

            for t in range(TILES):
                act.wait_ge(S["fin_acc"], t + 1)
                act.activation(sq_junk, acc[:, t, :], ACT.Square, accum_out=ssf[:, t:t + 1])
                act.drain().then_inc(S["fin_ss"], 1)
                if t:
                    store(t - 1)
            store(TILES - 1)

        @block.vector
        def _(dve):
            TT, TS, STT = dve.tensor_tensor, dve.tensor_scalar, dve.scalar_tensor_tensor
            dve.wait_ge(S["csil_ready"], 1)

            def mod_sums(i, h, a):
                n = NB * i + h
                dve.wait_ge(wada_ld[h], 32 * i + 32)
                wait(dve, S["mod_mm"], n - 1)
                for k in range(KD):
                    s = mod_acc[a][k % 2]
                    if k < 2:
                        TS(s, wada[h][:, k, :], csil[:, k:k + 1], None, ALU.mult)
                    else:
                        ins = STT(s, wada[h][:, k, :], csil[:, k:k + 1], s, ALU.mult, ALU.add)
                    if k % 2 and k < KD - 1:
                        dve.drain()
                ins.then_inc(S["acc_ready"], 1)

            def mod_out(i, h, a):
                n = NB * i + h
                dve.wait_ge(S["mod_mm"], n + 1)
                cols = slice(n * 512, n * 512 + 512) if isinstance(n, int) else bass.ds(n * 512, 512)
                TT(modb.rearrange("p a b -> p (a b)")[:, cols], bank[a][:], bada[h], ALU.add).then_inc(S["mod_evac"], 1)

            steps = 2 * NB
            for j in range(steps):
                mod_sums(j // NB, j % NB, j % 2)
                if j:
                    mod_out((j - 1) // NB, (j - 1) % NB, (j - 1) % 2)
            for j in range(steps, 6 * D // 512):
                mod_sums(j // NB, j % NB, j % 2)
                mod_out((j - 1) // NB, (j - 1) % NB, (j - 1) % 2)
            j = 6 * D // 512 - 1
            mod_out(j // NB, j % NB, j % 2)
            dve.drain()
            for n, piece in enumerate((2, 5)):
                dve.tensor_copy(gate_rows[:, n, :], modb[:, piece, :])
            dve.wait_ge(S["setup_mm"], 1)
            dve.wait_ge(S["params_ld"], 16 * PARAMS)
            dve.tensor_copy(mod_col.rearrange("p a b -> p (a b)"), bank[2][:, 0:4 * KD])
            dve.drain()
            STT(scale1, mod_col[:, 1, :], 1.0, g1c, ALU.add, ALU.mult)
            STT(scale2, mod_col[:, 3, :], 1.0, g2c, ALU.add, ALU.mult)
            dve.wait_ge(S["setup_mm"], 2)
            dve.tensor_copy(wsT.rearrange("p a b -> p (a b)"), bank[3][:])
            dve.drain()
            dve.memset(wsT[CHUNK:P, :, 0:CHUNK], 0.0)
            for s in range(2):
                dve.memset(state[s].rearrange("p a b -> p (a b)"), 0.0)
            dve.memset(zT.rearrange("p a b -> p (a b)"), 0.0)
            dve.memset(sT.rearrange("p a b c -> p (a b c)"), 0.0)
            dve.memset(r_["run"], 0.0)
            dve.drain().then_inc(S["loop_ready"], 1)

            def mean_sq(src, dst, n, done):
                TS(dst, src, 1.0 / n, EPS, ALU.mult, ALU.add).then_inc(done, 1)

            def norm_in(t):
                dve.wait_ge(S["xss"], t + 1)
                mean_sq(ss1, ms1, D, S["ms1"])
                dve.wait_ge(S["rs1"], t + 1)
                wait(dve, S["x_tr"], t)
                TS(x_nrm, x_in, rs1, None, ALU.mult).then_inc(S["xn_ready"], 1)

            def hT_half(dst, scale, shift, n, ready, done):
                dve.wait_ge(ready, n)
                for k in range(4, 8):
                    ins = TS(dst[:, k, :], bank[1][:, (k - 4) * P:(k - 3) * P], scale[:, k:k + 1],
                             mod_col[:, shift, k:k + 1], ALU.mult, ALU.add)
                ins.then_inc(done, 1)

            def conv_product(t):
                dve.wait_ge(S["ccx_ready"], t + 1)
                TT(z_sb, ccx_sb[:, 0:CDIM], ccx_sb[:, CDIM:], ALU.mult).then_inc(S["z_ready"], 1)

            def gate_log(t):
                dve.wait_ge(S["z_mm"], t + 1)
                TS(lg1, bank[6][:, 0:KDIM], 0.0, None, ALU.min)
                dve.drain()
                STT(lg2, lg1, 2.0, bank[6][:, 0:KDIM], ALU.mult, ALU.subtract).then_inc(S["absz"], 1)
                dve.wait_ge(S["lnz"], t + 1)
                TT(lg1, lg1, lg2, ALU.subtract).then_inc(S["L_ready"], 1)

            by_group = lambda v: v.rearrange("p (g i) -> p g i", g=GROUPS)
            wide = lambda v: v.unsqueeze(2).to_broadcast([P, GROUPS, PER])
            rev_b = rev.unsqueeze(1).to_broadcast([P, GROUPS, PER])

            def first_max(src, best, onehot):
                dve.tensor_reduce(g_[best], by_group(r_[src]), AX, ALU.max)
                dve.drain()
                TT(by_group(r_["c"]), by_group(r_[src]), wide(g_[best]), ALU.is_equal)
                dve.drain()
                TT(by_group(r_["c"]), by_group(r_["c"]), rev_b, ALU.mult)
                dve.drain()
                dve.tensor_reduce(g_["r"], by_group(r_["c"]), AX, ALU.max)
                dve.drain()
                TT(by_group(r_[onehot]), rev_b, wide(g_["r"]), ALU.is_equal)
                dve.drain()

            def logits(t):
                dve.wait_ge(S["r_mm"], t + 1)
                TT(r_["lg"], bank[5][:, 0:E], rb, ALU.add)
                dve.drain().then_inc(S["lg_read"], 1)

            def choose(t):
                dve.tensor_reduce(row_max, r_["lg"], AX, ALU.max)
                dve.drain()
                TS(neg_max, row_max, -1.0, None, ALU.mult).then_inc(S["lg_ready"], 1)
                dve.wait_ge(S["e_ready"], t + 1)
                dve.reciprocal(exp_rec, exp_sum)
                dve.drain()
                TS(r_["p"], r_["e"], exp_rec, None, ALU.mult)
                dve.drain()
                first_max("p", "m1", "oh1")
                STT(r_["p2"], r_["oh1"], -2.0, r_["p"], ALU.mult, ALU.add)
                dve.drain()
                first_max("p2", "m2", "oh2")
                TT(g_["gs"], g_["m1"], g_["m2"], ALU.add)
                dve.drain()
                dve.tensor_reduce(best_g, g_["gs"], AX, ALU.max)
                dve.drain()
                STT(g_["t"], g_["gs"], best_g, revg, ALU.is_equal, ALU.mult)
                dve.drain()
                dve.tensor_reduce(pick_g, g_["t"], AX, ALU.max)
                dve.drain()
                TS(g_["sel"], revg, pick_g, None, ALU.is_equal)
                dve.drain()
                TT(by_group(r_["sel1"]), by_group(r_["oh1"]), wide(g_["sel"]), ALU.mult)
                TT(by_group(r_["sel2"]), by_group(r_["oh2"]), wide(g_["sel"]), ALU.mult)
                dve.drain()
                TT(r_["m"], r_["sel1"], r_["sel2"], ALU.add).then_inc(S["m_ready"], 1)
                dve.tensor_tensor_reduce(out=g_["t"], in0=g_["m1"], in1=g_["sel"], scale=1.0, scalar=0.0, op0=ALU.mult,
                                         op1=ALU.add, accum_out=top2[:, 0:1])
                dve.tensor_tensor_reduce(out=g_["r"], in0=g_["m2"], in1=g_["sel"], scale=1.0, scalar=0.0, op0=ALU.mult,
                                         op1=ALU.add, accum_out=top2[:, 1:2])
                dve.drain()
                TT(w_sum, top2[:, 0:1], top2[:, 1:2], ALU.add)
                dve.drain()
                dve.reciprocal(w_rec, w_sum)
                dve.drain()
                TS(top_w[:, t, :] if isinstance(t, int) else top_w[:, bass.ds(t, 1), :].rearrange("p a b -> p (a b)"),
                   top2, w_rec, None, ALU.mult)

            def place(t):
                dve.wait_ge(S["pos_mm"], t + 1)
                STT(r_["a"], bank[5][:, 0:E], float(E), eidx, ALU.mult, ALU.add)
                dve.drain().then_inc(S["pos_read"], 1)
                TT(r_["run"], r_["run"], r_["m"], ALU.add).then_inc(S["run_ready"], 1)
                for k in range(2):
                    dve.tensor_tensor_reduce(out=r_["t"], in0=r_["a"], in1=r_[f"sel{k + 1}"], scale=1.0, scalar=0.0,
                                             op0=ALU.mult, op1=ALU.add, accum_out=idx_f[:, k:k + 1])
                    dve.drain()
                for k in range(2):
                    wait(dve, S[f"list_sc{k}"], 16 * t)
                dve.tensor_copy(idx_now, idx_f).then_inc(S["idx_ready"], 1)

            norm_in(0)
            hT_half(hT, scale1, 0, 1, S["x_tr"], S["hT_dve"])
            norm_in(1)
            conv_product(0)
            gate_log(0)

            def tile(t):
                nxt = before(t, TILES - 1)
                dve.wait_ge(S["uv_ready"], t + 1)
                dve.bn_stats(bn6, uv[:, ADIM:])
                dve.drain()
                dve.bn_aggr(mv, bn6)
                dve.drain()
                TS(bn_v, mv[:, 1:2], EPS, None, ALU.add).then_inc(S["bn"], 1)
                if nxt:
                    hT_half(hT, scale1, 0, t + 2, S["x_tr"], S["hT_dve"])
                dve.wait_ge(S["bnr"], t + 1)
                wait(dve, S["x2_st"], 32 * t)
                wait(dve, S["x2_tr"], t)
                TS(vn, uv[:, ADIM:], mv[:, 0:1], bn_r, ALU.subtract, ALU.mult).then_inc(S["vn0"], 1)
                dve.wait_ge(S["exps"], t + 1)
                STT(q1, qk_sb[:, 0:KDIM], DK ** -0.5, E1, ALU.mult, ALU.mult)
                TT(k2, qk_sb[:, KDIM:], E2, ALU.mult)
                STT(qe, qk_sb[:, 0:KDIM], DK ** -0.5, E4, ALU.mult, ALU.mult)
                TT(k3, qk_sb[:, KDIM:], E3, ALU.mult)
                dve.drain().then_inc(S["prods"], 1)
                if after(t, 0):
                    logits(t - 1)
                dve.wait_ge(S["zT_ready"], t + 1)
                for j in range(2):
                    TS(conv_acc[:, j, :], zT[:, j, 0:P], convw[:, 0, j:j + 1], convb[:, j:j + 1], ALU.mult, ALU.add)
                dve.drain()
                for s in (1, 2):
                    for j in range(2):
                        STT(conv_acc[:, j, :], zT[:, j, s:s + P], convw[:, s, j:j + 1], conv_acc[:, j, :], ALU.mult, ALU.add)
                    dve.drain()
                wait(dve, S["out_mm"], t)
                TT(yT[:, 6:8, :], conv_acc, cbT, ALU.mult)
                dve.tensor_copy(zT[:, :, 0:2], zT[:, :, P:P + 2])
                dve.drain().then_inc(S["conv_done"], 1)

                def step(src, dst, ch):
                    for p in range(PAIRS):
                        for hh in range(2):
                            r = slice(hh * DK, (hh + 1) * DK)
                            cols = slice(hh * DV, (hh + 1) * DV)
                            STT(dst[r, p, cols], src[r, p, cols], dec[r, 2 * p + ch:2 * p + ch + 1],
                                bank[2 + ch][r, p * 2 * DV + hh * DV:p * 2 * DV + (hh + 1) * DV], ALU.mult, ALU.add)

                dve.wait_ge(S["kv_mm"], t + 1)
                step(state[0], state[1], 0)
                dve.drain().then_inc(S["state1"], 1)
                dve.wait_ge(S["sc_mm"], t + 1)
                dve.sem_inc(S["dve_passed"], 1)
                for hh in range(2):
                    dve.copy_predicated(sT[:, hh], tri.bitcast(I32).unsqueeze(1).to_broadcast([P, PAIRS, P]),
                                        bank[hh][:, 0:PAIRS * P].rearrange("p (a b) -> p a b", a=PAIRS))
                dve.drain().then_inc(S["sT_ready"], 1)
                if nxt:
                    conv_product(t + 1)
                dve.wait_ge(S["sv_mm"], t + 1)
                for h in range(AH):
                    c_ = slice(h * HD, (h + 1) * HD)
                    STT(ya[:, c_], bank[5][:, c_], bs_col[:, h:h + 1], uv[:, c_], ALU.add, ALU.mult)
                dve.drain().then_inc(S["ya_ready"], 1)
                dve.wait_ge(S["o_mm"], t + 1)
                step(state[1], state[0], 1)
                dve.drain().then_inc(S["state0"], 1)
                dve.wait_ge(S["oss"], t + 1)
                mean_sq(oss, oms, DV, S["oms"])
                dve.wait_ge(S["ors"], t + 1)
                for h in range(BH):
                    c_ = slice(h * DV, (h + 1) * DV)
                    STT(yb[:, c_], bank[4][:, c_], ors[:, h:h + 1], gla_g[:, c_], ALU.mult, ALU.mult)
                dve.drain()
                TT(yb, yb, og, ALU.mult).then_inc(S["yb_ready"], 1)
                if nxt:
                    gate_log(t + 1)
                if after(t, 0):
                    choose(t - 1)
                dve.wait_ge(S["xr_ld"], 16 * t + 16)
                dve.wait_ge(S["out_mm"], t + 1)
                for n in range(2):
                    TT(x_nrm2[:, n * 512:(n + 1) * 512], bank[2 + n][:], gate_rows[:, 0, n * 512:(n + 1) * 512], ALU.mult)
                dve.drain()
                TT(x_res, x_res, x_nrm2, ALU.add).then_inc(S["x2_ready"], 1)
                dve.wait_ge(S["x2ss"], t + 1)
                mean_sq(ss2, ms2, D, S["ms2"])
                dve.wait_ge(S["rs2"], t + 1)
                TS(x_nrm2, x_res, rs2, None, ALU.mult).then_inc(S["xn2_ready"], 1)
                if before(t, TILES - 2):
                    norm_in(t + 2)
                if after(t, 0):
                    place(t - 1)
                hT_half(h2T, scale2, 2, t + 1, S["x2_tr"], S["h2_dve"])

            tiles(dve, tile)
            logits(TILES - 1)
            choose(TILES - 1)
            place(TILES - 1)

            dve.wait_ge(S["cnt_mm"], 1)
            dve.tensor_copy(count_f, bank[5][:, 0:E])
            dve.drain()
            dve.tensor_reduce(row_max, count_f, AX, ALU.max)
            dve.drain()
            dve.tensor_copy(count_i, row_max).then_inc(S["cnt_ready"], 1)
            dve.wait_ge(S["slots_ld"], 16)
            TS(slots_tok.rearrange("p a b -> p (a b)"), slots.rearrange("p a b -> p (a b)"), 1, None,
               ALU.logical_shift_right).then_inc(S["slots_ready"], 1)

            def x_evac(h, e):
                dve.wait_ge(S["xt_tr"], e + 1)
                for k in range(4, 8):
                    ins = TS(xT[h][:, k, :], bank[1][:, (k - 4) * P:(k - 3) * P], scale2[:, k:k + 1],
                             mod_col[:, 2, k:k + 1], ALU.mult, ALU.add)
                ins.then_inc(S["xT_dve"], 1)

            def y_evac(h, e, stored):
                dve.wait_ge(S["y_mm"], e + 1)
                wait(dve, scat[h], stored)
                for j in range(2):
                    ins = TT(y_sb[h][:, j * 512:(j + 1) * 512], bank[5 + j][:], gate_rows[:, 1, j * 512:(j + 1) * 512],
                             ALU.mult)
                ins.then_inc(S["y_ready"], 1)

            def expert(e, h, half_e):
                dve.wait_ge(S["h3_mm"], e + 1)
                dve.wait_ge(S["sil_ready"], e + 1)
                wait(dve, S["h_tr"], e)
                TT(hid, bank[3][:], sil, ALU.mult).then_inc(S["h_ready"], 1)
                if before(e, E - 1):
                    x_evac(1 - h, e + 1)
                if after(e, 0):
                    y_evac(1 - h, e - 1, 16 * (half_e - 1 + h))

            x_evac(0, 0)
            for e in range(3):
                expert(e, e % 2, e // 2)
            with dve.Fori(1, E // 2 - 1) as i:
                for j in range(2):
                    expert(2 * i + 1 + j, 1 - j, i + j)
            expert(E - 1, 1, E // 2 - 1)
            y_evac(1, E - 1, 16 * (E // 2 - 1))
            dve.wait_ge(S["cnt_ready"], 1)
            most = dve.value_load(count_i[0:1, 0:1], min_val=0, max_val=T)
            with dve.If(most > cap):
                dve.wait_ge(S["ov_iota"], 1)
                TS(ob, count_f, float(cap), None, ALU.is_gt)
                dve.drain()
                for j in range(2, LISTS):
                    STT(ob, count_f, float(cap * j), ob, ALU.is_gt, ALU.add)
                    dve.drain()
                src, dst = ob, cum
                s = 1
                while s < E:
                    dve.tensor_copy(dst[:, 0:s], src[:, 0:s])
                    TT(dst[:, s:], src[:, s:], src[:, 0:E - s], ALU.add)
                    dve.drain()
                    src, dst = dst, (cum2 if dst is cum else cum)
                    s *= 2
                TT(le3, src.unsqueeze(1).to_broadcast([P, OVER, E]), bidx, ALU.is_le)
                dve.drain()
                TT(ob3, ob.unsqueeze(1).to_broadcast([P, OVER, E]), le3, ALU.mult)
                dve.tensor_reduce(eb, le3, AX, ALU.add)
                dve.drain()
                dve.tensor_reduce(jb, ob3, AX, ALU.add)
                TS(is_none, eb, float(E), float(LISTS), ALU.is_ge, ALU.mult)
                dve.drain()
                TS(eb, eb, float(E - 1), None, ALU.min)
                TT(jb, nb, jb, ALU.subtract)
                dve.drain()
                TS(jb, jb, 1.0, float(LISTS), ALU.add, ALU.min)
                dve.drain()
                TT(jb, jb, is_none, ALU.max)
                dve.drain()
                STT(jb, jb, float(E), eb, ALU.mult, ALU.add)
                dve.tensor_copy(table[:, 0, :], eb)
                dve.drain()
                dve.tensor_copy(table[:, 1, :], jb).then_inc(S["ov_table"], 1)
                for h in range(2):
                    dve.wait_ge(scat[h], 16 * E // 2)
                with dve.Fori(0, OVER) as b:
                    dve.wait_ge(S["ov_sil"], b + 1)
                    TT(hid, bank[3][:], sil, ALU.mult).then_inc(S["ov_hid"], 1)
                    dve.wait_ge(S["ov_y"], b + 2)
                    for j in range(2):
                        ins = TT(y_sb[0][:, j * 512:(j + 1) * 512], bank[5 + j][:],
                                 gate_rows[:, 1, j * 512:(j + 1) * 512], ALU.mult)
                    ins.then_inc(S["ov_ysb"], 1)
            dve.wait_ge(S["early_ld"], 32)

            def finish(t):
                dve.wait_ge(S["fin_ss"], t + 1)
                mean_sq(ssf[:, t:t + 1], msf[:, t:t + 1], D, S["fin_ms"])
                dve.wait_ge(S["fin_rs"], t + 1)
                STT(acc[:, t, :], acc[:, t, :], rsf[:, t:t + 1], gfin, ALU.mult, ALU.mult).then_inc(S["fin_out"], 1)

            for t in range(TILES):
                for h, (a, b) in enumerate(y_parts):
                    if a == t:
                        dve.wait_ge(y_ld[h], 16)
                STT(acc[:, t, :], yy[:, t, 0:D], top_w[:, t, 0:1], x2_all[:, t, :], ALU.mult, ALU.add)
                dve.drain()
                STT(acc[:, t, :], yy[:, t, D:], top_w[:, t, 1:2], acc[:, t, :], ALU.mult, ALU.add).then_inc(S["fin_acc"], 1)
                if t:
                    finish(t - 1)
            finish(TILES - 1)


_INS = ['x', 'c', 'w_ada', 'b_ada', 'g_norm1', 'g_norm2', 'w_in', 'w_out', 'gmlp_ln_g', 'gmlp_ln_b', 'gmlp_ws', 'gmlp_bs',
        'gla_w_gate', 'gla_b_gate', 'gla_norm_g', 'conv_w', 'conv_b', 'router_w', 'router_b', 'exp_w1', 'exp_w3', 'exp_w2',
        'g_final']
_OUTS = [((1, 1024, 1024), 'float32')]


def kernel(**inputs):
    import numpy as _np
    import concourse.bacc as _bacc
    from concourse import mybir as _mybir
    from concourse.bass_utils import run_bass_kernel_spmd as _run

    nc = _bacc.Bacc("TRN2", target_bir_lowering=False, num_devices=1)
    arrays, args = {}, []
    for name in _INS:
        a = _np.ascontiguousarray(inputs[name])
        arrays[f"in_{name}_dram"] = a
        args.append(nc.dram_tensor(f"in_{name}_dram", a.shape, _mybir.dt.from_np(a.dtype), kind="ExternalInput").ap())
    for i, (shape, dtype) in enumerate(_OUTS):
        dt = _mybir.dt.from_np(_np.dtype(dtype))
        args.append(nc.dram_tensor(f"out_{i}_dram", shape, dt, kind="ExternalOutput").ap())
    build(nc, *args)
    r = _run(nc, [arrays], core_ids=[0])
    got = tuple(r.results[0][f"out_{i}_dram"] for i in range(len(_OUTS)))
    return got[0]
```

```python
from contextlib import ExitStack

import concourse.bass as bass
from concourse import mybir

ALU = mybir.AluOpType
ACT = mybir.ActivationFunctionType
AX = mybir.AxisListType.X
F32 = mybir.dt.float32
I32 = mybir.dt.int32
F32R = mybir.dt.float32r

P = 128
EPS = 1e-6
TAU = 16.0
CHUNK = 64


def build(nc, x, c, w_ada, b_ada, g_norm1, g_norm2, w_in, w_out, gmlp_ln_g, gmlp_ln_b, gmlp_ws, gmlp_bs,
          gla_w_gate, gla_b_gate, gla_norm_g, conv_w, conv_b, router_w, router_b, exp_w1, exp_w3, exp_w2,
          g_final, out, cap=P):
    T, D = x.shape[1], x.shape[2]
    TILES = T // P
    KD = D // P
    PIN = w_in.shape[2]
    RANK, KDIM = gla_w_gate.shape[1], gla_w_gate.shape[2]
    VDIM = gla_norm_g.shape[1]
    ADIM = gmlp_ln_g.shape[1]
    CDIM = conv_b.shape[1]
    AH = gmlp_ws.shape[1]
    HD = ADIM // AH
    BH = 4
    DK, DV = KDIM // BH, VDIM // BH
    PAIRS = BH // 2
    E = exp_w1.shape[1]
    FF = exp_w1.shape[3]
    KF = FF // P
    GROUPS = 4
    PER = E // GROUPS
    OVER = 2 * T // cap - 1
    LISTS = T // cap
    NONE = 4 * T
    at, col = 0, {}
    for name, n in (("uv", 2 * ADIM), ("q", KDIM), ("k", KDIM), ("v", VDIM), ("g", RANK), ("og", VDIM),
                    ("cb", CDIM), ("cc", CDIM), ("cx", CDIM)):
        col[name] = at
        at += n

    x2_dram = nc.dram_tensor("x2_dram", (T, D), F32, kind="Internal").ap()
    xn2_dram = nc.dram_tensor("xn2_dram", (T, D), F32, kind="Internal").ap()
    y_dram = nc.dram_tensor("y_dram", (2 * T, D), F32, kind="Internal").ap()
    list_dram = nc.dram_tensor("list_dram", ((LISTS + 1) * cap * E, 1), I32, kind="Internal").ap()

    with ExitStack() as ctx:
        def sb(name, shape, dt=F32):
            return ctx.enter_context(nc.sbuf_tensor(name, shape, dt))[:]

        def sem(name):
            return ctx.enter_context(nc.semaphore(name))

        def wait(eng, s, n):
            if not isinstance(n, int) or n > 0:
                eng.wait_ge(s, n)

        ident = sb("ident", [P, P])
        ones = sb("ones", [P, P])
        gate_rows = sb("gate_rows", [P, 2, D])
        mod_col = sb("mod_col", [P, 4, KD])
        scale1, scale2 = sb("scale1", [P, KD]), sb("scale2", [P, KD])
        top_w = sb("top_w", [P, TILES, 2])
        count_f = sb("count_f", [P, E])
        count_i = sb("count_i", [P, 1], I32)
        slots = sb("slots", [P, LISTS + 1, E], I32)
        slots_tok = sb("slots_tok", [P, LISTS + 1, E], I32)
        gather_idx = sb("gather_idx", [P, 4], I32)
        scatter_idx = sb("scatter_idx", [P, 2], I32)
        aid = sb("aid", [P, TILES, 2], I32)
        aid_now = sb("aid_now", [P, 2], I32)
        idx_now = sb("idx_now", [P, 2], I32)
        idx_f = sb("idx_f", [P, 2])
        table = sb("table", [P, 2, OVER], I32)
        half = sb("half", [P, 1])
        stats = sb("stats", [P, 64])
        n_stats = [0]

        def stat(n=1):
            n_stats[0] += n
            return stats[:, n_stats[0] - n:n_stats[0]]

        ss1, ms1, rs1, ss2, ms2, rs2, bn_v, bn_r = (stat() for _ in range(8))
        ssf, msf, rsf = (stat(TILES) for _ in range(3))
        row_max, neg_max, exp_sum, exp_rec, best_g, pick_g, w_sum, w_rec = (stat() for _ in range(8))
        top2, oss, oms, ors = stat(2), stat(BH), stat(BH), stat(BH)

        LOW, HIGH = 38912, 10588
        arena = [sb("arena_low", [P, LOW])]
        with nc.sbuf_tensor("arena_high", [P, HIGH], F32) as high:
            arena.append(high[:])
        split = sb("split", [P, 2 * KF * D + 4 * KF * P], F32R)
        assert 2 * KF * D + 4 * KF * P <= HIGH

        class Region:
            def __init__(self, start, part=0):
                self.at, self.part = start, part

            def take(self, *dims):
                n = 1
                for d in dims:
                    n *= d
                assert self.at + n <= (LOW, HIGH, HIGH)[self.part], self.at + n
                v = (split if self.part == 2 else arena[self.part])[:, self.at:self.at + n]
                self.at += n
                if len(dims) == 2:
                    return v.rearrange("p (a b) -> p a b", a=dims[0])
                if len(dims) == 3:
                    return v.rearrange("p (a b c) -> p a b c", a=dims[0], b=dims[1])
                return v

        R = Region(0)
        groups = (("qk", 2 * KDIM, ("q",)), ("ccx", 2 * CDIM, ("cc",)), ("cbg", CDIM + RANK, ("cb", "g")), ("v", VDIM, ("v",)),
                  ("uv", 2 * ADIM, ("uv",)), ("og", VDIM, ("og",)))
        win, win_at = {}, {}
        for name, n, _ in groups:
            win_at[name] = R.at
            win[name] = R.take(KD, n)
        wout_at = R.at
        wout = R.take(KD, D)
        tri, tri_ref, tri_last, strict = (R.take(P) for _ in range(4))
        chunk_ind = R.take(2)
        wsT = R.take(AH, P)
        bs_col = R.take(AH)
        ln_g, ln_b = R.take(ADIM), R.take(ADIM)
        gla_g = R.take(VDIM)
        wgate = R.take(KDIM)
        rw = R.take(KD, E)
        rb = R.take(E)
        convw, convb = R.take(3, 2), R.take(2)
        g1c, g2c, c_col = R.take(KD), R.take(KD), R.take(KD)
        rev, revg, eidx = R.take(PER), R.take(GROUPS), R.take(E)
        csil = R.take(KD)
        state = [R.take(PAIRS, 2 * DV) for _ in range(2)]
        mod_at = R.at
        x_res, x_nrm2 = R.take(D), R.take(D)
        yT = R.take(KD, P)
        qkT, cbT, conv_acc = R.take(4, P), R.take(2, P), R.take(2, P)
        R = Region(0, 1)
        E1, E2, E3, E4 = (R.take(KDIM) for _ in range(4))
        qeT = R.take(2, P)
        x_in, x_nrm = R.take(D), R.take(D)
        hT, h2T = R.take(KD, P), R.take(KD, P)
        qk_sb = R.take(2 * KDIM)
        q1, k2, k3, qe = E1, E2, E3, E4
        dec = R.take(4)
        v_sb = R.take(VDIM)
        uv = R.take(2 * ADIM)
        og = R.take(VDIM)
        lg1, lg2 = R.take(KDIM), R.take(KDIM)
        ccx_sb, cbg_sb, z_sb = R.take(2 * CDIM), R.take(CDIM + RANK), R.take(CDIM)
        zT = R.take(2, P + 2)
        ya = R.take(ADIM)
        yb, vn = x_nrm2[:, 0:VDIM], x_nrm2[:, VDIM:VDIM + ADIM]
        gT = R.take(P)
        sT = R.take(2, PAIRS, P)
        bn6, mv = R.take(6), R.take(2)
        r_ = {n: R.take(E) for n in ("lg", "e", "p", "c", "oh1", "oh2", "p2", "sel1", "sel2", "m", "run", "a", "t")}
        g_ = {n: R.take(GROUPS) for n in ("m1", "m2", "r", "gs", "sel", "t")}
        MOD = 6 * D // 512
        FIRST = 4
        among = {"qk": 4, "cbg": 5, "v": 6, "uv": 7}
        AMONG = 8
        k_of_step = lambda n: 1 if FIRST <= n < AMONG else 3
        wada = [Region(o).take(KD, 512) for o in (wout_at, wout_at + KD * 512)]
        Z = Region(mod_at)
        bada = [Z.take(512) for _ in range(2)]
        mod_acc = [Z.take(512) for _ in range(2)]
        mod_row = Z.take(2, D)
        csil_wide = Region(0, 1).take(KD, P)
        W1 = [Region(win_at["qk"]).take(KD, FF), Region(win_at["uv"]).take(KD, FF)]
        W3 = [Region(win_at["ccx"]).take(KD, FF), Region(win_at["og"]).take(KD, FF)]
        W2 = [Region(win_at["v"]).take(KF, D), Region(wout_at).take(KF, D)]
        M_at = wout_at + KF * D
        M = Region(M_at)
        xg = [M.take(D) for _ in range(4)]
        xT = [M.take(KD, P) for _ in range(2)]
        H = Region(0, 2)
        hT_hi, hT_lo = ([H.take(KF, P) for _ in range(2)] for _ in range(2))
        w2_hi, w2_lo = (H.take(KF, D) for _ in range(2))
        sil, hid = M.take(FF), M.take(FF)
        y_sb = [M.take(D) for _ in range(2)]
        V = Region(win_at["v"])
        ob, cum, cum2 = V.take(E), V.take(E), V.take(E)
        le3, bidx, ob3 = V.take(OVER, E), V.take(OVER, E), V.take(OVER, E)
        eb, jb, nb, is_none = V.take(OVER), V.take(OVER), V.take(OVER), V.take(OVER)
        hT_whole = xg[1][:, 0:KF * P].rearrange("p (a b) -> p a b", a=KF)
        gfin = M.take(D)
        F = Region(0)
        acc = F.take(TILES, D)
        assert F.at <= win_at["cbg"]
        yy = F.take(TILES, 2 * D)
        sq_junk = F.take(D)
        y_parts = ((0, 1), (1, 2), (2, 4), (4, 6), (6, TILES))
        assert F.at <= M_at

        bank = [ctx.enter_context(nc.psum_tensor(f"bank{i}", [P, 512], F32)) for i in range(8)]

        S = {}
        for n in ("params_ld", "consts", "wout_ld", "c_ld", "csil_ready", "lists_st", "setup_mm", "scale_ready", "loop_ready",
                  "acc_ready", "mod_mm", "mod_evac",
                  "x_ld", "xr_ld", "xss", "ms1", "rs1", "xn_ready", "x_tr", "hT_act", "hT_dve",
                  "qk_mm", "ccx_mm", "cbg_mm", "v_mm", "uv_mm", "og_mm",
                  "g_tr", "gT_ready", "z_mm", "absz", "lnz", "L_ready", "qk_ready", "ccx_ready", "cbg_ready",
                  "D_mm", "exps", "prods", "qk_tr", "qkT_ready", "v_ready", "kv_mm", "state1", "state0", "sc_mm", "sT_ready",
                  "o_mm", "oss", "oms", "ors", "yb_ready", "uv_ready", "og_ready", "z_ready", "z_tr", "zT_ready",
                  "conv_done", "bn", "bnr", "vn0", "vn1", "vn_ready", "sv_mm", "ya_ready", "y_tr", "yT_ready", "out_mm",
                  "x2_ready", "x2ss", "ms2", "rs2", "xn2_ready", "x2_st", "x2_tr", "h2_act", "h2_dve", "r_mm",
                  "lg_read", "lg_ready", "e_ready", "m_ready", "pos_mm", "pos_read", "idx_ready", "aid_ready",
                  "list_sc0", "list_sc1", "run_ready", "cnt_mm", "slots_ld", "slots_ready",
                  "gidx", "sidx", "xt_tr", "xT_act", "xT_dve", "h1_mm", "h3_mm", "sil_ready", "h_ready",
                  "h_tr", "hT_hi_ready", "hT_lo_ready", "w2_hi_half", "w2_lo_ready", "y_mm", "y_ready",
                  "ov_iota", "ov_table", "ov_w", "ov_gather", "ov_tr", "ov_xT", "ov_h", "ov_sil", "ov_hid",
                  "ov_htr", "ov_hT", "ov_y", "ov_ysb", "ov_sc", "gp_passed", "dve_passed",
                  "early_ld", "fin_acc", "fin_ss", "fin_ms", "fin_rs", "fin_out"):
            S[n] = sem(n)
        win_ld = {name: sem(f"win_ld_{name}") for name, _, _ in groups}
        wada_ld = [sem(f"wada_ld{h}") for h in range(2)]
        w1_ld = [sem(f"w1_ld{h}") for h in range(2)]
        w3_ld = [sem(f"w3_ld{h}") for h in range(2)]
        w2_ld = [sem(f"w2_ld{h}") for h in range(2)]
        gath = [sem(f"gath{h}") for h in range(4)]
        scat = [sem(f"scat{h}") for h in range(2)]
        y_ld = [sem(f"y_ld{h}") for h in range(len(y_parts))]
        out_st = sem("out_st")

        x_t = x[0].rearrange("(t p) d -> t p d", p=P)
        wada_v = w_ada[0].rearrange("(p k) n -> p k n", k=KD)
        win_v = w_in[0].rearrange("(p k) n -> p k n", k=KD)
        wout_v = w_out[0].rearrange("(k p) n -> p k n", k=KD)
        x2_t = x2_dram.rearrange("(t p) d -> t p d", p=P)
        xn2_t = xn2_dram.rearrange("(t p) d -> t p d", p=P)
        y_t = y_dram.rearrange("(t p two) d -> p t (two d)", p=P, two=2)
        out_t = out[0].rearrange("(t p) d -> t p d", p=P)
        list_v = list_dram.rearrange("(j s e) one -> s j (e one)", s=cap, e=E)
        w1_v = exp_w1[0].rearrange("e (p k) f -> e p (k f)", k=KD)
        w3_v = exp_w3[0].rearrange("e (p k) f -> e p (k f)", k=KD)
        w2_v = exp_w2[0].rearrange("e (p k) f -> e p (k f)", k=KF)
        flat = lambda v: v.rearrange("p k f -> p (k f)")

        def one(v, i):
            return v[i] if isinstance(i, int) else v[bass.ds(i, 1)].rearrange("a p n -> (a p) n")

        def column(v, i):
            return v[:, i:i + 1] if isinstance(i, int) else v[:, bass.ds(i, 1)]

        def tiles(eng, body):
            body(0)
            with eng.Fori(1, TILES - 2) as t:
                body(t)
            body(TILES - 2)
            body(TILES - 1)

        def before(t, last):
            return not isinstance(t, int) or t < last

        def after(t, first):
            return not isinstance(t, int) or t > first

        block = ctx.enter_context(nc.Block())
        PARAMS = 14

        @block.sync
        def _(sp):
            with nc.allow_non_contiguous_dma(reason="small parameter vectors"):
                sp.dma_start(c_col, c.rearrange("a (p k) -> p (a k)", k=KD)).then_inc(S["c_ld"], 16)
                sp.dma_start(g1c, g_norm1.rearrange("a (p k) -> p (a k)", k=KD)).then_inc(S["c_ld"], 16)

                def ada(n, h):
                    wait(sp, S["mod_mm"], n - 1)
                    cols = slice(n * 512, n * 512 + 512) if isinstance(n, int) else bass.ds(n * 512, 512)
                    sp.dma_start(wada[h], wada_v[:, :, cols]).then_inc(wada_ld[h], 16)
                    sp.dma_start(bada[h][0:1, :], b_ada[:, cols]).then_inc(wada_ld[h], 16)

                ada(0, 0)
                sp.dma_start(x_in, x_t[0]).then_inc(S["x_ld"], 16)
                ada(1, 1)
                for dst, src in (
                    (g2c, g_norm2.rearrange("a (p k) -> p (a k)", k=KD)),
                    (wsT, gmlp_ws[0].rearrange("h t s -> t h s")),
                    (bs_col, gmlp_bs[0].rearrange("h t -> t h")),
                    (ln_g, gmlp_ln_g.partition_broadcast(P).rearrange("p a n -> p (a n)")),
                    (ln_b, gmlp_ln_b.partition_broadcast(P).rearrange("p a n -> p (a n)")),
                    (gla_g, gla_norm_g.partition_broadcast(P).rearrange("p a n -> p (a n)")),
                    (wgate[0:RANK, :], gla_w_gate[0]),
                    (wgate[RANK:RANK + 1, :], gla_b_gate),
                    (rw, router_w.rearrange("(p k) e -> p k e", k=KD)),
                    (rb, router_b.rearrange("(a e) -> a e", a=1).partition_broadcast(P).rearrange("p a n -> p (a n)")),
                    (convw[:, 0, :], conv_w[0, 0].rearrange("(t p) -> p t", p=P)),
                    (convw[:, 1, :], conv_w[0, 1].rearrange("(t p) -> p t", p=P)),
                    (convw[:, 2, :], conv_w[0, 2].rearrange("(t p) -> p t", p=P)),
                    (convb, conv_b[0].rearrange("(t p) -> p t", p=P)),
                ):
                    sp.dma_start(dst, src).then_inc(S["params_ld"], 16)

            for n in range(2, FIRST):
                ada(n, n % 2)
            sp.wait_ge(S["xn_ready"], 1)
            sp.dma_start(x_in, x_t[1]).then_inc(S["x_ld"], 16)
            sp.wait_ge(S["consts"], 1)
            sp.dma_start(list_v, slots[0:cap]).then_inc(S["lists_st"], 16)
            for name, n, parts in groups:
                at_ = 0
                for part in parts:
                    size = RANK if part == "g" else n - RANK * (len(parts) - 1)
                    sp.dma_start(win[name][:, :, at_:at_ + size],
                                 win_v[:, :, col[part]:col[part] + size]).then_inc(win_ld[name], 16)
                    at_ += size
                if name in among:
                    ada(among[name], among[name] % 2)
            with sp.Fori(AMONG // 2, MOD // 2) as i:
                for h in range(2):
                    ada(2 * i + h, h)
            sp.wait_ge(S["mod_mm"], MOD)
            sp.dma_start(wout, wout_v).then_inc(S["wout_ld"], 16)
            sp.wait_ge(S["loop_ready"], 1)

            def load_residual(t):
                wait(sp, S["x2_st"], 32 * t)
                sp.dma_start(x_res, one(x_t, t)).then_inc(S["xr_ld"], 16)

            def store_rows(t):
                sp.wait_ge(S["x2_ready"], t + 1)
                sp.dma_start(one(x2_t, t), x_res).then_inc(S["x2_st"], 16)
                sp.wait_ge(S["xn2_ready"], t + 1)
                sp.dma_start(one(xn2_t, t), x_nrm2).then_inc(S["x2_st"], 16)

            def tile(t):
                load_residual(t)
                if before(t, TILES - 2):
                    sp.wait_ge(S["xn_ready"], t + 2)
                    sp.dma_start(x_in, one(x_t, t + 2)).then_inc(S["x_ld"], 16)
                store_rows(t)

            def expert_weights(e, h):
                wait(sp, S["h1_mm"], e - 1)
                sp.dma_start(flat(W1[h]), one(w1_v, e)).then_inc(w1_ld[h], 16)
                wait(sp, S["h3_mm"], e - 1)
                sp.dma_start(flat(W3[h]), one(w3_v, e)).then_inc(w3_ld[h], 16)
                wait(sp, S["w2_lo_ready"], e - 1)
                sp.dma_start(flat(W2[h]), one(w2_v, e)).then_inc(w2_ld[h], 16)

            tile(0)
            with sp.Fori(1, TILES - 2) as t:
                tile(t)
            tile(TILES - 2)
            load_residual(TILES - 1)
            sp.wait_ge(S["og_mm"], TILES)
            sp.dma_start(flat(W1[0]), w1_v[0]).then_inc(w1_ld[0], 16)
            sp.dma_start(flat(W3[0]), w3_v[0]).then_inc(w3_ld[0], 16)
            sp.dma_start(flat(W2[0]), w2_v[0]).then_inc(w2_ld[0], 16)
            sp.dma_start(flat(W1[1]), w1_v[1]).then_inc(w1_ld[1], 16)
            sp.dma_start(flat(W3[1]), w3_v[1]).then_inc(w3_ld[1], 16)
            store_rows(TILES - 1)
            sp.dma_start(flat(W2[1]), w2_v[1]).then_inc(w2_ld[1], 16)
            for k in range(2):
                sp.wait_ge(S[f"list_sc{k}"], 16 * TILES)
            sp.dma_start(slots[0:cap], list_v).then_inc(S["slots_ld"], 16)
            with sp.Fori(1, E // 2) as i:
                for h in range(2):
                    expert_weights(2 * i + h, h)
            sp.wait_ge(S["x2_st"], 32 * TILES)
            sp.dma_start(gfin, g_final.rearrange("(a n) -> a n", a=1).partition_broadcast(P)
                         .rearrange("p a n -> p (a n)")).then_inc(S["early_ld"], 16)
            sp.wait_ge(S["h3_mm"], E - 1)
            sp.dma_start(acc, x2_dram.rearrange("(t p) d -> p t d", p=P)).then_inc(S["early_ld"], 16)
            most = sp.value_load(count_i[0:1, 0:1], min_val=0, max_val=T)
            with sp.If(most > cap):
                sp.wait_ge(S["y_mm"], E)
                sp.wait_ge(S["ov_table"], 1)
                with sp.Fori(0, OVER) as b:
                    sp.wait_ge(S["ov_y"], b + 1)
                    e = sp.value_load(table[0:1, 0, bass.ds(b, 1)], min_val=0, max_val=E - 1)
                    sp.dma_start(flat(W1[1]), one(w1_v, e)).then_inc(S["ov_w"], 16)
                    sp.dma_start(flat(W3[1]), one(w3_v, e)).then_inc(S["ov_w"], 16)
                    sp.dma_start(flat(W2[1]), one(w2_v, e)).then_inc(S["ov_w"], 16)
                sp.wait_ge(S["ov_sc"], 16 * OVER)
            for h in range(2):
                sp.wait_ge(scat[h], 16 * E // 2)
            for h, (a, b) in enumerate(y_parts):
                sp.dma_start(yy[:, a:b, :], y_t[:, a:b, :]).then_inc(y_ld[h], 16)
            sp.wait_ge(out_st, 16 * TILES)

        @block.gpsimd
        def _(gp):
            gp.memset(slots.rearrange("p a b -> p (a b)"), NONE).then_inc(S["consts"], 1)
            gp.memset(half, -0.5)
            gp.memset(ones, 1.0)
            gp.memset(ident, 0.0)
            gp.drain()
            gp.affine_select(out=ident, in_=ident, pattern=[[-1, P]], compare_op=ALU.not_equal, fill=1.0, base=0,
                             channel_multiplier=1).then_inc(S["consts"], 1)
            for m in (tri, tri_ref, tri_last):
                gp.memset(m, 1.0 / TAU)
            gp.memset(chunk_ind, 1.0 / TAU)
            gp.memset(strict, 1.0)
            gp.iota(rev, pattern=[[-1, PER]], base=PER, channel_multiplier=0, allow_small_or_imprecise_dtypes=True)
            gp.iota(revg, pattern=[[-1, GROUPS]], base=GROUPS, channel_multiplier=0, allow_small_or_imprecise_dtypes=True)
            gp.iota(eidx, pattern=[[1, E]], base=0, channel_multiplier=0, allow_small_or_imprecise_dtypes=True)
            gp.iota(aid, pattern=[[2 * P, TILES], [1, 2]], base=0, channel_multiplier=2)
            gp.drain()

            def keep(v, base, per_row, per_col, n):
                gp.affine_select(out=v, in_=v, pattern=[[per_col, n]], compare_op=ALU.is_ge, fill=0.0, base=base,
                                 channel_multiplier=per_row)
                gp.drain()

            C = CHUNK
            keep(strict, -1, -1, 1, P)
            keep(tri, 0, -1, 1, P)
            keep(tri[:, C:P], -C, 1, 0, C)
            keep(tri_last, -1, 1, -1, P)
            keep(tri_last[:, 0:C], C - 1, -1, 0, C)
            keep(tri_ref[:, 0:C], C // 2, -1, 0, C)
            keep(tri_ref[:, C:P], C + C // 2, -1, 0, C)
            keep(tri_ref[:, C:P], -C, 1, 0, C)
            keep(chunk_ind[:, 0:1], C - 1, -1, 0, 1)
            keep(chunk_ind[:, 1:2], -C, 1, 0, 1)
            gp.tensor_tensor(tri_ref, tri, tri_ref, ALU.subtract).then_inc(S["consts"], 1)

            def rsqrt(dst, src, n, ready, value, done):
                gp.wait_ge(ready, value)
                gp.tensor_tensor(dst, src, half.to_broadcast([P, n]) if n > 1 else half, ALU.pow).then_inc(done, 1)

            def enlist(t):
                for k in range(2):
                    wait(gp, S[f"list_sc{k}"], 16 * t)
                gp.tensor_copy(aid_now, aid[:, t, :] if isinstance(t, int) else
                               aid[:, bass.ds(t, 1), :].rearrange("p a b -> p (a b)")).then_inc(S["aid_ready"], 1)
                gp.wait_ge(S["aid_ready"], t + 1)
                gp.wait_ge(S["idx_ready"], t + 1)
                gp.sem_inc(S["gp_passed"], 1)
                for k in range(2):
                    gp.indirect_dma_start(out=list_dram, out_offset=bass.IndirectOffsetOnAxis(ap=idx_now[:, k:k + 1], axis=0),
                                          in_=aid_now[:, k:k + 1], in_offset=None, bounds_check=LISTS * cap * E - 1,
                                          oob_is_err=False).then_inc(S[f"list_sc{k}"], 16)

            def tile(t):
                rsqrt(bn_r, bn_v, 1, S["bn"], t + 1, S["bnr"])
                gp.wait_ge(S["vn0"], t + 1)
                gp.tensor_tensor(vn, vn, ln_g, ALU.mult).then_inc(S["vn1"], 1)
                gp.wait_ge(S["vn1"], t + 1)
                gp.tensor_tensor(vn, vn, ln_b, ALU.add).then_inc(S["vn_ready"], 1)
                if before(t, TILES - 2):
                    rsqrt(rs1, ms1, 1, S["ms1"], t + 3, S["rs1"])
                rsqrt(ors, oms, BH, S["oms"], t + 1, S["ors"])
                rsqrt(rs2, ms2, 1, S["ms2"], t + 1, S["rs2"])
                if after(t, 0):
                    enlist(t - 1)

            for t in range(2):
                rsqrt(rs1, ms1, 1, S["ms1"], t + 1, S["rs1"])
            gp.wait_ge(S["lists_st"], 16)
            tiles(gp, tile)
            enlist(TILES - 1)

            gp.wait_ge(S["slots_ready"], 1)
            gp.wait_ge(S["x2_st"], 32 * TILES)

            def gather(e, h):
                gp.tensor_copy(gather_idx[:, h:h + 1], column(slots_tok[:, 0, :], e)).then_inc(S["gidx"], 1)
                gp.wait_ge(S["gidx"], e + 1)
                gp.sem_inc(S["gp_passed"], 1)
                gp.indirect_dma_start(out=xg[h], out_offset=None, in_=xn2_dram,
                                      in_offset=bass.IndirectOffsetOnAxis(ap=gather_idx[:, h:h + 1], axis=0),
                                      bounds_check=T - 1, oob_is_err=False).then_inc(gath[h], 16)

            def scatter(e, h, before_):
                wait(gp, scat[h], before_)
                gp.tensor_copy(scatter_idx[:, h:h + 1], column(slots[:, 0, :], e)).then_inc(S["sidx"], 1)
                gp.wait_ge(S["sidx"], e + 1)
                gp.wait_ge(S["y_ready"], e + 1)
                gp.sem_inc(S["gp_passed"], 1)
                gp.indirect_dma_start(out=y_dram, out_offset=bass.IndirectOffsetOnAxis(ap=scatter_idx[:, h:h + 1], axis=0),
                                      in_=y_sb[h], in_offset=None, bounds_check=2 * T - 1,
                                      oob_is_err=False).then_inc(scat[h], 16)

            for e in range(4):
                gather(e, e)

            def step(e, j, half_e):
                if before(e, E - 3):
                    gp.wait_ge(S["xt_tr"], e)
                    gather(e + 3, (j + 3) % 4)
                if after(e, 1):
                    scatter(e - 2, j % 2, 16 * (half_e - 1))

            for e in range(1, 4):
                step(e, e, e // 2)
            with gp.Fori(1, E // 4 - 1) as i:
                for j in range(4):
                    step(4 * i + j, j, 2 * i + j // 2)
            for e in range(E - 4, E + 2):
                step(e, e % 4, e // 2)
            most = gp.value_load(count_i[0:1, 0:1], min_val=0, max_val=T)
            with gp.If(most > cap):
                gp.iota(bidx.rearrange("p a b -> p (a b)"), pattern=[[1, OVER], [0, E]], base=0, channel_multiplier=0,
                        allow_small_or_imprecise_dtypes=True)
                gp.iota(nb, pattern=[[1, OVER]], base=0, channel_multiplier=0,
                        allow_small_or_imprecise_dtypes=True).then_inc(S["ov_iota"], 1)
                gp.wait_ge(S["ov_table"], 1)
                for h in range(2):
                    gp.wait_ge(scat[h], 16 * E // 2)
                with gp.Fori(0, OVER) as b:
                    at_ = gp.value_load(table[0:1, 1, bass.ds(b, 1)], min_val=0, max_val=(LISTS + 1) * E - 1)
                    gp.tensor_copy(gather_idx[:, 0:1], slots_tok.rearrange("p a b -> p (a b)")[:, bass.ds(at_, 1)]).then_inc(S["gidx"], 1)
                    gp.tensor_copy(scatter_idx[:, 0:1], slots.rearrange("p a b -> p (a b)")[:, bass.ds(at_, 1)]).then_inc(S["sidx"], 1)
                    gp.wait_ge(S["gidx"], E + b + 1)
                    gp.wait_ge(S["sidx"], E + b + 1)
                    gp.sem_inc(S["gp_passed"], 1)
                    gp.indirect_dma_start(out=xg[0], out_offset=None, in_=xn2_dram,
                                          in_offset=bass.IndirectOffsetOnAxis(ap=gather_idx[:, 0:1], axis=0),
                                          bounds_check=T - 1, oob_is_err=False).then_inc(S["ov_gather"], 16)
                    gp.wait_ge(S["ov_ysb"], b + 1)
                    gp.sem_inc(S["gp_passed"], 1)
                    gp.indirect_dma_start(out=y_dram, out_offset=bass.IndirectOffsetOnAxis(ap=scatter_idx[:, 0:1], axis=0),
                                          in_=y_sb[0], in_offset=None, bounds_check=2 * T - 1,
                                          oob_is_err=False).then_inc(S["ov_sc"], 16)
                    gp.wait_ge(S["ov_gather"], 16 * b + 16)
                    gp.wait_ge(S["ov_sc"], 16 * b + 16)
            for t in range(TILES):
                rsqrt(rsf[:, t:t + 1], msf[:, t:t + 1], 1, S["fin_ms"], t + 1, S["fin_rs"])

        @block.tensor
        def _(pe):
            pe.wait_ge(S["consts"], 2)
            pe.wait_ge(S["csil_ready"], 2)

            def mod_product(n):
                h, round_ = n % 2, n // 2
                pe.wait_ge(wada_ld[h], 32 * round_ + 32)
                wait(pe, S["mod_evac"], n - 1)
                for k in range(k_of_step(n)):
                    pe.matmul(bank[2 + h][:], csil_wide[:, k, :], wada[h][:, k, :], start=(k == 0), stop=False)
                pe.wait_ge(S["acc_ready"], n + 1)
                pe.matmul(bank[2 + h][:], ones, mod_acc[h], start=False, stop=True).then_inc(S["mod_mm"], 1)

            def mod_columns(out_):
                for n in range(2):
                    row = mod_row[0:1, n, :].rearrange("p (m k) -> p k m", k=KD)
                    for k in range(KD):
                        c_ = n * KD + k
                        mm = pe.matmul(out_[:, c_:c_ + 1], row[:, k, :], ones[0:1, 0:1], start=True, stop=True)
                mm.then_inc(S["setup_mm"], 1)

            for n in range(FIRST):
                mod_product(n)
            def rows(out_, name, n, done):
                for k in range(KD):
                    mm = pe.matmul(out_, hT[:, k, :], win[name][:, k, :], start=(k == 0), stop=(k == KD - 1))
                mm.then_inc(done, 1)

            def transpose8(src, done):
                cols = src.rearrange("p (m k) -> p k m", k=KD)
                for k in range(KD):
                    mm = pe.transpose(bank[k // 4][:, (k % 4) * P:(k % 4 + 1) * P], cols[:, k, :], ident)
                mm.then_inc(done, 1)

            def gates(t):
                pe.wait_ge(S["L_ready"], t + 1)
                wait(pe, S["x2_ready"], t)
                pe.matmul(bank[2][:, 0:KDIM], tri, lg1, start=True, stop=True)
                pe.matmul(bank[2][:, KDIM:2 * KDIM], tri_ref, lg1, start=True, stop=True)
                pe.matmul(bank[3][:, 0:KDIM], tri_last, lg1, start=True, stop=True)
                for p in range(PAIRS):
                    mm = pe.matmul(bank[3][:, KDIM + 2 * p:KDIM + 2 * p + 2], lg1[:, p * P:(p + 1) * P], chunk_ind,
                                   start=True, stop=True)
                mm.then_inc(S["D_mm"], 1)

            def low_rank_turn(t):
                pe.wait_ge(S["cbg_ready"], t + 1)
                pe.transpose(bank[6][0:RANK, 0:P], cbg_sb[:, CDIM:], ident).then_inc(S["g_tr"], 1)

            def low_rank(t):
                pe.wait_ge(S["gT_ready"], t + 1)
                pe.matmul(bank[6][:, 0:KDIM], gT[0:RANK + 1, :], wgate[0:RANK + 1, :], start=True,
                          stop=True).then_inc(S["z_mm"], 1)

            def router(t):
                pe.wait_ge(S["h2_act"], t + 1)
                pe.wait_ge(S["h2_dve"], t + 1)
                wait(pe, S["pos_read"], t)
                for k in range(KD):
                    mm = pe.matmul(bank[5][:, 0:E], h2T[:, k, :], rw[:, k, :], start=(k == 0), stop=(k == KD - 1))
                mm.then_inc(S["r_mm"], 1)

            def places(t):
                pe.wait_ge(S["m_ready"], t + 1)
                pe.matmul(bank[5][:, 0:E], strict, r_["m"], start=True, stop=False)
                pe.matmul(bank[5][:, 0:E], ones, r_["run"], start=False, stop=True).then_inc(S["pos_mm"], 1)

            pe.wait_ge(S["xn_ready"], 1)
            transpose8(x_nrm, S["x_tr"])
            pe.wait_ge(S["mod_evac"], FIRST)
            mod_columns(bank[2])
            pe.wait_ge(S["hT_act"], 1)
            pe.wait_ge(S["hT_dve"], 1)
            pe.wait_ge(win_ld["qk"], 16)
            rows(bank[7][:], "qk", 2 * KDIM, S["qk_mm"])
            mod_product(4)
            pe.wait_ge(win_ld["ccx"], 16)
            rows(bank[4][:], "ccx", 2 * CDIM, S["ccx_mm"])
            pe.wait_ge(win_ld["cbg"], 32)
            pe.wait_ge(S["qk_ready"], 1)
            rows(bank[7][:, 0:CDIM + RANK], "cbg", CDIM + RANK, S["cbg_mm"])
            pe.wait_ge(S["params_ld"], 16 * PARAMS)
            mod_product(5)
            low_rank_turn(0)
            low_rank(0)
            pe.wait_ge(win_ld["v"], 16)
            pe.wait_ge(S["cbg_ready"], 1)
            rows(bank[7][:], "v", VDIM, S["v_mm"])
            mod_product(6)
            pe.wait_ge(win_ld["uv"], 16)
            rows(bank[5][:], "uv", 2 * ADIM, S["uv_mm"])
            mod_product(7)
            pe.wait_ge(win_ld["og"], 16)
            pe.wait_ge(S["v_ready"], 1)
            rows(bank[7][:], "og", VDIM, S["og_mm"])
            for n in range(AMONG, MOD - 2):
                mod_product(n)
            pe.wait_ge(S["hT_act"], 1)
            pe.wait_ge(S["hT_dve"], 1)
            pe.wait_ge(S["params_ld"], 16 * PARAMS)
            for h in range(AH):
                mm = pe.transpose(bank[0][:, h * P:(h + 1) * P], wsT[:, h, :], ident)
            mm.then_inc(S["setup_mm"], 1)
            pe.wait_ge(S["mod_evac"], 10)
            mod_columns(bank[1])
            for n in range(MOD - 2, MOD):
                mod_product(n)
            pe.wait_ge(S["mod_evac"], MOD)
            pe.wait_ge(S["loop_ready"], 1)

            def tile(t):
                nxt = before(t, TILES - 1)
                gates(t)
                if nxt:
                    pe.wait_ge(S["xn_ready"], t + 2)
                    wait(pe, S["h2_act"], t)
                    wait(pe, S["h2_dve"], t)
                    transpose8(x_nrm, S["x_tr"])
                pe.wait_ge(S["z_ready"], t + 1)
                pe.wait_ge(S["cbg_ready"], t + 1)
                wait(pe, S["yb_ready"], t)
                for j in range(2):
                    pe.transpose(bank[4][:, j * P:(j + 1) * P], z_sb[:, j * P:(j + 1) * P], ident)
                for j in range(2):
                    mm = pe.transpose(bank[4][:, (2 + j) * P:(3 + j) * P], cbg_sb[:, j * P:(j + 1) * P], ident)
                mm.then_inc(S["z_tr"], 1)
                if after(t, 0):
                    pe.wait_ge(S["uv_ready"], t + 1)
                    router(t - 1)
                if nxt:
                    pe.wait_ge(S["hT_act"], t + 2)
                    pe.wait_ge(S["hT_dve"], t + 2)
                    pe.wait_ge(S["og_ready"], t + 1)
                    rows(bank[7][:], "qk", 2 * KDIM, S["qk_mm"])
                    pe.wait_ge(S["zT_ready"], t + 1)
                    rows(bank[4][:], "ccx", 2 * CDIM, S["ccx_mm"])
                pe.wait_ge(S["prods"], t + 1)
                for j in range(2):
                    pe.transpose(bank[0][:, j * P:(j + 1) * P], q1[:, j * P:(j + 1) * P], ident)
                    pe.transpose(bank[0][:, (2 + j) * P:(3 + j) * P], k2[:, j * P:(j + 1) * P], ident)
                    mm = pe.transpose(bank[1][:, j * P:(j + 1) * P], qe[:, j * P:(j + 1) * P], ident)
                mm.then_inc(S["qk_tr"], 1)
                for ch in range(2):
                    r = slice(ch * CHUNK, (ch + 1) * CHUNK)
                    for p in range(PAIRS):
                        mm = pe.matmul(bank[2 + ch][:, p * 2 * DV:(p + 1) * 2 * DV], k3[r, p * P:(p + 1) * P],
                                       v_sb[r, p * 2 * DV:(p + 1) * 2 * DV], start=True, stop=True)
                mm.then_inc(S["kv_mm"], 1)
                if nxt:
                    pe.wait_ge(S["qk_ready"], t + 2)
                    rows(bank[7][:, 0:CDIM + RANK], "cbg", CDIM + RANK, S["cbg_mm"])
                pe.wait_ge(S["qkT_ready"], t + 1)
                for hh in range(2):
                    r = slice(hh * DK, (hh + 1) * DK)
                    for p in range(PAIRS):
                        mm = pe.matmul(bank[hh][:, p * P:(p + 1) * P], qkT[r, 2 + p, :], qkT[r, p, :],
                                       start=True, stop=True)
                mm.then_inc(S["sc_mm"], 1)
                pe.wait_ge(S["vn_ready"], t + 1)
                wait(pe, S["lg_read"], t)
                for h in range(AH):
                    mm = pe.matmul(bank[5][:, h * HD:(h + 1) * HD], wsT[:, h, :], vn[:, h * HD:(h + 1) * HD],
                                   start=True, stop=True)
                mm.then_inc(S["sv_mm"], 1)
                if nxt:
                    low_rank_turn(t + 1)
                pe.wait_ge(S["sT_ready"], t + 1)
                pe.wait_ge(S["state1"], t + 1)
                if nxt:
                    pe.wait_ge(S["ccx_ready"], t + 2)
                for p in range(PAIRS):
                    cols = slice(p * 2 * DV, (p + 1) * 2 * DV)
                    for ch in range(2):
                        r = slice(ch * CHUNK, (ch + 1) * CHUNK)
                        pe.matmul(bank[4][r, cols], qeT[:, p, r], state[ch][:, p, :], start=True, stop=False,
                                  skip_group_check=True)
                    for hh in range(2):
                        h = 2 * p + hh
                        mm = pe.matmul(bank[4][:, h * DV:(h + 1) * DV], sT[:, hh, p, :], v_sb[:, h * DV:(h + 1) * DV],
                                       start=False, stop=True, skip_group_check=True)
                mm.then_inc(S["o_mm"], 1)
                if nxt:
                    pe.wait_ge(S["cbg_ready"], t + 2)
                    rows(bank[7][:], "v", VDIM, S["v_mm"])
                pe.wait_ge(S["ya_ready"], t + 1)
                for j in range(2):
                    pe.transpose(bank[0][:, j * P:(j + 1) * P], ya[:, j * P:(j + 1) * P], ident)
                pe.wait_ge(S["yb_ready"], t + 1)
                for j in range(4):
                    mm = pe.transpose(bank[j // 2][:, (2 * (j < 2) + j % 2) * P:(2 * (j < 2) + j % 2 + 1) * P],
                                      yb[:, j * P:(j + 1) * P], ident)
                mm.then_inc(S["y_tr"], 1)
                if nxt:
                    rows(bank[5][:], "uv", 2 * ADIM, S["uv_mm"])
                    low_rank(t + 1)
                pe.wait_ge(S["yT_ready"], t + 1)
                pe.wait_ge(S["conv_done"], t + 1)
                pe.wait_ge(S["state0"], t + 1)
                if not after(t, 0):
                    pe.wait_ge(S["wout_ld"], 16)
                for n in range(2):
                    for k in range(KD):
                        mm = pe.matmul(bank[2 + n][:], yT[:, k, :], wout[:, k, n * 512:(n + 1) * 512],
                                       start=(k == 0), stop=(k == KD - 1))
                mm.then_inc(S["out_mm"], 1)
                if nxt:
                    pe.wait_ge(S["v_ready"], t + 2)
                    rows(bank[7][:], "og", VDIM, S["og_mm"])
                if after(t, 0):
                    if nxt:
                        pe.wait_ge(S["uv_ready"], t + 2)
                    places(t - 1)
                pe.wait_ge(S["xn2_ready"], t + 1)
                transpose8(x_nrm2, S["x2_tr"])

            tiles(pe, tile)
            router(TILES - 1)
            pe.wait_ge(S["lg_read"], TILES)
            places(TILES - 1)
            pe.wait_ge(S["run_ready"], TILES)
            pe.wait_ge(S["pos_read"], TILES)
            pe.matmul(bank[5][:, 0:E], ones, r_["run"], start=True, stop=True).then_inc(S["cnt_mm"], 1)

            def x_turn(buf, ready, n, done):
                pe.wait_ge(ready, n)
                cols = buf.rearrange("p (m k) -> p k m", k=KD)
                for k in range(KD):
                    mm = pe.transpose(bank[k // 4][:, (k % 4) * P:(k % 4 + 1) * P], cols[:, k, :], ident)
                mm.then_inc(done, 1)

            def up(h, n, e):
                pe.wait_ge(S["xT_act"], e + 1)
                pe.wait_ge(S["xT_dve"], e + 1)
                pe.wait_ge(w1_ld[h], 16 * n + 16)
                wait(pe, S["sil_ready"], e)
                for k in range(KD):
                    mm = pe.matmul(bank[2][:], xT[h][:, k, :], W1[h][:, k, :], start=(k == 0), stop=(k == KD - 1))
                mm.then_inc(S["h1_mm"], 1)
                pe.wait_ge(w3_ld[h], 16 * n + 16)
                wait(pe, S["h_ready"], e)
                for k in range(KD):
                    mm = pe.matmul(bank[3][:], xT[h][:, k, :], W3[h][:, k, :], start=(k == 0), stop=(k == KD - 1))
                mm.then_inc(S["h3_mm"], 1)

            def h_turn(h, e):
                pe.wait_ge(S["h_ready"], e + 1)
                wait(pe, S["hT_lo_ready"], e)
                cols = hid.rearrange("p (m k) -> p k m", k=KF)
                for k in range(KF):
                    mm = pe.transpose(bank[4][:, k * P:(k + 1) * P], cols[:, k, :], ident)
                mm.then_inc(S["h_tr"], 1)

            def down(h, e):
                pe.wait_ge(S["hT_hi_ready"], e + 1)
                pe.wait_ge(S["hT_lo_ready"], e + 1)
                pe.wait_ge(S["w2_lo_ready"], e + 1)
                wait(pe, S["y_ready"], e)
                for j in range(2):
                    parts = [(a, b, k) for k in range(KF) for a, b in ((hT_hi, w2_hi), (hT_hi, w2_lo), (hT_lo, w2_hi))]
                    for n, (a, b, k) in enumerate(parts):
                        mm = pe.matmul(bank[5 + j][:], a[h][:, k, :], b[:, k, j * 512:(j + 1) * 512],
                                       start=(n == 0), stop=(n == len(parts) - 1))
                mm.then_inc(S["y_mm"], 1)

            def down_whole(done):
                for j in range(2):
                    for k in range(KF):
                        mm = pe.matmul(bank[5 + j][:], hT_whole[:, k, :], W2[1][:, k, j * 512:(j + 1) * 512],
                                       start=(k == 0), stop=(k == KF - 1))
                mm.then_inc(done, 1)

            def expert(e, j, half_e, quarter):
                h = j % 2
                up(h, half_e, e)
                if before(e, E - 1):
                    x_turn(xg[(j + 1) % 4], gath[(j + 1) % 4], 16 * quarter + 16, S["xt_tr"])
                if after(e, 0):
                    down(1 - h, e - 1)
                h_turn(h, e)

            x_turn(xg[0], gath[0], 16, S["xt_tr"])
            for e in range(3):
                expert(e, e, e // 2, (e + 1) // 4)
            with pe.Fori(0, E // 4 - 1) as i:
                for j in range(4):
                    expert(4 * i + 3 + j, (3 + j) % 4, 2 * i + (3 + j) // 2, i + 1 + j // 4)
            expert(E - 1, (E - 1) % 4, (E - 1) // 2, E // 4)
            pe.wait_ge(S["hT_hi_ready"], E)
            pe.wait_ge(w2_ld[1], 16 * (E // 2))
            pe.wait_ge(S["y_ready"], E - 1)
            down_whole(S["y_mm"])
            most = pe.value_load(count_i[0:1, 0:1], min_val=0, max_val=T)
            with pe.If(most > cap):
                pe.sem_inc(S["ov_y"], 1)
                with pe.Fori(0, OVER) as b:
                    x_turn(xg[0], S["ov_gather"], 16 * b + 16, S["ov_tr"])
                    pe.wait_ge(S["ov_xT"], b + 1)
                    pe.wait_ge(S["ov_w"], 48 * b + 48)
                    for w, bk in ((W1[1], 2), (W3[1], 3)):
                        for k in range(KD):
                            mm = pe.matmul(bank[bk][:], xT[0][:, k, :], w[:, k, :], start=(k == 0), stop=(k == KD - 1))
                    mm.then_inc(S["ov_h"], 1)
                    pe.wait_ge(S["ov_hid"], b + 1)
                    cols = hid.rearrange("p (m k) -> p k m", k=KF)
                    for k in range(KF):
                        mm = pe.transpose(bank[4][:, k * P:(k + 1) * P], cols[:, k, :], ident)
                    mm.then_inc(S["ov_htr"], 1)
                    pe.wait_ge(S["ov_hT"], b + 1)
                    down_whole(S["ov_y"])

        @block.scalar
        def _(act):
            act.wait_ge(S["c_ld"], 32)
            act.activation(csil, c_col, ACT.Silu).then_inc(S["csil_ready"], 1)

            def norm_in(t):
                act.wait_ge(S["x_ld"], 16 * t + 16)
                act.activation(h2T.rearrange("p a b -> p (a b)"), x_in, ACT.Square, accum_out=ss1)
                act.drain().then_inc(S["xss"], 1)

            def hT_half(dst, scale, shift, n, ready, done):
                act.wait_ge(ready, n)
                for k in range(4):
                    ins = act.activation(dst[:, k, :], bank[0][:, k * P:(k + 1) * P], ACT.Identity,
                                         scale=scale[:, k:k + 1], bias=mod_col[:, shift, k:k + 1])
                ins.then_inc(done, 1)

            def copy(dst, src, ready, n, done):
                act.wait_ge(ready, n)
                act.copy(dst, src).then_inc(done, 1)

            def mod_out(n):
                piece, cols = n // 2, slice(n % 2 * 512, n % 2 * 512 + 512)
                act.wait_ge(S["mod_mm"], n + 1)
                if piece % 3 == 2:
                    ins = act.copy(gate_rows[:, piece // 3, cols], bank[2 + n % 2][:])
                else:
                    ins = act.copy(mod_row[0:1, piece % 3, cols], bank[2 + n % 2][0:1, :])
                ins.then_inc(S["mod_evac"], 1)

            def copy_qk(t):
                wait(act, S["prods"], t)
                copy(qk_sb, bank[7][:], S["qk_mm"], t + 1, S["qk_ready"])

            def copy_cbg(t):
                copy(cbg_sb, bank[7][:, 0:CDIM + RANK], S["cbg_mm"], t + 1, S["cbg_ready"])

            def log_part(t):
                act.wait_ge(S["absz"], t + 1)
                act.activation(lg2, lg2, ACT.Exp)
                act.drain()
                act.activation(lg2, lg2, ACT.Ln, bias=1.0).then_inc(S["lnz"], 1)

            def softmax_exp(t):
                act.wait_ge(S["lg_ready"], t + 1)
                act.activation(r_["e"], r_["lg"], ACT.Exp, bias=neg_max, accum_out=exp_sum)
                act.drain().then_inc(S["e_ready"], 1)

            norm_in(0)
            for n in range(FIRST):
                mod_out(n)
            act.wait_ge(S["scale_ready"], 1)
            hT_half(hT, scale1, 0, 1, S["x_tr"], S["hT_act"])
            norm_in(1)
            copy_qk(0)
            mod_out(4)
            copy(ccx_sb, bank[4][:], S["ccx_mm"], 1, S["ccx_ready"])
            copy_cbg(0)
            mod_out(5)
            copy(gT[0:RANK, :], bank[6][0:RANK, 0:P], S["g_tr"], 1, S["gT_ready"])
            log_part(0)
            copy(v_sb, bank[7][:], S["v_mm"], 1, S["v_ready"])
            mod_out(6)
            act.wait_ge(S["uv_mm"], 1)
            act.activation(uv, bank[5][:], ACT.Gelu).then_inc(S["uv_ready"], 1)
            mod_out(7)
            act.wait_ge(S["og_mm"], 1)
            act.activation(og, bank[7][:], ACT.Silu).then_inc(S["og_ready"], 1)
            for n in range(AMONG, MOD):
                mod_out(n)
            act.wait_ge(S["loop_ready"], 1)

            def tile(t):
                nxt = before(t, TILES - 1)
                if nxt:
                    hT_half(hT, scale1, 0, t + 2, S["x_tr"], S["hT_act"])
                act.wait_ge(S["D_mm"], t + 1)
                act.activation(E1, bank[2][:, KDIM:2 * KDIM], ACT.Exp)
                act.activation(E4, bank[2][:, 0:KDIM], ACT.Exp)
                act.activation(E2, bank[2][:, KDIM:2 * KDIM], ACT.Exp, scale=-1.0)
                act.activation(E3, bank[3][:, 0:KDIM], ACT.Exp)
                act.activation(dec, bank[3][:, KDIM:KDIM + 4], ACT.Exp)
                act.drain().then_inc(S["exps"], 1)
                act.wait_ge(S["z_tr"], t + 1)
                wait(act, S["conv_done"], t)
                act.copy(zT[:, :, 2:], bank[4][:, 0:2 * P].rearrange("p (a b) -> p a b", a=2))
                act.copy(cbT, bank[4][:, 2 * P:4 * P].rearrange("p (a b) -> p a b", a=2))
                act.drain().then_inc(S["zT_ready"], 1)
                if nxt:
                    copy_qk(t + 1)
                if before(t, TILES - 2):
                    norm_in(t + 2)
                if nxt:
                    copy(ccx_sb, bank[4][:], S["ccx_mm"], t + 2, S["ccx_ready"])
                act.wait_ge(S["qk_tr"], t + 1)
                act.copy(qkT.rearrange("p a b -> p (a b)"), bank[0][:])
                act.copy(qeT.rearrange("p a b -> p (a b)"), bank[1][:, 0:2 * P])
                act.drain().then_inc(S["qkT_ready"], 1)
                if nxt:
                    copy_cbg(t + 1)
                    copy(gT[0:RANK, :], bank[6][0:RANK, 0:P], S["g_tr"], t + 2, S["gT_ready"])
                act.wait_ge(S["o_mm"], t + 1)
                for h in range(BH):
                    act.activation(lg2[:, 0:DV], bank[4][:, h * DV:(h + 1) * DV], ACT.Square, accum_out=oss[:, h:h + 1])
                    act.drain()
                act.sem_inc(S["oss"], 1)
                if nxt:
                    copy(v_sb, bank[7][:], S["v_mm"], t + 2, S["v_ready"])
                act.wait_ge(S["y_tr"], t + 1)
                act.copy(yT[:, 0:4, :].rearrange("p a b -> p (a b)"), bank[0][:])
                act.copy(yT[:, 4:6, :].rearrange("p a b -> p (a b)"), bank[1][:, 0:2 * P])
                act.drain().then_inc(S["yT_ready"], 1)
                if nxt:
                    log_part(t + 1)
                if after(t, 0):
                    softmax_exp(t - 1)
                if nxt:
                    act.wait_ge(S["uv_mm"], t + 2)
                    act.activation(uv, bank[5][:], ACT.Gelu).then_inc(S["uv_ready"], 1)
                act.wait_ge(S["x2_ready"], t + 1)
                act.activation(yT.rearrange("p a b -> p (a b)"), x_res, ACT.Square, accum_out=ss2)
                act.drain().then_inc(S["x2ss"], 1)
                if nxt:
                    act.wait_ge(S["og_mm"], t + 2)
                    act.activation(og, bank[7][:], ACT.Silu).then_inc(S["og_ready"], 1)
                hT_half(h2T, scale2, 2, t + 1, S["x2_tr"], S["h2_act"])

            tiles(act, tile)
            softmax_exp(TILES - 1)

            def x_evac(h, e):
                act.wait_ge(S["xt_tr"], e + 1)
                for k in range(4):
                    ins = act.activation(xT[h][:, k, :], bank[0][:, k * P:(k + 1) * P], ACT.Identity,
                                         scale=scale2[:, k:k + 1], bias=mod_col[:, 2, k:k + 1])
                ins.then_inc(S["xT_act"], 1)

            def expert(e, h):
                act.wait_ge(S["h1_mm"], e + 1)
                wait(act, S["h_ready"], e)
                act.activation(sil, bank[2][:], ACT.Silu).then_inc(S["sil_ready"], 1)
                if before(e, E - 1):
                    x_evac(1 - h, e + 1)
                act.wait_ge(S["h_tr"], e + 1)
                wait(act, S["y_mm"], e - 1)
                dst = hT_hi[h] if before(e, E - 1) else hT_whole
                act.copy(dst.rearrange("p a b -> p (a b)"), bank[4][:]).then_inc(S["hT_hi_ready"], 1)

            def w2_high(h, n, e):
                act.wait_ge(w2_ld[h], 16 * n + 16)
                wait(act, S["y_mm"], e)
                for k in range(0, KF, KF // 2):
                    act.copy(w2_hi[:, k:k + KF // 2, :].rearrange("p a b -> p (a b)"),
                             W2[h][:, k:k + KF // 2, :].rearrange("p a b -> p (a b)")).then_inc(S["w2_hi_half"], 1)

            x_evac(0, 0)
            for e in range(2):
                expert(e, e)
                w2_high(e, 0, e)
            with act.Fori(1, E // 2 - 1) as i:
                for h in range(2):
                    expert(2 * i + h, h)
                    w2_high(h, i, 2 * i + h)
            expert(E - 2, 0)
            w2_high(0, E // 2 - 1, E - 2)
            expert(E - 1, 1)
            most = act.value_load(count_i[0:1, 0:1], min_val=0, max_val=T)
            with act.If(most > cap):
                act.wait_ge(S["y_mm"], E)
                with act.Fori(0, OVER) as b:
                    act.wait_ge(S["ov_tr"], b + 1)
                    for k in range(KD):
                        ins = act.activation(xT[0][:, k, :], bank[k // 4][:, (k % 4) * P:(k % 4 + 1) * P], ACT.Identity,
                                             scale=scale2[:, k:k + 1], bias=mod_col[:, 2, k:k + 1])
                    ins.then_inc(S["ov_xT"], 1)
                    act.wait_ge(S["ov_h"], b + 1)
                    act.activation(sil, bank[2][:], ACT.Silu).then_inc(S["ov_sil"], 1)
                    act.wait_ge(S["ov_htr"], b + 1)
                    act.copy(hT_whole.rearrange("p a b -> p (a b)"), bank[4][:]).then_inc(S["ov_hT"], 1)
            def store(t):
                act.wait_ge(S["fin_out"], t + 1)
                act.dma_start(out_t[t], acc[:, t, :]).then_inc(out_st, 16)

            for t in range(TILES):
                act.wait_ge(S["fin_acc"], t + 1)
                act.activation(sq_junk, acc[:, t, :], ACT.Square, accum_out=ssf[:, t:t + 1])
                act.drain().then_inc(S["fin_ss"], 1)
                if t:
                    store(t - 1)
            store(TILES - 1)

        @block.vector
        def _(dve):
            TT, TS, STT = dve.tensor_tensor, dve.tensor_scalar, dve.scalar_tensor_tensor
            for s in range(2):
                dve.memset(state[s].rearrange("p a b -> p (a b)"), 0.0)
            dve.memset(zT.rearrange("p a b -> p (a b)"), 0.0)
            dve.memset(sT.rearrange("p a b c -> p (a b c)"), 0.0)
            dve.memset(r_["run"], 0.0)
            dve.memset(gT, 1.0)
            dve.wait_ge(S["csil_ready"], 1)
            for k in range(KD):
                dve.tensor_copy(csil_wide[:, k, :], csil[:, k:k + 1].to_broadcast([P, P]))
            dve.drain().then_inc(S["csil_ready"], 1)

            def mod_sums(n):
                h, k_pe = n % 2, k_of_step(n)
                dve.wait_ge(wada_ld[h], 32 * (n // 2) + 32)
                wait(dve, S["mod_mm"], n - 1)
                TS(mod_acc[h], wada[h][:, k_pe, :], csil[:, k_pe:k_pe + 1], None, ALU.mult)
                for k in range(k_pe + 1, KD):
                    dve.drain()
                    STT(mod_acc[h], wada[h][:, k, :], csil[:, k:k + 1], mod_acc[h], ALU.mult, ALU.add)
                dve.drain()
                TT(mod_acc[h][0:1, :], mod_acc[h][0:1, :], bada[h][0:1, :], ALU.add).then_inc(S["acc_ready"], 1)

            def mean_sq(src, dst, n, done):
                TS(dst, src, 1.0 / n, EPS, ALU.mult, ALU.add).then_inc(done, 1)

            def norm_in(t):
                dve.wait_ge(S["xss"], t + 1)
                mean_sq(ss1, ms1, D, S["ms1"])
                dve.wait_ge(S["rs1"], t + 1)
                wait(dve, S["x_tr"], t)
                TS(x_nrm, x_in, rs1, None, ALU.mult).then_inc(S["xn_ready"], 1)

            def hT_half(dst, scale, shift, n, ready, done):
                dve.wait_ge(ready, n)
                for k in range(4, 8):
                    ins = TS(dst[:, k, :], bank[1][:, (k - 4) * P:(k - 3) * P], scale[:, k:k + 1],
                             mod_col[:, shift, k:k + 1], ALU.mult, ALU.add)
                ins.then_inc(done, 1)

            def conv_product(t):
                dve.wait_ge(S["ccx_ready"], t + 1)
                TT(z_sb, ccx_sb[:, 0:CDIM], ccx_sb[:, CDIM:], ALU.mult).then_inc(S["z_ready"], 1)

            def gate_log(t):
                dve.wait_ge(S["z_mm"], t + 1)
                TS(lg1, bank[6][:, 0:KDIM], 0.0, None, ALU.min)
                dve.drain()
                STT(lg2, lg1, 2.0, bank[6][:, 0:KDIM], ALU.mult, ALU.subtract).then_inc(S["absz"], 1)
                dve.wait_ge(S["lnz"], t + 1)
                TT(lg1, lg1, lg2, ALU.subtract).then_inc(S["L_ready"], 1)

            by_group = lambda v: v.rearrange("p (g i) -> p g i", g=GROUPS)
            wide = lambda v: v.unsqueeze(2).to_broadcast([P, GROUPS, PER])
            rev_b = rev.unsqueeze(1).to_broadcast([P, GROUPS, PER])

            def first_max(src, best, onehot):
                dve.tensor_reduce(g_[best], by_group(r_[src]), AX, ALU.max)
                dve.drain()
                TT(by_group(r_["c"]), by_group(r_[src]), wide(g_[best]), ALU.is_equal)
                dve.drain()
                TT(by_group(r_["c"]), by_group(r_["c"]), rev_b, ALU.mult)
                dve.drain()
                dve.tensor_reduce(g_["r"], by_group(r_["c"]), AX, ALU.max)
                dve.drain()
                TT(by_group(r_[onehot]), rev_b, wide(g_["r"]), ALU.is_equal)
                dve.drain()

            def logits(t):
                dve.wait_ge(S["r_mm"], t + 1)
                TT(r_["lg"], bank[5][:, 0:E], rb, ALU.add)
                dve.drain().then_inc(S["lg_read"], 1)

            def choose(t):
                dve.tensor_reduce(row_max, r_["lg"], AX, ALU.max)
                dve.drain()
                TS(neg_max, row_max, -1.0, None, ALU.mult).then_inc(S["lg_ready"], 1)
                dve.wait_ge(S["e_ready"], t + 1)
                dve.reciprocal(exp_rec, exp_sum)
                dve.drain()
                TS(r_["p"], r_["e"], exp_rec, None, ALU.mult)
                dve.drain()
                first_max("p", "m1", "oh1")
                STT(r_["p2"], r_["oh1"], -2.0, r_["p"], ALU.mult, ALU.add)
                dve.drain()
                first_max("p2", "m2", "oh2")
                TT(g_["gs"], g_["m1"], g_["m2"], ALU.add)
                dve.drain()
                dve.tensor_reduce(best_g, g_["gs"], AX, ALU.max)
                dve.drain()
                STT(g_["t"], g_["gs"], best_g, revg, ALU.is_equal, ALU.mult)
                dve.drain()
                dve.tensor_reduce(pick_g, g_["t"], AX, ALU.max)
                dve.drain()
                TS(g_["sel"], revg, pick_g, None, ALU.is_equal)
                dve.drain()
                TT(by_group(r_["sel1"]), by_group(r_["oh1"]), wide(g_["sel"]), ALU.mult)
                TT(by_group(r_["sel2"]), by_group(r_["oh2"]), wide(g_["sel"]), ALU.mult)
                dve.drain()
                TT(r_["m"], r_["sel1"], r_["sel2"], ALU.add).then_inc(S["m_ready"], 1)
                dve.tensor_tensor_reduce(out=g_["t"], in0=g_["m1"], in1=g_["sel"], scale=1.0, scalar=0.0, op0=ALU.mult,
                                         op1=ALU.add, accum_out=top2[:, 0:1])
                dve.tensor_tensor_reduce(out=g_["r"], in0=g_["m2"], in1=g_["sel"], scale=1.0, scalar=0.0, op0=ALU.mult,
                                         op1=ALU.add, accum_out=top2[:, 1:2])
                dve.drain()
                TT(w_sum, top2[:, 0:1], top2[:, 1:2], ALU.add)
                dve.drain()
                dve.reciprocal(w_rec, w_sum)
                dve.drain()
                TS(top_w[:, t, :] if isinstance(t, int) else top_w[:, bass.ds(t, 1), :].rearrange("p a b -> p (a b)"),
                   top2, w_rec, None, ALU.mult)

            def place(t):
                dve.wait_ge(S["pos_mm"], t + 1)
                STT(r_["a"], bank[5][:, 0:E], float(E), eidx, ALU.mult, ALU.add)
                dve.drain().then_inc(S["pos_read"], 1)
                TT(r_["run"], r_["run"], r_["m"], ALU.add).then_inc(S["run_ready"], 1)
                for k in range(2):
                    dve.tensor_tensor_reduce(out=r_["t"], in0=r_["a"], in1=r_[f"sel{k + 1}"], scale=1.0, scalar=0.0,
                                             op0=ALU.mult, op1=ALU.add, accum_out=idx_f[:, k:k + 1])
                    dve.drain()
                for k in range(2):
                    wait(dve, S[f"list_sc{k}"], 16 * t)
                dve.tensor_copy(idx_now, idx_f).then_inc(S["idx_ready"], 1)

            def columns(src, part, scale, gain):
                dve.tensor_copy(mod_col[:, 2 * part:2 * part + 2, :].rearrange("p a b -> p (a b)"), src[:, 0:2 * KD])
                dve.drain()
                STT(scale, mod_col[:, 2 * part + 1, :], 1.0, gain, ALU.add, ALU.mult)

            mod_sums(0)
            norm_in(0)
            for n in range(1, FIRST):
                mod_sums(n)
            dve.wait_ge(S["setup_mm"], 1)
            dve.wait_ge(S["c_ld"], 32)
            columns(bank[2], 0, scale1, g1c)
            dve.drain().then_inc(S["scale_ready"], 1)
            hT_half(hT, scale1, 0, 1, S["x_tr"], S["hT_dve"])
            norm_in(1)
            mod_sums(4)
            conv_product(0)
            mod_sums(5)
            gate_log(0)
            for n in range(6, MOD):
                mod_sums(n)
            dve.wait_ge(S["setup_mm"], 2)
            dve.tensor_copy(wsT.rearrange("p a b -> p (a b)"), bank[0][:])
            dve.drain()
            dve.memset(wsT[CHUNK:P, :, 0:CHUNK], 0.0)
            dve.wait_ge(S["setup_mm"], 3)
            dve.wait_ge(S["params_ld"], 16 * PARAMS)
            columns(bank[1], 1, scale2, g2c)
            dve.drain().then_inc(S["loop_ready"], 1)

            def tile(t):
                nxt = before(t, TILES - 1)
                dve.wait_ge(S["uv_ready"], t + 1)
                dve.bn_stats(bn6, uv[:, ADIM:])
                dve.drain()
                dve.bn_aggr(mv, bn6)
                dve.drain()
                TS(bn_v, mv[:, 1:2], EPS, None, ALU.add).then_inc(S["bn"], 1)
                if nxt:
                    hT_half(hT, scale1, 0, t + 2, S["x_tr"], S["hT_dve"])
                dve.wait_ge(S["bnr"], t + 1)
                wait(dve, S["x2_st"], 32 * t)
                wait(dve, S["x2_tr"], t)
                TS(vn, uv[:, ADIM:], mv[:, 0:1], bn_r, ALU.subtract, ALU.mult).then_inc(S["vn0"], 1)
                dve.wait_ge(S["exps"], t + 1)
                STT(q1, qk_sb[:, 0:KDIM], DK ** -0.5, E1, ALU.mult, ALU.mult)
                TT(k2, qk_sb[:, KDIM:], E2, ALU.mult)
                STT(qe, qk_sb[:, 0:KDIM], DK ** -0.5, E4, ALU.mult, ALU.mult)
                TT(k3, qk_sb[:, KDIM:], E3, ALU.mult)
                dve.drain().then_inc(S["prods"], 1)
                if after(t, 0):
                    logits(t - 1)
                dve.wait_ge(S["zT_ready"], t + 1)
                for j in range(2):
                    TS(conv_acc[:, j, :], zT[:, j, 0:P], convw[:, 0, j:j + 1], convb[:, j:j + 1], ALU.mult, ALU.add)
                dve.drain()
                for s in (1, 2):
                    for j in range(2):
                        STT(conv_acc[:, j, :], zT[:, j, s:s + P], convw[:, s, j:j + 1], conv_acc[:, j, :], ALU.mult, ALU.add)
                    dve.drain()
                wait(dve, S["out_mm"], t)
                TT(yT[:, 6:8, :], conv_acc, cbT, ALU.mult)
                dve.tensor_copy(zT[:, :, 0:2], zT[:, :, P:P + 2])
                dve.drain().then_inc(S["conv_done"], 1)

                def step(src, dst, ch):
                    for p in range(PAIRS):
                        for hh in range(2):
                            r = slice(hh * DK, (hh + 1) * DK)
                            cols = slice(hh * DV, (hh + 1) * DV)
                            STT(dst[r, p, cols], src[r, p, cols], dec[r, 2 * p + ch:2 * p + ch + 1],
                                bank[2 + ch][r, p * 2 * DV + hh * DV:p * 2 * DV + (hh + 1) * DV], ALU.mult, ALU.add)

                dve.wait_ge(S["kv_mm"], t + 1)
                step(state[0], state[1], 0)
                dve.drain().then_inc(S["state1"], 1)
                dve.wait_ge(S["sc_mm"], t + 1)
                dve.sem_inc(S["dve_passed"], 1)
                for hh in range(2):
                    dve.copy_predicated(sT[:, hh], tri.bitcast(I32).unsqueeze(1).to_broadcast([P, PAIRS, P]),
                                        bank[hh][:, 0:PAIRS * P].rearrange("p (a b) -> p a b", a=PAIRS))
                dve.drain().then_inc(S["sT_ready"], 1)
                if nxt:
                    conv_product(t + 1)
                if before(t, TILES - 2):
                    norm_in(t + 2)
                dve.wait_ge(S["sv_mm"], t + 1)
                for h in range(AH):
                    c_ = slice(h * HD, (h + 1) * HD)
                    STT(ya[:, c_], bank[5][:, c_], bs_col[:, h:h + 1], uv[:, c_], ALU.add, ALU.mult)
                dve.drain().then_inc(S["ya_ready"], 1)
                dve.wait_ge(S["o_mm"], t + 1)
                step(state[1], state[0], 1)
                dve.drain().then_inc(S["state0"], 1)
                dve.wait_ge(S["oss"], t + 1)
                mean_sq(oss, oms, DV, S["oms"])
                dve.wait_ge(S["ors"], t + 1)
                for h in range(BH):
                    c_ = slice(h * DV, (h + 1) * DV)
                    STT(yb[:, c_], bank[4][:, c_], ors[:, h:h + 1], gla_g[:, c_], ALU.mult, ALU.mult)
                dve.drain()
                TT(yb, yb, og, ALU.mult).then_inc(S["yb_ready"], 1)
                if nxt:
                    gate_log(t + 1)
                if after(t, 0):
                    choose(t - 1)
                dve.wait_ge(S["xr_ld"], 16 * t + 16)
                dve.wait_ge(S["out_mm"], t + 1)
                for n in range(2):
                    TT(x_nrm2[:, n * 512:(n + 1) * 512], bank[2 + n][:], gate_rows[:, 0, n * 512:(n + 1) * 512], ALU.mult)
                dve.drain()
                TT(x_res, x_res, x_nrm2, ALU.add).then_inc(S["x2_ready"], 1)
                dve.wait_ge(S["x2ss"], t + 1)
                mean_sq(ss2, ms2, D, S["ms2"])
                dve.wait_ge(S["rs2"], t + 1)
                TS(x_nrm2, x_res, rs2, None, ALU.mult).then_inc(S["xn2_ready"], 1)
                if after(t, 0):
                    place(t - 1)
                hT_half(h2T, scale2, 2, t + 1, S["x2_tr"], S["h2_dve"])

            tiles(dve, tile)
            logits(TILES - 1)
            choose(TILES - 1)
            place(TILES - 1)

            dve.wait_ge(S["cnt_mm"], 1)
            dve.tensor_copy(count_f, bank[5][:, 0:E])
            dve.drain()
            dve.tensor_reduce(row_max, count_f, AX, ALU.max)
            dve.drain()
            dve.tensor_copy(count_i, row_max)
            for h in range(4):
                dve.memset(xg[h], 0.0)
            dve.drain()
            dve.wait_ge(S["slots_ld"], 16)
            TS(slots_tok.rearrange("p a b -> p (a b)"), slots.rearrange("p a b -> p (a b)"), 1, None,
               ALU.logical_shift_right).then_inc(S["slots_ready"], 1)

            def x_evac(h, e):
                dve.wait_ge(S["xt_tr"], e + 1)
                for k in range(4, 8):
                    ins = TS(xT[h][:, k, :], bank[1][:, (k - 4) * P:(k - 3) * P], scale2[:, k:k + 1],
                             mod_col[:, 2, k:k + 1], ALU.mult, ALU.add)
                ins.then_inc(S["xT_dve"], 1)

            def y_evac(h, e, stored):
                dve.wait_ge(S["y_mm"], e + 1)
                wait(dve, scat[h], stored)
                for j in range(2):
                    ins = TT(y_sb[h][:, j * 512:(j + 1) * 512], bank[5 + j][:], gate_rows[:, 1, j * 512:(j + 1) * 512],
                             ALU.mult)
                ins.then_inc(S["y_ready"], 1)

            def w2_low(h, e):
                for n in range(2):
                    dve.wait_ge(S["w2_hi_half"], 2 * e + n + 1)
                    if n == 0:
                        wait(dve, S["y_mm"], e)
                    k = slice(n * (KF // 2), (n + 1) * (KF // 2))
                    ins = TT(w2_lo[:, k, :], W2[h][:, k, :], w2_hi[:, k, :].bitcast(F32), ALU.subtract)
                ins.then_inc(S["w2_lo_ready"], 1)

            def hT_low(h, e):
                dve.wait_ge(S["hT_hi_ready"], e + 1)
                wait(dve, S["y_mm"], e - 1)
                TT(hT_lo[h].rearrange("p a b -> p (a b)"), bank[4][:],
                   hT_hi[h].rearrange("p a b -> p (a b)").bitcast(F32), ALU.subtract).then_inc(S["hT_lo_ready"], 1)

            def expert(e, h, half_e):
                if after(e, 0):
                    hT_low(1 - h, e - 1)
                    w2_low(1 - h, e - 1)
                dve.wait_ge(S["h3_mm"], e + 1)
                dve.wait_ge(S["sil_ready"], e + 1)
                wait(dve, S["h_tr"], e)
                TT(hid, bank[3][:], sil, ALU.mult).then_inc(S["h_ready"], 1)
                if before(e, E - 1):
                    x_evac(1 - h, e + 1)
                if after(e, 0):
                    y_evac(1 - h, e - 1, 16 * (half_e - 1 + h))

            x_evac(0, 0)
            for e in range(3):
                expert(e, e % 2, e // 2)
            with dve.Fori(1, E // 2 - 1) as i:
                for j in range(2):
                    expert(2 * i + 1 + j, 1 - j, i + j)
            expert(E - 1, 1, E // 2 - 1)
            y_evac(1, E - 1, 16 * (E // 2 - 1))
            most = dve.value_load(count_i[0:1, 0:1], min_val=0, max_val=T)
            with dve.If(most > cap):
                dve.wait_ge(S["ov_iota"], 1)
                TS(ob, count_f, float(cap), None, ALU.is_gt)
                dve.drain()
                for j in range(2, LISTS):
                    STT(ob, count_f, float(cap * j), ob, ALU.is_gt, ALU.add)
                    dve.drain()
                src, dst = ob, cum
                s = 1
                while s < E:
                    dve.tensor_copy(dst[:, 0:s], src[:, 0:s])
                    TT(dst[:, s:], src[:, s:], src[:, 0:E - s], ALU.add)
                    dve.drain()
                    src, dst = dst, (cum2 if dst is cum else cum)
                    s *= 2
                TT(le3, src.unsqueeze(1).to_broadcast([P, OVER, E]), bidx, ALU.is_le)
                dve.drain()
                TT(ob3, ob.unsqueeze(1).to_broadcast([P, OVER, E]), le3, ALU.mult)
                dve.tensor_reduce(eb, le3, AX, ALU.add)
                dve.drain()
                dve.tensor_reduce(jb, ob3, AX, ALU.add)
                TS(is_none, eb, float(E), float(LISTS), ALU.is_ge, ALU.mult)
                dve.drain()
                TS(eb, eb, float(E - 1), None, ALU.min)
                TT(jb, nb, jb, ALU.subtract)
                dve.drain()
                TS(jb, jb, 1.0, float(LISTS), ALU.add, ALU.min)
                dve.drain()
                TT(jb, jb, is_none, ALU.max)
                dve.drain()
                STT(jb, jb, float(E), eb, ALU.mult, ALU.add)
                dve.tensor_copy(table[:, 0, :], eb)
                dve.drain()
                dve.tensor_copy(table[:, 1, :], jb).then_inc(S["ov_table"], 1)
                for h in range(2):
                    dve.wait_ge(scat[h], 16 * E // 2)
                with dve.Fori(0, OVER) as b:
                    dve.wait_ge(S["ov_sil"], b + 1)
                    TT(hid, bank[3][:], sil, ALU.mult).then_inc(S["ov_hid"], 1)
                    dve.wait_ge(S["ov_y"], b + 2)
                    for j in range(2):
                        ins = TT(y_sb[0][:, j * 512:(j + 1) * 512], bank[5 + j][:],
                                 gate_rows[:, 1, j * 512:(j + 1) * 512], ALU.mult)
                    ins.then_inc(S["ov_ysb"], 1)
            dve.wait_ge(S["early_ld"], 32)

            def mean_of_tile(t):
                dve.wait_ge(S["fin_ss"], t + 1)
                mean_sq(ssf[:, t:t + 1], msf[:, t:t + 1], D, S["fin_ms"])

            def finish(t):
                dve.wait_ge(S["fin_rs"], t + 1)
                STT(acc[:, t, :], acc[:, t, :], rsf[:, t:t + 1], gfin, ALU.mult, ALU.mult).then_inc(S["fin_out"], 1)

            for t in range(TILES):
                for h, (a, b) in enumerate(y_parts):
                    if a == t:
                        dve.wait_ge(y_ld[h], 16)
                STT(acc[:, t, :], yy[:, t, 0:D], top_w[:, t, 0:1], acc[:, t, :], ALU.mult, ALU.add)
                dve.drain()
                if t:
                    mean_of_tile(t - 1)
                STT(acc[:, t, :], yy[:, t, D:], top_w[:, t, 1:2], acc[:, t, :], ALU.mult, ALU.add).then_inc(S["fin_acc"], 1)
                if t:
                    finish(t - 1)
            mean_of_tile(TILES - 1)
            finish(TILES - 1)


_INS = ['x', 'c', 'w_ada', 'b_ada', 'g_norm1', 'g_norm2', 'w_in', 'w_out', 'gmlp_ln_g', 'gmlp_ln_b', 'gmlp_ws', 'gmlp_bs',
        'gla_w_gate', 'gla_b_gate', 'gla_norm_g', 'conv_w', 'conv_b', 'router_w', 'router_b', 'exp_w1', 'exp_w3', 'exp_w2',
        'g_final']
_OUTS = [((1, 1024, 1024), 'float32')]


def kernel(**inputs):
    import numpy as _np
    import concourse.bacc as _bacc
    from concourse import mybir as _mybir
    from concourse.bass_utils import run_bass_kernel_spmd as _run

    nc = _bacc.Bacc("TRN2", target_bir_lowering=False, num_devices=1)
    arrays, args = {}, []
    for name in _INS:
        a = _np.ascontiguousarray(inputs[name])
        arrays[f"in_{name}_dram"] = a
        args.append(nc.dram_tensor(f"in_{name}_dram", a.shape, _mybir.dt.from_np(a.dtype), kind="ExternalInput").ap())
    for i, (shape, dtype) in enumerate(_OUTS):
        dt = _mybir.dt.from_np(_np.dtype(dtype))
        args.append(nc.dram_tensor(f"out_{i}_dram", shape, dt, kind="ExternalOutput").ap())
    build(nc, *args)
    r = _run(nc, [arrays], core_ids=[0])
    got = tuple(r.results[0][f"out_{i}_dram"] for i in range(len(_OUTS)))
    return got[0]
```
